# Optimizing a Trainium2 kernel written in Bass

```python
import jax, jax.numpy as jnp
from jax import lax
import numpy as np

D_MODEL = 1024
BATCH = 1
SEQ = 1024
DEPTH = 1

N_HEADS_A = 8
N_KV_GROUPS = 2
HEADS_PER_GROUP = N_HEADS_A // N_KV_GROUPS
HEAD_DIM = 64
L_CMP = 32
D_CMP = 16
CMP_HIDDEN = 256
L_SLC = 64
N_SELECT = 16
WINDOW = 512
Q_BLOCK = 128
ROPE_THETA = 10000.0
FORCE_SCORE = 1e4
NEG_INF = -1e30
N_HEADS_B = 8
HEAD_DIM_B = 64
W_LORA = 64
A_LORA = 64
G_LORA = 128
GN_EPS = 64e-5
N_GROUPS = 4
EXPERTS_PER_GROUP = 8
N_EXPERTS = N_GROUPS * EXPERTS_PER_GROUP
TOP_K = 2
D_EXPERT = 256
MOE_BLOCK = 256
RMS_EPS = 1e-6
WIDTH_A = N_HEADS_A * HEAD_DIM
KV_WIDTH = N_KV_GROUPS * HEAD_DIM
WIDTH_B = N_HEADS_B * HEAD_DIM_B
C_RWKV = 3 * WIDTH_B + W_LORA + A_LORA + G_LORA
C_IN = WIDTH_A + 6 * KV_WIDTH + 3 * N_HEADS_A + C_RWKV + 2 * D_MODEL

kernel_name = "hybrid_nsa_rwkv7_hiermoe"

def rms_norm(x, g):
    xf = x.astype(jnp.float32)
    y = xf * lax.rsqrt(jnp.mean(xf * xf, axis=-1, keepdims=True) + RMS_EPS)
    return (y * g.astype(jnp.float32)).astype(x.dtype)

def rope(x, pos):
    half = x.shape[-1] // 2
    freqs = jnp.power(ROPE_THETA, -jnp.arange(half, dtype=jnp.float32) / half)
    ang = pos.astype(jnp.float32)[..., None] * freqs
    cos, sin = jnp.cos(ang)[:, :, None, :], jnp.sin(ang)[:, :, None, :]
    xf = x.astype(jnp.float32)
    x1, x2 = xf[..., :half], xf[..., half:]
    return jnp.concatenate([x1 * cos - x2 * sin, x1 * sin + x2 * cos], axis=-1).astype(x.dtype)

def masked_softmax(s, valid):
    p = jax.nn.softmax(jnp.where(valid, s, NEG_INF), axis=-1)
    return jnp.where(valid, p, 0.0)

def compress(kv, pe, w1, b1, w2, b2):
    bsz, s = kv.shape[:2]
    n_cmp = (s - L_CMP) // D_CMP + 1
    idx = np.arange(n_cmp)[:, None] * D_CMP + np.arange(L_CMP)[None, :]
    blk = kv[:, idx] + pe[:, None, :]
    blk = blk.transpose(0, 1, 3, 2, 4).reshape(bsz, n_cmp, N_KV_GROUPS, L_CMP * HEAD_DIM)
    return jax.nn.gelu(blk @ w1 + b1) @ w2 + b2

def nsa_mixer(q, k_c, v_c, k_slc, v_slc, k_win, v_win, gates):
    bsz, s = q.shape[:2]
    n_cmp = k_c.shape[1]
    n_slc = s // L_SLC
    n_top = min(N_SELECT, n_slc)
    scale = HEAD_DIM ** -0.5
    f32 = jnp.float32
    cmp_end = jnp.arange(n_cmp) * D_CMP + (L_CMP - 1)
    ii = np.arange(n_cmp)[:, None]
    jj = np.arange(n_slc)[None, :]
    overlap = jnp.asarray((ii * D_CMP < (jj + 1) * L_SLC) & (ii * D_CMP + L_CMP > jj * L_SLC), f32)
    blk_ids = jnp.arange(n_slc)
    ks_blk = k_slc.reshape(bsz, n_slc, L_SLC, N_KV_GROUPS, HEAD_DIM).transpose(0, 3, 1, 2, 4)
    vs_blk = v_slc.reshape(bsz, n_slc, L_SLC, N_KV_GROUPS, HEAD_DIM).transpose(0, 3, 1, 2, 4)
    pad = ((0, 0), (WINDOW, 0), (0, 0), (0, 0))
    kw_pad, vw_pad = jnp.pad(k_win, pad), jnp.pad(v_win, pad)
    bi = jnp.arange(bsz)[:, None, None, None]
    gi = jnp.arange(N_KV_GROUPS)[None, :, None, None]
    v_c32 = v_c.astype(f32)

    def block(qb_i):
        s0 = qb_i * Q_BLOCK
        t = s0 + jnp.arange(Q_BLOCK)
        qb = lax.dynamic_slice_in_dim(q, s0, Q_BLOCK, axis=1).reshape(
            bsz, Q_BLOCK, N_KV_GROUPS, HEADS_PER_GROUP, HEAD_DIM)
        gb = jax.nn.sigmoid(lax.dynamic_slice_in_dim(gates, s0, Q_BLOCK, axis=1).astype(f32)).reshape(
            bsz, Q_BLOCK, N_KV_GROUPS, HEADS_PER_GROUP, 3)
        s_c = jnp.einsum('bqghd,bngd->bghqn', qb, k_c, preferred_element_type=f32) * scale
        p_c = masked_softmax(s_c, cmp_end[None, :] <= t[:, None])
        o_c = jnp.einsum('bghqn,bngd->bqghd', p_c, v_c32)
        imp = jnp.einsum('bghqn,nj->bgqj', p_c, overlap)
        cur = t // L_SLC
        valid_s = blk_ids[None, :] <= cur[:, None]
        forced = (blk_ids[None, :] == 0) | (blk_ids[None, :] == cur[:, None]) | (blk_ids[None, :] == cur[:, None] - 1)
        score = jnp.where(forced, FORCE_SCORE, jnp.where(valid_s, imp, -1.0))
        _, sel = lax.top_k(score, n_top)
        k_sel = ks_blk[bi, gi, sel].reshape(bsz, N_KV_GROUPS, Q_BLOCK, n_top * L_SLC, HEAD_DIM)
        v_sel = vs_blk[bi, gi, sel].reshape(bsz, N_KV_GROUPS, Q_BLOCK, n_top * L_SLC, HEAD_DIM)
        pos_sel = (sel[..., None] * L_SLC + jnp.arange(L_SLC)).reshape(bsz, N_KV_GROUPS, Q_BLOCK, n_top * L_SLC)
        s_s = jnp.einsum('bqghd,bgqkd->bghqk', qb, k_sel, preferred_element_type=f32) * scale
        p_s = masked_softmax(s_s, (pos_sel <= t[:, None])[:, :, None])
        o_s = jnp.einsum('bghqk,bgqkd->bqghd', p_s, v_sel.astype(f32))
        kw = lax.dynamic_slice_in_dim(kw_pad, s0, WINDOW + Q_BLOCK, axis=1)
        vw = lax.dynamic_slice_in_dim(vw_pad, s0, WINDOW + Q_BLOCK, axis=1)
        pos_w = s0 - WINDOW + jnp.arange(WINDOW + Q_BLOCK)
        valid_w = (pos_w[None, :] <= t[:, None]) & (pos_w[None, :] > t[:, None] - WINDOW) & (pos_w[None, :] >= 0)
        s_w = jnp.einsum('bqghd,bkgd->bghqk', qb, kw, preferred_element_type=f32) * scale
        p_w = masked_softmax(s_w, valid_w)
        o_w = jnp.einsum('bghqk,bkgd->bqghd', p_w, vw.astype(f32))
        o = gb[..., 0:1] * o_c + gb[..., 1:2] * o_s + gb[..., 2:3] * o_w
        return o.reshape(bsz, Q_BLOCK, WIDTH_A).astype(q.dtype)

    out = lax.map(block, jnp.arange(s // Q_BLOCK))
    return out.transpose(1, 0, 2, 3).reshape(bsz, s, WIDTH_A)

def rwkv7_mixer(p, mu, w0, w2, a0, a2, g2, k_k, k_a, r_k, ln_w, ln_b):
    bsz, s = p.shape[:2]
    f32 = jnp.float32
    p_prev = jnp.pad(p[:, :-1], ((0, 0), (1, 0), (0, 0)))
    xs = p + (p_prev - p) * mu
    r, k, v, xw, xa, xg = jnp.split(xs, np.cumsum([WIDTH_B, WIDTH_B, WIDTH_B, W_LORA, A_LORA]), axis=-1)
    w_log = -jax.nn.softplus(-(w0 + jnp.tanh(xw) @ w2)) - 0.5
    decay = jnp.exp(-jnp.exp(w_log.astype(f32)))
    a = jax.nn.sigmoid(a0 + xa @ a2)
    g = jax.nn.sigmoid(xg) @ g2
    heads = lambda z: z.reshape(bsz, s, N_HEADS_B, HEAD_DIM_B).astype(f32)
    kk = heads(k * k_k)
    kk = kk / jnp.maximum(jnp.linalg.norm(kk, axis=-1, keepdims=True), 1e-12)
    k = k * (1 + (a - 1) * k_a)
    rh, kh, vh, ah, wh = heads(r), heads(k), heads(v), heads(a), heads(decay)

    def step(state, inp):
        r_t, w_t, k_t, v_t, kk_t, a_t = inp
        sa = jnp.einsum('bhvk,bhk->bhv', state, -kk_t)
        state = state * w_t[:, :, None, :] + sa[..., None] * (kk_t * a_t)[:, :, None, :] \
            + v_t[..., None] * k_t[:, :, None, :]
        return state, jnp.einsum('bhvk,bhk->bhv', state, r_t)

    tm = lambda z: jnp.swapaxes(z, 0, 1)
    state0 = jnp.zeros((bsz, N_HEADS_B, HEAD_DIM_B, HEAD_DIM_B), f32)
    _, y = lax.scan(step, state0, (tm(rh), tm(wh), tm(kh), tm(vh), tm(kk), tm(ah)))
    y = tm(y)
    mean = jnp.mean(y, axis=-1, keepdims=True)
    var = jnp.mean(jnp.square(y - mean), axis=-1, keepdims=True)
    y = ((y - mean) * lax.rsqrt(var + GN_EPS)).reshape(bsz, s, WIDTH_B) * ln_w + ln_b
    bonus = jnp.sum(rh * kh * r_k, axis=-1, keepdims=True) * vh
    y = y + bonus.reshape(bsz, s, WIDTH_B)
    return (y * g).astype(p.dtype)

def hier_moe(h, w_grp, b_grp, w_exp, b_exp, e_w1, e_w3, e_w2):
    bsz, s, d = h.shape
    n_tok = bsz * s
    f32 = jnp.float32
    t = h.reshape(n_tok, d)
    grp_logits = (t @ w_grp + b_grp).astype(f32)
    p_grp = jax.nn.softmax(grp_logits, axis=-1)
    g_star = jnp.argmax(grp_logits, axis=-1)
    p_g = jnp.take_along_axis(p_grp, g_star[:, None], axis=1)[:, 0]
    exp_logits = (t @ w_exp + b_exp).astype(f32).reshape(n_tok, N_GROUPS, EXPERTS_PER_GROUP)
    in_grp = jnp.take_along_axis(exp_logits, g_star[:, None, None], axis=1)[:, 0]
    top_p, top_j = lax.top_k(jax.nn.softmax(in_grp, axis=-1), TOP_K)
    gate = p_g[:, None] * top_p / jnp.sum(top_p, axis=-1, keepdims=True)
    expert = g_star[:, None] * EXPERTS_PER_GROUP + top_j
    n_asg = n_tok * TOP_K
    e_flat = expert.reshape(n_asg)
    tok_flat = jnp.repeat(jnp.arange(n_tok), TOP_K)
    gate_flat = gate.reshape(n_asg)
    order = jnp.argsort(e_flat)
    e_sorted = e_flat[order]
    counts = jnp.bincount(e_flat, length=N_EXPERTS)
    padded = (counts + MOE_BLOCK - 1) // MOE_BLOCK * MOE_BLOCK
    pad_end = jnp.cumsum(padded)
    pad_start = pad_end - padded
    start = jnp.cumsum(counts) - counts
    dest = pad_start[e_sorted] + (jnp.arange(n_asg) - start[e_sorted])
    n_pad = n_asg + N_EXPERTS * MOE_BLOCK
    buf_tok = jnp.zeros((n_pad,), jnp.int32).at[dest].set(tok_flat[order].astype(jnp.int32))
    buf_gate = jnp.zeros((n_pad,), f32).at[dest].set(gate_flat[order])
    n_blk = n_pad // MOE_BLOCK
    blk_expert = jnp.minimum(jnp.searchsorted(pad_end, jnp.arange(n_blk) * MOE_BLOCK, side='right'), N_EXPERTS - 1)

    def run_block(args):
        tok_idx, g_b, e = args
        xb = t[tok_idx]
        hid = jax.nn.silu(xb @ e_w1[e]) * (xb @ e_w3[e])
        return ((hid @ e_w2[e]) * g_b[:, None]).astype(t.dtype)

    y = lax.map(run_block, (buf_tok.reshape(n_blk, MOE_BLOCK), buf_gate.reshape(n_blk, MOE_BLOCK), blk_expert))
    out = jax.ops.segment_sum(y.reshape(n_pad, d), buf_tok, num_segments=n_tok)
    return out.reshape(bsz, s, d).astype(h.dtype)

def setup_inputs(seed: int = 0) -> dict:
    key = jax.random.key(seed)
    ks = iter(jax.random.split(key, 48))
    f32 = jnp.float32
    nrm = lambda shape, sc: jax.random.normal(next(ks), shape, f32) * sc
    gain = lambda shape: 1.0 + nrm(shape, 0.02)
    L = DEPTH
    inp = {}
    inp['x'] = nrm((BATCH, SEQ, D_MODEL), 1.0)
    inp['positions'] = jnp.broadcast_to(jnp.arange(SEQ, dtype=jnp.int32), (BATCH, SEQ))
    inp['g_mix'] = gain((L, D_MODEL))
    inp['w_in'] = nrm((L, D_MODEL, C_IN), D_MODEL ** -0.5)
    for nm in ('k', 'v'):
        inp['cmp_pe_' + nm] = nrm((L, L_CMP, HEAD_DIM), 0.1)
        inp['cmp_w1_' + nm] = nrm((L, L_CMP * HEAD_DIM, CMP_HIDDEN), (L_CMP * HEAD_DIM) ** -0.5)
        inp['cmp_b1_' + nm] = nrm((L, CMP_HIDDEN), 0.02)
        inp['cmp_w2_' + nm] = nrm((L, CMP_HIDDEN, HEAD_DIM), CMP_HIDDEN ** -0.5)
        inp['cmp_b2_' + nm] = nrm((L, HEAD_DIM), 0.02)
    inp['rwkv_mu'] = jax.random.uniform(next(ks), (L, C_RWKV), f32)
    inp['rwkv_w0'] = jax.random.uniform(next(ks), (L, WIDTH_B), f32, -5.0, 1.0)
    inp['rwkv_w2'] = nrm((L, W_LORA, WIDTH_B), W_LORA ** -0.5)
    inp['rwkv_a0'] = nrm((L, WIDTH_B), 0.5)
    inp['rwkv_a2'] = nrm((L, A_LORA, WIDTH_B), A_LORA ** -0.5)
    inp['rwkv_g2'] = nrm((L, G_LORA, WIDTH_B), G_LORA ** -0.5)
    inp['rwkv_k_k'] = 0.85 + nrm((L, WIDTH_B), 0.05)
    inp['rwkv_k_a'] = 1.0 + nrm((L, WIDTH_B), 0.05)
    inp['rwkv_r_k'] = nrm((L, N_HEADS_B, HEAD_DIM_B), 0.1)
    inp['rwkv_ln_w'] = gain((L, WIDTH_B))
    inp['rwkv_ln_b'] = nrm((L, WIDTH_B), 0.02)
    inp['w_proj_a'] = nrm((L, WIDTH_A, D_MODEL), WIDTH_A ** -0.5)
    inp['w_proj_b'] = nrm((L, WIDTH_B, D_MODEL), WIDTH_B ** -0.5)
    inp['w_out'] = nrm((L, D_MODEL, D_MODEL), D_MODEL ** -0.5)
    inp['g_ffn'] = gain((L, D_MODEL))
    inp['w_grp'] = nrm((L, D_MODEL, N_GROUPS), D_MODEL ** -0.5)
    inp['b_grp'] = nrm((L, N_GROUPS), 0.01)
    inp['w_exp'] = nrm((L, D_MODEL, N_EXPERTS), D_MODEL ** -0.5)
    inp['b_exp'] = nrm((L, N_EXPERTS), 0.01)
    inp['e_w1'] = nrm((L, N_EXPERTS, D_MODEL, D_EXPERT), D_MODEL ** -0.5)
    inp['e_w3'] = nrm((L, N_EXPERTS, D_MODEL, D_EXPERT), D_MODEL ** -0.5)
    inp['e_w2'] = nrm((L, N_EXPERTS, D_EXPERT, D_MODEL), D_EXPERT ** -0.5)
    inp['g_final'] = gain((D_MODEL,))
    return inp

def reference(x, positions, g_mix, w_in,
              cmp_pe_k, cmp_w1_k, cmp_b1_k, cmp_w2_k, cmp_b2_k,
              cmp_pe_v, cmp_w1_v, cmp_b1_v, cmp_w2_v, cmp_b2_v,
              rwkv_mu, rwkv_w0, rwkv_w2, rwkv_a0, rwkv_a2, rwkv_g2,
              rwkv_k_k, rwkv_k_a, rwkv_r_k, rwkv_ln_w, rwkv_ln_b,
              w_proj_a, w_proj_b, w_out, g_ffn,
              w_grp, b_grp, w_exp, b_exp, e_w1, e_w3, e_w2, g_final):
    bsz, s, _ = x.shape
    splits = np.cumsum([WIDTH_A] + [KV_WIDTH] * 6 + [3 * N_HEADS_A, C_RWKV, D_MODEL])
    for l in range(DEPTH):
        h = rms_norm(x, g_mix[l])
        p = h @ w_in[l]
        q, kc, vc, ksl, vsl, kwn, vwn, nsa_g, p_rwkv, gate_a, gate_b = jnp.split(p, splits, axis=-1)
        hd = lambda z, n: z.reshape(bsz, s, n, HEAD_DIM)
        q = rope(hd(q, N_HEADS_A), positions)
        kc = rope(hd(kc, N_KV_GROUPS), positions)
        ksl = rope(hd(ksl, N_KV_GROUPS), positions)
        kwn = rope(hd(kwn, N_KV_GROUPS), positions)
        vc, vsl, vwn = hd(vc, N_KV_GROUPS), hd(vsl, N_KV_GROUPS), hd(vwn, N_KV_GROUPS)
        k_c = compress(kc, cmp_pe_k[l], cmp_w1_k[l], cmp_b1_k[l], cmp_w2_k[l], cmp_b2_k[l])
        v_c = compress(vc, cmp_pe_v[l], cmp_w1_v[l], cmp_b1_v[l], cmp_w2_v[l], cmp_b2_v[l])
        o_a = nsa_mixer(q, k_c, v_c, ksl, vsl, kwn, vwn, nsa_g.reshape(bsz, s, N_HEADS_A, 3))
        o_b = rwkv7_mixer(p_rwkv, rwkv_mu[l], rwkv_w0[l], rwkv_w2[l], rwkv_a0[l], rwkv_a2[l], rwkv_g2[l],
                          rwkv_k_k[l], rwkv_k_a[l], rwkv_r_k[l], rwkv_ln_w[l], rwkv_ln_b[l])
        merged = jax.nn.sigmoid(gate_a) * (o_a @ w_proj_a[l]) + jax.nn.sigmoid(gate_b) * (o_b @ w_proj_b[l])
        x = x + merged @ w_out[l]
        h2 = rms_norm(x, g_ffn[l])
        x = x + hier_moe(h2, w_grp[l], b_grp[l], w_exp[l], b_exp[l], e_w1[l], e_w3[l], e_w2[l])
    return rms_norm(x, g_final)


_drawn_inputs = setup_inputs


def setup_inputs(seed=0):
    import zlib

    import numpy as np

    out = dict(_drawn_inputs(seed))
    spreads = {}
    factors = {'cmp_pe_k': 32.066,
     'cmp_b1_k': 64.0,
     'cmp_b2_k': 64.0,
     'cmp_b1_v': 14.892,
     'cmp_b2_v': 10.349,
     'rwkv_k_k': 2.839,
     'rwkv_ln_w': 3.946,
     'rwkv_ln_b': 9.594,
     'b_grp': 3.245,
     'b_exp': 10.151,
     'g_final': 8.668,
     'cmp_pe_v': 3.299,
     'g_ffn': 3.324}
    for name, (base, spread) in spreads.items():
        noise = np.random.default_rng([zlib.crc32(name.encode()), seed]).standard_normal(out[name].shape)
        drawn = base * np.exp(spread * noise) if base else spread * noise
        out[name] = __import__('jax').numpy.asarray(drawn.astype(out[name].dtype))
    for name, factor in factors.items():
        out[name] = (out[name] * factor).astype(out[name].dtype)
    return out
```

```python
from contextlib import ExitStack
import math

import numpy as np
import concourse.bass as bass
from concourse import mybir

F32 = mybir.dt.float32
I32 = mybir.dt.int32
U32 = mybir.dt.uint32
ACT = mybir.ActivationFunctionType
ALU = mybir.AluOpType
AXX = mybir.AxisListType.X

P = 128
S = 1024
D = 1024
KT = D // P
TT = S // P
HALF = 512
HD = 64
PAIRS = 4
N_CMP = 63
CMP_HID = 256
N_GRP, N_EXP, PER_GRP = 4, 32, 8
N_LOG = N_GRP + N_EXP
D_EXP = 256
RMS_EPS = 1e-6
GN_EPS = 64e-5
OVER = S * 2 // P - 1
N_BLK = N_EXP + OVER
W_DECAY = -math.exp(-0.5)

T_XWA, T_XG = 0, 1
T_RKV = 2
T_QKV = 14
N_QKV = 8
T_GATE = 22
N_ROPE = 7
TOKW = 2 * P + 24
NEG = -1e30


class Steps:

    def __init__(self, eng, sem):
        self.eng, self.sem, self.base, self.n = eng, sem, 0, 0

    def __call__(self, ins):
        self.n += 1
        ins.then_inc(self.sem, 1)
        self.eng.wait_ge(self.sem, self.base + self.n)

    def enter(self, i, per):
        self.start, self.per = self.base + self.n, per
        self.base, self.n = i * per + self.start, 0

    def leave(self, trips):
        assert self.n == self.per, f"steps per turn: {self.n}"
        self.base, self.n = self.start + trips * self.per, 0


class Names:
    pass


def flat(ap):
    return ap.rearrange("p a n -> p (a n)")


def allocators(nc, ctx):
    sems = []

    def retire():
        nc.clear_and_free_semaphores(sems)
        nc.all_engine_barrier()

    ctx.callback(retire)

    def sb(name, shape, dt=F32):
        return ctx.enter_context(nc.sbuf_tensor(name, shape, dt))

    def psum(name, shape):
        return ctx.enter_context(nc.psum_tensor(name, shape, F32))

    def sem(name):
        sems.append(nc.alloc_semaphore(name))
        return sems[-1]

    return sb, psum, sem


def stage_normalise(nc, g, m):
    with ExitStack() as ctx:
        sb, psum, sem = allocators(nc, ctx)
        ps = psum("ps_norm", [P, 8, HALF])
        ones = sb("ones_n", [P, P])
        square = sb("square", [P, 2, S])
        rstd = sb("rstd_x", [P, S])
        gmix = sb("gmix", [P, KT])
        wlo = sb("wlo", [P, 2, KT * P])
        mu = sb("mu_lo", [P, 2])
        shift = sb("shift_n", [P, 2, S])
        x_in = [sem(f"x_in{k}") for k in range(KT)]
        small_in, w_in = sem("small_in"), sem("w_in_n")
        ones_set, squared, summed = sem("ones_set"), sem("squared"), sem("summed")
        root_done, h_ready = sem("root_done"), sem("h_ready")
        lo_done, lo_out, lo_mixed = sem("lo_done"), sem("lo_out"), sem("lo_mixed")
        act_done, vstep = sem("act_done_n"), sem("vstep_n")
        zeros = sb("zeros_n", [P, D])
        zeros_set, zeros_out = sem("zeros_set"), sem("zeros_out")
        block = ctx.enter_context(nc.Block())

        @block.sync
        def _(sy):
            for k in range(KT):
                sy.dma_start(m.hT[:, k, :], g.xT[:, k * S:(k + 1) * S]).then_inc(x_in[k], 16)
            for dst, src in ((gmix[:], g.gmix), (mu[:], g.mu_lo), (m.ident[:], g.ident), (m.col[:], g.col)):
                sy.dma_start(dst, src).then_inc(small_in, 16)
            for t in range(2):
                sy.dma_start(wlo[:, t, :], g.w_tiles[:, T_XWA + t, :]).then_inc(w_in, 16)
            sy.wait_ge(zeros_set, 1)
            with nc.sync.Fori(0, OVER) as b:
                sy.dma_start(g.y[bass.ds(b * P + N_EXP * P, P), :], zeros[:]).then_inc(zeros_out, 16)
            sy.wait_ge(zeros_out, 16 * OVER)

        @block.tensor
        def _(pe):
            pe.wait_ge(ones_set, 1)
            for k in range(KT):
                pe.wait_ge(squared, k + 1)
                for h in range(2):
                    ins = nc.tensor.matmul(ps[:, 4 + h, :], ones[:], square[:, k % 2, h * HALF:(h + 1) * HALF],
                                           start=(k == 0), stop=(k == KT - 1))
                ins.then_inc(summed, 1)
            pe.wait_ge(w_in, 32)
            for t in range(2):
                for h in range(2):
                    for k in range(KT):
                        pe.wait_ge(h_ready, k + 1)
                        ins = nc.tensor.matmul(ps[:, 2 * t + h, :], wlo[:, t, k * P:(k + 1) * P],
                                               m.hT[:, k, h * HALF:(h + 1) * HALF], start=(k == 0), stop=(k == KT - 1))
                    ins.then_inc(lo_done, 1)

        @block.scalar
        def _(act):
            for k in range(KT):
                act.wait_ge(x_in[k], 16)
                if k >= 2:
                    act.wait_ge(summed, k - 1)
                nc.scalar.activation(square[:, k % 2, :], m.hT[:, k, :], ACT.Square).then_inc(squared, 1)
            act.wait_ge(small_in, 64)
            act.wait_ge(summed, KT)
            for h in range(2):
                nc.scalar.activation(rstd[:, h * HALF:(h + 1) * HALF], ps[:, 4 + h, :], ACT.Sqrt,
                                     bias=m.col[:, 3:4], scale=1.0 / D).then_inc(root_done, 1)
            for t in range(2):
                for h in range(2):
                    act.wait_ge(lo_done, 2 * t + h + 1)
                    nc.scalar.activation(m.lo[:, t, h * HALF:(h + 1) * HALF], ps[:, 2 * t + h, :], ACT.Copy)\
                      .then_inc(lo_out, 1)
            act.wait_ge(lo_mixed, 2)
            nc.scalar.activation(m.lo[0:HD, 0, :], m.lo[0:HD, 0, :], ACT.Tanh).then_inc(act_done, 1)
            nc.scalar.activation(m.lo[:, 1, :], m.lo[:, 1, :], ACT.Sigmoid).then_inc(act_done, 1)
            act.wait_ge(act_done, 2)

        @block.vector
        def _(dve):
            step = Steps(dve, vstep)
            nc.vector.memset(ones[:], 1.0).then_inc(ones_set, 1)
            nc.vector.memset(zeros[:], 0.0).then_inc(zeros_set, 1)
            dve.wait_ge(small_in, 64)
            dve.wait_ge(root_done, 2)
            step(nc.vector.reciprocal(rstd[:], rstd[:]))
            for k in range(KT):
                dve.wait_ge(x_in[k], 16)
                nc.vector.scalar_tensor_tensor(out=m.hT[:, k, :], in0=m.hT[:, k, :], scalar=gmix[:, k:k + 1],
                                               in1=rstd[:], op0=ALU.mult, op1=ALU.mult).then_inc(h_ready, 1)
            for t in range(2):
                dve.wait_ge(lo_out, 2 * t + 2)
                token_shift(nc, step, m.lo[:, t, :], m.lo[:, t, :], shift[:, t, :], mu[:, t:t + 1], lo_mixed)
            dve.wait_ge(lo_mixed, 2)


def token_shift(nc, step, out, raw, tmp, mu, done):
    nc.vector.tensor_tensor(tmp[:, 1:S], raw[:, 0:S - 1], raw[:, 1:S], ALU.subtract)
    step(nc.vector.tensor_scalar(tmp[:, 0:1], raw[:, 0:1], -1.0, None, ALU.mult))
    nc.vector.scalar_tensor_tensor(out=out, in0=tmp, scalar=mu, in1=raw, op0=ALU.mult, op1=ALU.add).then_inc(done, 1)


LANES = 2
ROUNDS = 2
LEVELS = 7
MID = P // 2 - 1
V_MU_R, V_MU_K, V_MU_V, V_W0, V_A0, V_KK, V_KA, V_RK, V_LNW, V_LNB = range(10)
N_VEC = 10
K_MT, K_RB, K_NT, K_RK = range(4)
TOK_A, TOK_B, TOK_K, TOK_V = range(4)
RECUR_STEPS = 19
LANE_SIGNALS = ("gram", "masked", "tt_set", "off", "t_turned", "t_set", "x_done", "x_out", "tx_done", "xt_done",
                "t_upd", "tt_upd", "nv_done", "nv_out", "wu_done", "wu_out", "gq_done", "gq_out", "rw_done",
                "rw_out", "y_done", "y_out")


def stage_recur(nc, g, m):
    with ExitStack() as ctx:
        sb, psum, sem = allocators(nc, ctx)
        ps = psum("ps_recur", [P, 8, HALF])
        wr = sb("wr", [P, 3, KT * P])
        lora = sb("lora", [P, 2, P])
        vecs = sb("vecs", [P, PAIRS, N_VEC])
        vec = sb("vec", [P, N_VEC])
        raw = sb("raw_r", [P, 3, S])
        mix = sb("mix_r", [P, 3, S])
        tmp = sb("tmp_r", [P, 2, S])
        av = sb("av", [P, S])
        sig = sb("sig", [P, S])
        lc = sb("lc", [P, S])
        kk = sb("kk", [P, S])
        bonus = sb("bonus", [P, S])
        yt = raw[:, 0, :]
        ar = sb("ar", [P, TT, 2, P])
        kt = sb("kt_r", [P, S])
        bt = sb("bt_r", [P, S])
        tok = sb("tok_r", [P, TT, 4, P])
        ones = sb("ones_r", [P, P])
        mask4 = sb("mask4", [P, 4 * P])
        lvl = sb("lvl", [P, LEVELS, P])
        heads1 = sb("heads1", [P, P])
        eye2 = sb("eye2", [P, HD])
        dcol = sb("dcol", [P, TT])
        state = sb("state", [P, TT + 1, HD])
        mm = [sb(f"mm{x}", [P, 4, 4, P]) for x in range(LANES)]
        tinv = [sb(f"tinv{x}", [P, 4, P]) for x in range(LANES)]
        tinvT = [sb(f"tinvT{x}", [P, 4, P]) for x in range(LANES)]
        xs = [sb(f"xs{x}", [P, 4, P]) for x in range(LANES)]
        moff = [sb(f"moff{x}", [P, 2, 4, P]) for x in range(LANES)]
        nv = [sb(f"nv{x}", [P, 4, HD]) for x in range(LANES)]
        wu = [xs[x][:].rearrange("p u (a n) -> p u a n", a=2) for x in range(LANES)]
        gm = [sb(f"gm{x}", [P, 2, HD]) for x in range(LANES)]
        qd = [sb(f"qd{x}", [P, 2, HD]) for x in range(LANES)]
        rw = [sb(f"rw{x}", [P, 2, P]) for x in range(LANES)]

        const_in, w_in, lora_in = sem("const_in_r"), sem("w_in_r"), sem("lora_in")
        vec_set, raw_done, raw_out, lo_done, lo_out = (sem(n) for n in ("vec_set", "raw_done", "raw_out", "lora_done",
                                                                        "lora_out"))
        mixed, kraw, ksq, kn_sum, kn_root = (sem(n) for n in ("mixed", "kraw", "ksq", "kn_sum", "kn_root"))
        lc_ready, exps, rk_ready, rk_sum, bonus_set = (sem(n) for n in ("lc_ready", "exps", "rk_ready", "rk_sum",
                                                                        "bonus_set"))
        factors, pool_factors, turned, turned_out = (sem(n) for n in ("factors", "pool_factors", "turned", "turned_out"))
        y_mean, y_cent, y_sq, y_var, y_root, bm_set = (sem(n) for n in ("y_mean", "y_cent", "y_sq", "y_var", "y_root",
                                                                        "bm_set"))
        g_done = sem("g_done")
        chain_open = sem("chain_open")
        zero_set, state_set, chained, vstep = sem("zero_set"), sem("state_set"), sem("chained"), sem("vstep_r")
        lane = [{what: sem(f"{what}_{x}") for what in LANE_SIGNALS} for x in range(LANES)]
        PRIME_Y, PRIME_ROOT, PRIME_BM = 1, 2, 1
        block = ctx.enter_context(nc.Block())
        N_CONST = 6

        spare = bt

        def head(j):
            return slice(HD * j, HD * j + HD)

        def units(r, x):
            return [(2 * cc + j, cc, 4 * r + 2 * x + cc, j) for cc in range(2) for j in range(2)]

        def half(h):
            return slice(h * HALF, (h + 1) * HALF)

        @block.sync
        def _(sy):
            def load_w(hp):
                sy.dma_start(wr[:], g.w_tiles[:, bass.ds(hp * 3 + T_RKV, 3), :]).then_inc(w_in, 16)

            def load_lora(hp):
                sy.dma_start(lora[:], g.lora[:, bass.ds(hp * 2, 2), :]).then_inc(lora_in, 16)

            load_w(0)
            load_lora(0)
            for dst, src in ((vecs[:], g.vecs), (ones[:], g.ones), (mask4[:], g.mask4), (lvl[:], g.lvl),
                             (heads1[:], g.heads1), (eye2[:], g.eye2)):
                sy.dma_start(dst, src).then_inc(const_in, 16)
            with nc.sync.Fori(1, PAIRS) as hp:
                sy.wait_ge(raw_done, 6 * hp)
                load_w(hp)
                sy.wait_ge(g_done, 2 * hp)
                load_lora(hp)

        @block.tensor
        def _(pe):
            pe.wait_ge(const_in, 16 * N_CONST)

            def front(hp):
                pe.wait_ge(w_in, 16 * hp + 16)
                pe.wait_ge(y_root, 2 * hp + PRIME_ROOT)
                pe.wait_ge(bm_set, hp + PRIME_BM)
                for t in range(3):
                    for h in range(2):
                        for k in range(KT):
                            ins = nc.tensor.matmul(ps[:, 2 * t + h, :], wr[:, t, k * P:(k + 1) * P],
                                                   m.hT[:, k, half(h)], start=(k == 0), stop=(k == KT - 1))
                        ins.then_inc(raw_done, 1)
                pe.wait_ge(lora_in, 16 * hp + 16)
                for h in range(2):
                    nc.tensor.matmul(ps[:, 6 + h, :], lora[0:HD, 0, :], m.lo[0:HD, 0, half(h)], start=True, stop=True)\
                      .then_inc(lo_done, 1)
                for h in range(2):
                    pe.wait_ge(raw_out, 6 * hp + h + 1)
                    nc.tensor.matmul(ps[:, h, :], lora[HD:P, 0, :], m.lo[HD:P, 0, half(h)], start=True, stop=True)\
                      .then_inc(lo_done, 1)
                for h in range(2):
                    pe.wait_ge(ksq, 2 * hp + h + 1)
                    nc.tensor.matmul(ps[:, 4 + h, :], heads1[:], bonus[:, half(h)], start=True, stop=True)\
                      .then_inc(kn_sum, 1)
                pe.wait_ge(lo_out, 4 * hp + 2)
                pe.wait_ge(rk_ready, hp + 1)
                for h in range(2):
                    nc.tensor.matmul(ps[:, 6 + h, :], heads1[:], tmp[:, 0, half(h)], start=True, stop=True)\
                      .then_inc(rk_sum, 1)
                pe.wait_ge(factors, 2 * hp + 2)
                pe.wait_ge(pool_factors, 2 * hp + 2)
                pe.wait_ge(lo_out, 4 * hp + 4)
                pe.wait_ge(kn_root, 2 * hp + 2)
                pe.wait_ge(bonus_set, 2 * hp + 2)
                for c in range(TT):
                    col = slice(c * P, (c + 1) * P)
                    for q, src in enumerate((ar[:, c, 0, :], bt[:, col], kt[:, col], mix[:, 2, col])):
                        ins = nc.tensor.transpose(ps[:, c, q * P:(q + 1) * P], src, m.ident[:])
                    ins.then_inc(turned, 1)

            def grams(hp, r, x, n):
                if r == 0:
                    pe.wait_ge(turned_out, 8 * hp + 4 * x + 4)
                else:
                    pe.wait_ge(state_set, 8 * hp + 2 * x + 2)
                pe.wait_ge(lane[x]["y_out"], n + PRIME_Y)
                for u, cc, c, j in units(r, x):
                    col = slice(c * P, (c + 1) * P)
                    nc.tensor.matmul(ps[:, 4 * x + u, 0:2 * P], bt[head(j), col], ar[head(j), c, :, :],
                                     start=True, stop=True)
                    nc.tensor.matmul(ps[:, 4 * x + u, 2 * P:4 * P], kt[head(j), col], ar[head(j), c, :, :],
                                     start=True, stop=True).then_inc(lane[x]["gram"], 1)

            def turn_t(hp, r, x, n):
                pe.wait_ge(lane[x]["tt_set"], n + 1)
                for u in range(4):
                    ins = nc.tensor.transpose(ps[:, 4 * x, u * P:(u + 1) * P], tinvT[x][:, u, :], m.ident[:])
                ins.then_inc(lane[x]["t_turned"], 1)

            def level_x(lv, hp, r, x, n):
                s = lane[x]
                pe.wait_ge(s["off"], 6 * n + lv)
                if lv == 1:
                    pe.wait_ge(s["t_set"], n + 1)
                else:
                    pe.wait_ge(s["t_upd"], 5 * n + lv - 1)
                for u in range(4):
                    ins = nc.tensor.matmul(ps[:, 4 * x + 1, u * P:(u + 1) * P], moff[x][:, lv % 2, u, :],
                                           tinv[x][:, u, :], start=True, stop=True)
                ins.then_inc(s["x_done"], 1)
                if lv == 1:
                    for u, cc, c, j in units(r, x):
                        ins = nc.tensor.matmul(ps[:, 4 * x, u * HD:(u + 1) * HD], mm[x][:, u, K_NT, :],
                                               tok[:, c, TOK_V, head(j)], start=True, stop=True)
                    ins.then_inc(s["nv_done"], 1)

            def level_t(lv, hp, r, x, n):
                s = lane[x]
                pe.wait_ge(s["x_out"], 6 * n + lv)
                if lv > 1:
                    pe.wait_ge(s["tt_upd"], 6 * n + lv - 1)
                if lv < LEVELS - 1:
                    for u in range(4):
                        ins = nc.tensor.matmul(ps[:, 4 * x + 2, u * P:(u + 1) * P], tinvT[x][:, u, :], xs[x][:, u, :],
                                               start=True, stop=True)
                    ins.then_inc(s["tx_done"], 1)
                for u in range(4):
                    ins = nc.tensor.matmul(ps[:, 4 * x + 3, u * P:(u + 1) * P], xs[x][:, u, :], tinvT[x][:, u, :],
                                           start=True, stop=True)
                ins.then_inc(s["xt_done"], 1)

            def apply_t(hp, r, x, n):
                s = lane[x]
                pe.wait_ge(s["tt_upd"], 6 * n + 6)
                pe.wait_ge(s["nv_out"], n + 1)
                for u, cc, c, j in units(r, x):
                    nc.tensor.matmul(ps[:, 4 * x + 1, u * P:u * P + HD], tinvT[x][:, u, :], tok[:, c, TOK_A, head(j)],
                                     start=True, stop=True)
                    ins = nc.tensor.matmul(ps[:, 4 * x + 1, u * P + HD:(u + 1) * P], tinvT[x][:, u, :],
                                           nv[x][:, u, :], start=True, stop=True)
                ins.then_inc(s["wu_done"], 1)

            def state_parts(hp, r, x, n):
                s = lane[x]
                pe.wait_ge(s["wu_out"], n + 1)
                for u, cc, c, j in units(r, x):
                    o = ps[head(j), 4 * x + 2, cc * P:(cc + 1) * P]
                    nc.tensor.matmul(o[:, 0:HD], wu[x][:, u, 0, :], tok[:, c, TOK_B, head(j)], start=True, stop=True)
                    nc.tensor.matmul(o[:, HD:P], tok[:, c, TOK_B, head(j)], wu[x][:, u, 1, :], start=True, stop=False)
                    ins = nc.tensor.matmul(o[:, HD:P], tok[:, c, TOK_K, head(j)], tok[:, c, TOK_V, head(j)],
                                           start=False, stop=True)
                ins.then_inc(s["gq_done"], 1)
                for u, cc, c, j in units(r, x):
                    ins = nc.tensor.matmul(ps[head(j), 4 * x + 3, cc * P:(cc + 1) * P], wu[x][:, u, 0, :],
                                           mm[x][:, u, K_RB, :], start=True, stop=True)
                ins.then_inc(s["rw_done"], 1)

            def chain(hp, r, x, n):
                pe.wait_ge(lane[x]["gq_out"], n + 1)
                for cc in range(2):
                    c = 4 * r + 2 * x + cc
                    if c:
                        pe.wait_ge(state_set, 8 * hp + c)
                    else:
                        pe.wait_ge(zero_set, 1)
                    nc.tensor.sem_inc(chain_open, 1)
                    for j in range(2):
                        ins = nc.tensor.matmul(ps[head(j), 4 * x, cc * HD:(cc + 1) * HD], gm[x][head(j), cc, :],
                                               state[head(j), c, :], start=True, stop=True)
                    ins.then_inc(chained, 1)

            def outputs(hp, r, x, n):
                s = lane[x]
                pe.wait_ge(s["rw_out"], n + 1)
                for u, cc, c, j in units(r, x):
                    o = ps[head(j), 4 * x + 1, cc * P:(cc + 1) * P]
                    nc.tensor.matmul(o, wu[x][:, u, 1, :], mm[x][:, u, K_RB, :], start=True, stop=False)
                    nc.tensor.matmul(o, state[head(j), c, :], rw[x][head(j), cc, :], start=False, stop=False)
                    ins = nc.tensor.matmul(o, tok[:, c, TOK_V, head(j)], mm[x][:, u, K_RK, :], start=False, stop=True)
                ins.then_inc(s["y_done"], 1)

            def group_norm(hp):
                pe.wait_ge(state_set, 8 * hp + 8)
                for x in range(LANES):
                    pe.wait_ge(lane[x]["y_out"], ROUNDS * hp + ROUNDS + PRIME_Y)
                for h in range(2):
                    nc.tensor.matmul(ps[:, h, :], heads1[:], yt[:, half(h)], start=True, stop=True).then_inc(y_mean, 1)
                for h in range(2):
                    nc.tensor.matmul(ps[:, 4 + h, :], lora[:, 1, :], m.lo[:, 1, half(h)], start=True, stop=True)\
                      .then_inc(g_done, 1)
                for h in range(2):
                    pe.wait_ge(y_sq, 2 * hp + h + 1)
                    nc.tensor.matmul(ps[:, 2 + h, :], heads1[:], tmp[:, 0, half(h)], start=True, stop=True)\
                      .then_inc(y_var, 1)

            with nc.tensor.Fori(0, PAIRS) as hp:
                front(hp)
                for r in range(ROUNDS):
                    n = ROUNDS * hp + r
                    for part in (grams, turn_t):
                        for x in range(LANES):
                            part(hp, r, x, n)
                    for lv in range(1, LEVELS):
                        for part in (level_x, level_t):
                            for x in range(LANES):
                                part(lv, hp, r, x, n)
                    for part in (apply_t, state_parts, chain, outputs):
                        for x in range(LANES):
                            part(hp, r, x, n)
                group_norm(hp)

        @block.scalar
        def _(act):
            nc.scalar.sem_inc(y_root, PRIME_ROOT)
            for x in range(LANES):
                nc.scalar.sem_inc(lane[x]["y_out"], PRIME_Y)
            act.wait_ge(const_in, 16 * N_CONST)
            with nc.scalar.Fori(0, PAIRS) as hp:
                act.wait_ge(bm_set, hp + PRIME_BM)
                for t in range(3):
                    for h in range(2):
                        act.wait_ge(raw_done, 6 * hp + 2 * t + h + 1)
                        nc.scalar.activation(raw[:, t, half(h)], ps[:, 2 * t + h, :], ACT.Copy).then_inc(raw_out, 1)
                act.wait_ge(vec_set, hp + 1)
                for q, (dst, bank, v) in enumerate(((sig, 6, V_W0), (av, 0, V_A0))):
                    for h in range(2):
                        act.wait_ge(lo_done, 4 * hp + 2 * q + h + 1)
                        nc.scalar.activation(dst[:, half(h)], ps[:, bank + h, :], ACT.Sigmoid,
                                             bias=vec[:, v:v + 1]).then_inc(lo_out, 1)
                for h in range(2):
                    act.wait_ge(kraw, hp + 1)
                    nc.scalar.activation(bonus[:, half(h)], kk[:, half(h)], ACT.Square).then_inc(ksq, 1)
                act.wait_ge(rk_ready, hp + 1)
                for h in range(2):
                    act.wait_ge(kn_sum, 2 * hp + h + 1)
                    nc.scalar.activation(spare[:, half(h)], ps[:, 4 + h, :], ACT.Sqrt).then_inc(kn_root, 1)
                act.wait_ge(lc_ready, hp + 1)
                nc.scalar.activation(dcol[:], dcol[:], ACT.Exp, scale=W_DECAY).then_inc(exps, 1)
                nc.scalar.activation(raw[:, 0, :], lc[:], ACT.Exp, scale=W_DECAY).then_inc(exps, 1)
                nc.scalar.activation(raw[:, 1, :], lc[:], ACT.Exp, scale=-W_DECAY).then_inc(exps, 1)
                nc.scalar.activation(raw[:, 2, :], tmp[:, 1, :], ACT.Exp, scale=W_DECAY).then_inc(exps, 1)
                for c in range(TT):
                    act.wait_ge(turned, 8 * hp + c + 1)
                    nc.scalar.activation(tok[:, c, :, :], ps[:, c, :], ACT.Copy).then_inc(turned_out, 1)
                for r in range(ROUNDS):
                    n = ROUNDS * hp + r
                    for x in range(LANES):
                        act.wait_ge(lane[x]["t_turned"], n + 1)
                        nc.scalar.activation(tinv[x][:], ps[:, 4 * x, :], ACT.Copy).then_inc(lane[x]["t_set"], 1)
                    for lv in range(1, LEVELS):
                        for x in range(LANES):
                            act.wait_ge(lane[x]["x_done"], 6 * n + lv)
                            nc.scalar.activation(xs[x][:], ps[:, 4 * x + 1, :], ACT.Copy).then_inc(lane[x]["x_out"], 1)
                            if lv == 1:
                                act.wait_ge(lane[x]["nv_done"], n + 1)
                                nc.scalar.activation(nv[x][:], ps[:, 4 * x, 0:4 * HD], ACT.Copy)\
                                  .then_inc(lane[x]["nv_out"], 1)
                    for x in range(LANES):
                        act.wait_ge(lane[x]["wu_done"], n + 1)
                        nc.scalar.activation(wu[x][:], ps[:, 4 * x + 1, :], ACT.Copy).then_inc(lane[x]["wu_out"], 1)
                    for x in range(LANES):
                        act.wait_ge(lane[x]["y_done"], n + 1)
                        c0 = 4 * r + 2 * x
                        nc.scalar.activation(yt[:, c0 * P:(c0 + 2) * P], ps[:, 4 * x + 1, 0:2 * P], ACT.Copy)\
                          .then_inc(lane[x]["y_out"], 1)
                for h in range(2):
                    act.wait_ge(y_cent, 2 * hp + h + 1)
                    nc.scalar.activation(tmp[:, 0, half(h)], kk[:, half(h)], ACT.Square).then_inc(y_sq, 1)
                for h in range(2):
                    act.wait_ge(y_var, 2 * hp + h + 1)
                    nc.scalar.activation(sig[:, half(h)], ps[:, 2 + h, :], ACT.Sqrt, bias=m.col[:, 4:5],
                                         scale=1.0 / HD).then_inc(y_root, 1)

        @block.gpsimd
        def _(pool):
            pool.wait_ge(const_in, 16 * N_CONST)
            with nc.gpsimd.Fori(0, PAIRS) as hp:
                pool.wait_ge(mixed, 3 * hp + 1)
                pool.wait_ge(exps, 4 * hp + 2)
                nc.gpsimd.tensor_tensor(ar[:, :, 1, :], mix[:, 0, :].rearrange("p (c t) -> p c t", c=TT),
                                        raw[:, 0, :].rearrange("p (c t) -> p c t", c=TT), ALU.mult)\
                  .then_inc(pool_factors, 1)
                pool.wait_ge(rk_ready, hp + 1)
                pool.wait_ge(exps, 4 * hp + 3)
                nc.gpsimd.tensor_tensor(kt[:], mix[:, 1, :], raw[:, 1, :], ALU.mult).then_inc(pool_factors, 1)
                for r in range(ROUNDS):
                    n = ROUNDS * hp + r
                    for lv in range(1, LEVELS):
                        for x in range(LANES):
                            pool.wait_ge(lane[x]["masked"], 4 * n + 4)
                            if lv >= 3:
                                pool.wait_ge(lane[x]["x_done"], 6 * n + lv - 2)
                            nc.gpsimd.tensor_tensor(moff[x][:, lv % 2, :, :], mm[x][:, :, K_MT, :],
                                                    lvl[:, lv:lv + 1, :].broadcast_to([P, 4, P]), ALU.mult)\
                              .then_inc(lane[x]["off"], 1)

        @block.vector
        def _(dve):
            step = Steps(dve, vstep)
            nc.vector.sem_inc(bm_set, PRIME_BM)
            nc.vector.memset(state[:, 0, :], 0.0).then_inc(zero_set, 1)
            dve.wait_ge(const_in, 16 * N_CONST)

            def col(v):
                return vec[:, v:v + 1]

            def front(hp):
                nc.vector.tensor_copy(vec[:], flat(vecs[:, bass.ds(hp, 1), :])).then_inc(vec_set, 1)
                dve.wait_ge(vec_set, hp + 1)
                for t in range(3):
                    dve.wait_ge(raw_out, 6 * hp + 2 * t + 2)
                    token_shift(nc, step, mix[:, t, :], raw[:, t, :], tmp[:, t % 2, :], col(V_MU_R + t), mixed)
                dve.wait_ge(mixed, 3 * hp + 3)
                nc.vector.tensor_scalar(kk[:], mix[:, 1, :], col(V_KK), None, ALU.mult).then_inc(kraw, 1)
                dve.wait_ge(lo_out, 4 * hp + 2)
                for c in range(TT):
                    chunk = slice(c * P, (c + 1) * P)
                    ins = nc.vector.tensor_tensor_scan(tmp[:, 0, chunk], ones[:], sig[:, chunk], 0.0, ALU.mult, ALU.add)
                step(ins)
                cum = tmp[:, 0, :].rearrange("p (c t) -> p c t", c=TT)
                lcv = lc[:].rearrange("p (c t) -> p c t", c=TT)
                step(nc.vector.tensor_tensor(lcv, cum, cum[:, :, MID:MID + 1].broadcast_to([P, TT, P]), ALU.subtract))
                nc.vector.tensor_copy(dcol[:, TT - 1:TT], lcv[:, TT - 1, P - 1:P])
                nc.vector.tensor_tensor(dcol[:, 0:TT - 1], lcv[:, 0:TT - 1, P - 1], cum[:, 1:TT, MID], ALU.add)
                nc.vector.tensor_tensor(tmp[:, 1, :], lc[:], sig[:], ALU.subtract).then_inc(lc_ready, 1)
                dve.wait_ge(lo_out, 4 * hp + 4)
                step(nc.vector.tensor_scalar(spare[:], av[:], 1.0, col(V_KA), ALU.subtract, ALU.mult))
                step(nc.vector.scalar_tensor_tensor(out=mix[:, 1, :], in0=spare[:], scalar=1.0, in1=mix[:, 1, :],
                                                    op0=ALU.add, op1=ALU.mult))
                nc.vector.scalar_tensor_tensor(out=tmp[:, 0, :], in0=mix[:, 0, :], scalar=col(V_RK), in1=mix[:, 1, :],
                                               op0=ALU.mult, op1=ALU.mult).then_inc(rk_ready, 1)
                dve.wait_ge(kn_root, 2 * hp + 2)
                step(nc.vector.tensor_scalar(spare[:], spare[:], 1e-12, None, ALU.max))
                step(nc.vector.reciprocal(spare[:], spare[:]))
                step(nc.vector.tensor_tensor(kk[:], kk[:], spare[:], ALU.mult))
                step(nc.vector.tensor_tensor(av[:], av[:], kk[:], ALU.mult))
                dve.wait_ge(exps, 4 * hp + 4)
                nc.vector.tensor_tensor(bt[:], av[:], raw[:, 1, :], ALU.mult).then_inc(factors, 1)
                nc.vector.scalar_tensor_tensor(out=ar[:, :, 0, :], in0=kk[:].rearrange("p (c t) -> p c t", c=TT),
                                               scalar=-1.0, in1=raw[:, 2, :].rearrange("p (c t) -> p c t", c=TT),
                                               op0=ALU.mult, op1=ALU.mult).then_inc(factors, 1)
                for h in range(2):
                    dve.wait_ge(rk_sum, 2 * hp + h + 1)
                    nc.vector.tensor_tensor(bonus[:, half(h)], ps[:, 6 + h, :], mix[:, 2, half(h)], ALU.mult)\
                      .then_inc(bonus_set, 1)

            def masks(hp, r, x, n):
                s = lane[x]
                dve.wait_ge(s["y_out"], n + PRIME_Y)
                for u in range(4):
                    dve.wait_ge(s["gram"], 4 * n + u + 1)
                    nc.vector.tensor_tensor(mm[x][:, u, :, :], ps[:, 4 * x + u, :], mask4[:], ALU.mult)\
                      .then_inc(s["masked"], 1)

            def blocks_of_2(hp, r, x, n):
                s = lane[x]
                dve.wait_ge(s["masked"], 4 * n + 4)
                step(nc.vector.tensor_tensor(tinvT[x][:], mm[x][:, :, K_MT, :], lvl[:, 0:1, :].broadcast_to([P, 4, P]),
                                             ALU.mult))
                nc.vector.tensor_tensor(tinvT[x][:], tinvT[x][:],
                                        m.ident[:].rearrange("p (a n) -> p a n", a=1).broadcast_to([P, 4, P]),
                                        ALU.add).then_inc(s["tt_set"], 1)

            def grow(lv, hp, r, x, n):
                s = lane[x]
                if lv < LEVELS - 1:
                    dve.wait_ge(s["tx_done"], 5 * n + lv)
                    nc.vector.tensor_tensor(tinv[x][:], ps[:, 4 * x + 2, :], tinv[x][:], ALU.add)\
                      .then_inc(s["t_upd"], 1)
                dve.wait_ge(s["xt_done"], 6 * n + lv)
                nc.vector.tensor_tensor(tinvT[x][:], ps[:, 4 * x + 3, :], tinvT[x][:], ALU.add)\
                  .then_inc(s["tt_upd"], 1)

            def state_parts(hp, r, x, n):
                s = lane[x]
                dve.wait_ge(s["gq_done"], n + 1)
                parts = ps[:, 4 * x + 2, 0:2 * P].rearrange("p (c n) -> p c n", c=2)
                nc.vector.tensor_tensor(gm[x][:], parts[:, :, 0:HD],
                                        eye2[:].rearrange("p (a n) -> p a n", a=1).broadcast_to([P, 2, HD]), ALU.add)
                for cc in range(2):
                    c = 4 * r + 2 * x + cc
                    ins = nc.vector.tensor_scalar(qd[x][:, cc, :], parts[:, cc, HD:P], dcol[:, c:c + 1], None, ALU.mult)
                ins.then_inc(s["gq_out"], 1)
                dve.wait_ge(s["rw_done"], n + 1)
                c0 = 4 * r + 2 * x
                nc.vector.tensor_tensor(rw[x][:], ps[:, 4 * x + 3, 0:2 * P].rearrange("p (c n) -> p c n", c=2),
                                        ar[:, c0:c0 + 2, 1, :], ALU.add).then_inc(s["rw_out"], 1)

            def chain(hp, r, x, n):
                dve.wait_ge(lane[x]["gq_out"], n + 1)
                for cc in range(2):
                    c = 4 * r + 2 * x + cc
                    dve.wait_ge(chained, 8 * hp + c + 1)
                    nc.vector.scalar_tensor_tensor(out=state[:, c + 1, :], in0=ps[:, 4 * x, cc * HD:(cc + 1) * HD],
                                                   scalar=dcol[:, c:c + 1], in1=qd[x][:, cc, :], op0=ALU.mult,
                                                   op1=ALU.add).then_inc(state_set, 1)

            def group_norm(hp):
                for h in range(2):
                    dve.wait_ge(y_mean, 2 * hp + h + 1)
                    nc.vector.scalar_tensor_tensor(out=kk[:, half(h)], in0=ps[:, h, :], scalar=-1.0 / HD,
                                                   in1=yt[:, half(h)], op0=ALU.mult, op1=ALU.add).then_inc(y_cent, 1)
                dve.wait_ge(y_root, 2 * hp + 2 + PRIME_ROOT)
                step(nc.vector.reciprocal(sig[:], sig[:]))
                step(nc.vector.tensor_tensor(kk[:], kk[:], sig[:], ALU.mult))
                step(nc.vector.tensor_scalar(kk[:], kk[:], col(V_LNW), col(V_LNB), ALU.mult, ALU.add))
                step(nc.vector.tensor_tensor(kk[:], kk[:], bonus[:], ALU.add))
                dve.wait_ge(g_done, 2 * hp + 2)
                nc.vector.tensor_tensor(flat(m.bmT[:, bass.ds(hp, 1), :]), ps[:, 4:6, :].rearrange("p a n -> p (a n)"),
                                        kk[:], ALU.mult).then_inc(bm_set, 1)
                dve.wait_ge(bm_set, hp + 1 + PRIME_BM)

            with nc.vector.Fori(0, PAIRS) as hp:
                step.enter(hp, RECUR_STEPS)
                front(hp)
                for r in range(ROUNDS):
                    n = ROUNDS * hp + r
                    for part in (masks, blocks_of_2):
                        for x in range(LANES):
                            part(hp, r, x, n)
                    for lv in range(1, LEVELS):
                        for x in range(LANES):
                            grow(lv, hp, r, x, n)
                    for part in (state_parts, chain):
                        for x in range(LANES):
                            part(hp, r, x, n)
                group_norm(hp)
                step.leave(PAIRS)


MAGIC = 1.5 * 2.0 ** 23
TWO_PI_PARTS = (6.28125, 0.0019350051879882812, 3.0198870e-07)
PI_IN = 3.1415925


def stage_project(nc, g, m):
    with ExitStack() as ctx:
        sb, psum, sem = allocators(nc, ctx)
        ps = psum("ps_proj", [P, 8, HALF])
        wslot = sb("wslot_p", [P, 2, KT * P])
        wtok = sb("wtok", [P, KT, TOKW])
        pos = sb("pos_i", [P, S], I32)
        angle = sb("angle", [P, S])
        turns = sb("turns", [P, S])
        cos_t = sb("cos_t", [P, S])
        sin_t = sb("sin_t", [P, S])
        swap = sb("swap", [P, 2, S])
        prod = sb("prod", [P, 2, S])
        paired = sb("paired", [P, 2, S])
        blk = sb("blk", [P, 16, 2, N_CMP])
        pe_t = sb("pe_t", [P, 2, 16])
        cw1 = sb("cw1", [P, 16, CMP_HID])
        cw2 = sb("cw2", [P, 2, 2, HD])
        cb1 = sb("cb1", [P, 2, 2])
        cb2k = sb("cb2k", [HD, 1])
        cb2v = sb("cb2v", [1, HD])
        one_row = sb("one_row", [1, HD])
        hid = sb("hid", [P, 2, 2 * N_CMP])

        small_in, wtok_in, cw1_in = sem("small_in_p"), sem("wtok_in"), sem("cw1_in")
        w_in = [sem(f"w_in_p{s}") for s in range(2)]
        tile_done, tile_out, vtok_done, vtok_out = sem("tile_done"), sem("tile_out"), sem("vtok_done"), sem("vtok_out")
        reduced, absed, tables = sem("reduced"), sem("absed"), sem("tables")
        swapped = [sem(f"swapped{s}") for s in range(2)]
        sin_prod, rotated, paired_in, blk_set = sem("sin_prod"), sem("rotated"), sem("paired_in"), sem("blk_set")
        row_set, hid_done, gelu_out, cmp_done, cmp_out = (sem(n) for n in ("row_set", "hid_done", "gelu_out", "cmp_done",
                                                                           "cmp_out"))
        vstep = sem("vstep_p")
        PRIME_TILE = 4
        TURNS = N_QKV // 2
        VC = N_QKV - 1
        N_SMALL = 6
        block = ctx.enter_context(nc.Block())

        def half(h):
            return slice(h * HALF, (h + 1) * HALF)

        def pair_up(sy, src):
            for grp in range(2):
                rows = slice(HD * grp, HD * grp + HD)
                sy.dma_start(paired[0:HD, grp, :], src[rows, :]).then_inc(paired_in, 16)
                sy.dma_start(paired[HD:P, grp, 0:S - 1], src[rows, 1:S]).then_inc(paired_in, 16)

        @block.sync
        def _(sy):
            sy.dma_start(pos[:], g.pos).then_inc(small_in, 16)
            for s in range(2):
                sy.dma_start(wslot[:, s, :], g.w_tiles[:, T_QKV + s, :]).then_inc(w_in[s], 16)
            for dst, src in ((pe_t[:], g.cmp_pe), (cw2[:], g.cmp_w2), (cb1[:], g.cmp_b1), (cb2k[:], g.cmp_b2k),
                             (cb2v[:], g.cmp_b2v)):
                sy.dma_start(dst, src).then_inc(small_in, 16)
            sy.dma_start(wtok[:], g.w_tok).then_inc(wtok_in, 16)
            sy.dma_start(cw1[:], g.cmp_w1[0]).then_inc(cw1_in, 16)
            with nc.sync.Fori(1, TURNS) as i:
                for s in range(2):
                    sy.wait_ge(tile_done, 4 * i + 2 * s - 2 + PRIME_TILE)
                    sy.dma_start(wslot[:, s, :], flat(g.w_tiles[:, bass.ds(2 * i + T_QKV + s, 1), :]))\
                      .then_inc(w_in[s], 16)
            for t in range(N_ROPE):
                sy.wait_ge(tile_out, 2 * (t + 1) + PRIME_TILE)
                if t >= 2:
                    sy.wait_ge(sin_prod, t - 1)
                for q in range(4):
                    o = q ^ 1
                    sy.dma_start(swap[32 * q:32 * q + 32, t % 2, :], m.qkv[32 * o:32 * o + 32, t, :])\
                      .then_inc(swapped[t % 2], 16)
                if t == 2:
                    sy.wait_ge(rotated, 1)
                    pair_up(sy, m.qkv[:, 0, :])
            sy.wait_ge(tile_out, 2 * (VC + 1) + PRIME_TILE)
            sy.wait_ge(blk_set, 1)
            pair_up(sy, m.qkv[:, VC, :])
            sy.wait_ge(hid_done, 1)
            sy.dma_start(cw1[:], g.cmp_w1[1]).then_inc(cw1_in, 16)

        @block.tensor
        def _(pe):
            nc.tensor.sem_inc(tile_done, PRIME_TILE)
            with nc.tensor.Fori(0, TURNS) as i:
                for s in range(2):
                    pe.wait_ge(w_in[s], 16 * i + 16)
                    for h in range(2):
                        pe.wait_ge(tile_out, 4 * i + 2 * s + h + 1)
                        for k in range(KT):
                            ins = nc.tensor.matmul(ps[:, 2 * s + h, :], wslot[:, s, k * P:(k + 1) * P],
                                                   m.hT[:, k, half(h)], start=(k == 0), stop=(k == KT - 1))
                        ins.then_inc(tile_done, 1)
            pe.wait_ge(wtok_in, 16)
            for t in range(TT):
                if t >= 2:
                    pe.wait_ge(vtok_out, t - 1)
                for k in range(KT):
                    ins = nc.tensor.matmul(ps[:, 4 + t % 2, 0:TOKW], m.hT[:, k, t * P:(t + 1) * P], wtok[:, k, :],
                                           start=(k == 0), stop=(k == KT - 1))
                ins.then_inc(vtok_done, 1)
            pe.wait_ge(small_in, 16 * N_SMALL)
            pe.wait_ge(row_set, 1)
            for kv in range(2):
                pe.wait_ge(cw1_in, 16 * (kv + 1))
                pe.wait_ge(blk_set, kv + 1)
                for f in range(2):
                    for c in range(16):
                        ins = nc.tensor.matmul(ps[:, 6, f * 2 * N_CMP:(f + 1) * 2 * N_CMP], cw1[:, c, f * P:(f + 1) * P],
                                               blk[:, c, :, :], start=(c == 0), stop=(c == 15))
                ins.then_inc(hid_done, 1)
                pe.wait_ge(gelu_out, 2 * kv + 2)
                if kv == 0:
                    for f in range(2):
                        ins = nc.tensor.matmul(ps[0:HD, 7, 0:2 * N_CMP], cw2[:, 0, f, :], hid[:, f, :],
                                               start=(f == 0), stop=(f == 1))
                    ins.then_inc(cmp_done, 1)
                else:
                    pe.wait_ge(cmp_out, 1)
                    for grp in range(2):
                        o = ps[0:N_CMP, 7, grp * HD:(grp + 1) * HD]
                        for f in range(2):
                            nc.tensor.matmul(o, hid[:, f, grp * N_CMP:(grp + 1) * N_CMP], cw2[:, 1, f, :],
                                             start=(f == 0), stop=False)
                        ins = nc.tensor.matmul(o, one_row[0:1, 0:N_CMP], cb2v[:], start=False, stop=True)
                    ins.then_inc(cmp_done, 1)

        @block.scalar
        def _(act):
            nc.scalar.sem_inc(tile_out, PRIME_TILE)
            act.wait_ge(reduced, 1)
            nc.scalar.activation(turns[:], angle[:], ACT.Abs).then_inc(absed, 1)
            nc.scalar.activation(sin_t[:], angle[:], ACT.Sin, scale=m.col[:, 1:2]).then_inc(tables, 1)
            act.wait_ge(absed, 1)
            nc.scalar.activation(cos_t[:], turns[:], ACT.Sin, bias=m.col[:, 2:3], scale=-1.0).then_inc(tables, 1)
            with nc.scalar.Fori(0, TURNS) as i:
                for s in range(2):
                    for h in range(2):
                        act.wait_ge(tile_done, 4 * i + 2 * s + h + 1 + PRIME_TILE)
                        nc.scalar.activation(flat(m.qkv[:, bass.ds(2 * i + s, 1), half(h)]), ps[:, 2 * s + h, :],
                                             ACT.Copy).then_inc(tile_out, 1)
            for t in range(TT):
                act.wait_ge(vtok_done, t + 1)
                nc.scalar.activation(m.vtok[:, t, :], ps[:, 4 + t % 2, 0:2 * P], ACT.Copy)
                nc.scalar.activation(m.gates[:, t, :], ps[:, 4 + t % 2, 2 * P:TOKW], ACT.Sigmoid).then_inc(vtok_out, 1)
            act.wait_ge(small_in, 16 * N_SMALL)
            for kv in range(2):
                act.wait_ge(hid_done, kv + 1)
                if kv:
                    act.wait_ge(cmp_done, 1)
                for f in range(2):
                    nc.scalar.activation(hid[:, f, :], ps[:, 6, f * 2 * N_CMP:(f + 1) * 2 * N_CMP], ACT.Gelu_apprx_tanh,
                                         bias=cb1[:, kv, f:f + 1]).then_inc(gelu_out, 1)
                act.wait_ge(cmp_done, kv + 1)
                if kv == 0:
                    for grp in range(2):
                        ins = nc.scalar.activation(m.kcmp[HD * grp:HD * grp + HD, :],
                                                   ps[0:HD, 7, grp * N_CMP:(grp + 1) * N_CMP], ACT.Identity, bias=cb2k[:])
                else:
                    ins = nc.scalar.activation(m.vcmp[0:N_CMP, :, :], ps[0:N_CMP, 7, 0:2 * HD], ACT.Copy)
                ins.then_inc(cmp_out, 1)
            act.wait_ge(cmp_out, 2)

        @block.gpsimd
        def _(pool):
            nc.gpsimd.memset(one_row[:], 1.0).then_inc(row_set, 1)
            pool.wait_ge(tables, 2)
            for t in range(N_ROPE):
                pool.wait_ge(swapped[t % 2], 64 * (t // 2 + 1))
                if t >= 2:
                    pool.wait_ge(rotated, t - 1)
                nc.gpsimd.tensor_tensor(prod[:, t % 2, :], swap[:, t % 2, :], sin_t[:], ALU.mult).then_inc(sin_prod, 1)

        @block.vector
        def _(dve):
            step = Steps(dve, vstep)
            dve.wait_ge(small_in, 16 * N_SMALL)
            step(nc.vector.tensor_copy(angle[:], pos[:]))
            step(nc.vector.tensor_scalar(angle[:], angle[:], m.col[:, 0:1], None, ALU.mult))
            step(nc.vector.tensor_scalar(turns[:], angle[:], 1.0 / (2 * math.pi), MAGIC, ALU.mult, ALU.add))
            step(nc.vector.tensor_scalar(turns[:], turns[:], MAGIC, None, ALU.subtract))
            for part in TWO_PI_PARTS:
                step(nc.vector.scalar_tensor_tensor(out=angle[:], in0=turns[:], scalar=-part, in1=angle[:],
                                                    op0=ALU.mult, op1=ALU.add))
            nc.vector.tensor_scalar(angle[:], angle[:], PI_IN, -PI_IN, ALU.min, ALU.max).then_inc(reduced, 1)
            dve.wait_ge(tables, 2)

            def blocks(kv):
                dve.wait_ge(paired_in, 64 * (kv + 1))
                if kv:
                    dve.wait_ge(hid_done, 1)
                for c in range(16):
                    ins = nc.vector.tensor_scalar(blk[:, c, :, :], paired[:, :, 2 * c:2 * c + 16 * (N_CMP - 1) + 1:16],
                                                  pe_t[:, kv, c:c + 1], None, ALU.add)
                ins.then_inc(blk_set, 1)

            for t in range(N_ROPE):
                dve.wait_ge(swapped[t % 2], 64 * (t // 2 + 1))
                step(nc.vector.tensor_tensor(m.qkv[:, t, :], m.qkv[:, t, :], cos_t[:], ALU.mult))
                dve.wait_ge(sin_prod, t + 1)
                nc.vector.tensor_tensor(m.qkv[:, t, :], m.qkv[:, t, :], prod[:, t % 2, :], ALU.add).then_inc(rotated, 1)
            blocks(0)
            blocks(1)
            dve.wait_ge(rotated, N_ROPE)


WIN_TILES = 4


def attention_units():
    units, chunks = [], 0
    for j in range(2):
        for qt in range(TT):
            for br, name in enumerate(("cmp", "slc", "win")):
                first = max(0, qt - WIN_TILES) if name == "win" else 0
                tiles = [None] if name == "cmp" else list(range(first, qt + 1))
                u = Names()
                u.n, u.j, u.qt, u.name, u.tiles, u.slot = len(units), j, qt, name, tiles, br
                u.gate = BRANCH_GATE[name]
                u.first_chunk = chunks
                u.chunks = [tiles[a:a + 4] for a in range(0, len(tiles), 4)]
                u.cols = N_CMP if name == "cmp" else P * len(tiles)
                chunks += len(u.chunks)
                units.append(u)
    return units, chunks


BRANCH_GATE = {"cmp": 0, "slc": 1, "win": 2}
AHEAD = 3


def stage_attend(nc, g, m):
    units, N_CHUNK = attention_units()
    N_UNIT = len(units)
    with ExitStack() as ctx:
        sb, psum, sem = allocators(nc, ctx)
        scores = [psum("ps_s_cmp", [P, HALF]), psum("ps_s_slc", [P, 2 * HALF]), psum("ps_s_win", [P, 2 * HALF])]
        ps_pt = psum("ps_pt", [P, 2, HALF])
        ps_o = psum("ps_o", [P, HALF])
        qcur = sb("qcur", [P, 2, S])
        gcur = sb("gcur", [P, TT, 2, 3])
        bias = sb("bias", [P, 2, P])
        bias_cmp = sb("bias_cmp", [P, TT, N_CMP])
        prob = [sb("prob_cmp", [P, N_CMP]), sb("prob_slc", [P, S]), sb("prob_win", [P, (WIN_TILES + 1) * P])]
        pt = sb("pt", [P, 2, HALF])
        nmax = sb("nmax", [P, AHEAD])
        rowsum = sb("rowsum", [P, AHEAD])
        weight = sb("weight", [P, AHEAD])

        const_in, q_set, copied, g_set = sem("const_in_t"), sem("q_set"), sem("g_copied"), sem("g_set")
        scored, biased, nmax_set, exp_done = sem("scored"), sem("biased"), sem("nmax_set"), sem("exp_done")
        pt_done, pt_out, o_done, weight_set, scaled, o_used = (sem(n) for n in ("pt_done", "pt_out", "o_done",
                                                                                "weight_set", "scaled", "o_used"))
        turn_open = sem("turn_open")
        block = ctx.enter_context(nc.Block())
        PRIME_U, PRIME_C, PRIME_O = AHEAD, 2, 1
        N_OUT = 2 * TT

        def head(j):
            return slice(HD * j, HD * j + HD)

        @block.sync
        def _(sy):
            sy.dma_start(bias[:], g.bias).then_inc(const_in, 16)
            sy.dma_start(bias_cmp[:], g.bias_cmp).then_inc(const_in, 16)

        @block.tensor
        def _(pe):
            def score(i, u):
                if u.n == 0:
                    pe.wait_ge(q_set, i + 1)
                pe.wait_ge(exp_done, N_UNIT * i + u.n - AHEAD + 1 + PRIME_U)
                q = qcur[:, u.j, u.qt * P:(u.qt + 1) * P]
                o = scores[u.slot]
                if u.name == "cmp":
                    ins = nc.tensor.matmul(o[:, 0:N_CMP], q, m.kcmp[:], start=True, stop=True)
                else:
                    keys = m.qkv[:, 1 if u.name == "slc" else 2, :]
                    for a in range(0, u.cols, HALF):
                        w = min(HALF, u.cols - a)
                        k0 = u.tiles[0] * P + a
                        ins = nc.tensor.matmul(o[:, a:a + w], q, keys[:, k0:k0 + w], start=True, stop=True)
                ins.then_inc(scored, 1)

            def turn(i, u, c):
                e = N_CHUNK * i + u.first_chunk + c
                if c == 0:
                    pe.wait_ge(scaled, N_UNIT * i + u.n + 1)
                slot = (u.first_chunk + c) % 2
                pe.wait_ge(pt_out, e - 2 + 1 + PRIME_C)
                if u.name == "cmp":
                    nc.tensor.sem_inc(turn_open, 1)
                for b, _ in enumerate(u.chunks[c]):
                    if u.name == "cmp":
                        ins = nc.tensor.transpose(ps_pt[0:N_CMP, slot, 0:P], prob[u.slot][:], m.ident[:])
                    else:
                        a = (4 * c + b) * P
                        ins = nc.tensor.transpose(ps_pt[:, slot, b * P:(b + 1) * P], prob[u.slot][:, a:a + P],
                                                  m.ident[:])
                ins.then_inc(pt_done, 1)

            def weigh(i, u, c):
                e = N_CHUNK * i + u.first_chunk + c
                slot = (u.first_chunk + c) % 2
                if u.name == "cmp":
                    pe.wait_ge(o_used, N_OUT * i + u.n // AHEAD + PRIME_O)
                pe.wait_ge(pt_out, e + 1 + PRIME_C)
                if u.name == "cmp":
                    nc.tensor.sem_inc(turn_open, 1)
                o = ps_o[0:HD, 0:P]
                for b, t in enumerate(u.chunks[c]):
                    if u.name == "cmp":
                        ins = nc.tensor.matmul(o, m.vcmp[0:N_CMP, u.j, :], pt[0:N_CMP, slot, 0:P], start=True, stop=False)
                    else:
                        v0 = (0 if u.name == "slc" else P) + u.j * HD
                        last = u.name == "win" and t == u.tiles[-1]
                        ins = nc.tensor.matmul(o, m.vtok[:, t, v0:v0 + HD], pt[:, slot, b * P:(b + 1) * P],
                                               start=False, stop=last)
                        if last:
                            ins.then_inc(o_done, 1)

            pe.wait_ge(const_in, 32)
            with nc.tensor.Fori(0, PAIRS) as i:
                for u in units[:AHEAD]:
                    score(i, u)
                for u in units:
                    n = len(u.chunks)
                    turn(i, u, 0)
                    if u.n + AHEAD < N_UNIT:
                        score(i, units[u.n + AHEAD])
                    for c in range(n):
                        if c + 1 < n:
                            turn(i, u, c + 1)
                        weigh(i, u, c)

        @block.scalar
        def _(act):
            nc.scalar.sem_inc(exp_done, PRIME_U)
            nc.scalar.sem_inc(pt_out, PRIME_C)
            with nc.scalar.Fori(0, PAIRS) as i:
                def softmax(u):
                    act.wait_ge(nmax_set, N_UNIT * i + u.n + 1)
                    s = u.slot
                    if u.n >= AHEAD:
                        b = units[u.n - AHEAD]
                        act.wait_ge(pt_done, N_CHUNK * i + b.first_chunk + len(b.chunks))
                    nc.scalar.activation(prob[s][:, 0:u.cols], scores[s][:, 0:u.cols], ACT.Exp, bias=nmax[:, s:s + 1],
                                         accum_out=rowsum[:, s:s + 1]).then_inc(exp_done, 1)

                def copy_pt(u, c):
                    e = N_CHUNK * i + u.first_chunk + c
                    slot = (u.first_chunk + c) % 2
                    act.wait_ge(pt_done, e + 1)
                    rows = N_CMP if u.name == "cmp" else P
                    w = P * len(u.chunks[c])
                    nc.scalar.activation(pt[0:rows, slot, 0:w], ps_pt[0:rows, slot, 0:w], ACT.Copy).then_inc(pt_out, 1)

                softmax(units[0])
                softmax(units[1])
                for u in units:
                    for c in range(len(u.chunks)):
                        copy_pt(u, c)
                    if u.n + 2 < N_UNIT:
                        softmax(units[u.n + 2])

        @block.vector
        def _(dve):
            nc.vector.sem_inc(o_used, PRIME_O)
            for j in range(2):
                nc.vector.memset(qcur[head(1 - j), j, :], 0.0)
            dve.wait_ge(const_in, 32)
            with nc.vector.Fori(0, PAIRS) as i:
                dve.wait_ge(o_used, N_OUT * i + PRIME_O)
                for j in range(2):
                    ins = nc.vector.tensor_scalar(qcur[head(j), j, :], flat(m.qkv[head(j), bass.ds(i + 3, 1), :]),
                                                  HD ** -0.5, None, ALU.mult)
                ins.then_inc(q_set, 1)
                for j in range(2):
                    ins = nc.vector.tensor_copy(gcur[:, :, j, :], m.gates[:, :, bass.ds(i * 3 + 3 * PAIRS * j, 3)])
                ins.then_inc(copied, 1)
                dve.wait_ge(copied, i + 1)
                nc.vector.tensor_scalar(gcur[:, 0, :, BRANCH_GATE["cmp"]], gcur[:, 0, :, BRANCH_GATE["cmp"]],
                                        m.col[:, 5:6], None, ALU.mult).then_inc(g_set, 1)
                dve.wait_ge(g_set, i + 1)

                def maximum(u):
                    n = N_UNIT * i + u.n
                    s = u.slot
                    dve.wait_ge(scored, n + 1)
                    if u.name == "cmp":
                        o, b = scores[s][:, 0:N_CMP], bias_cmp[:, u.qt, :]
                    elif u.name == "win" and len(u.tiles) == WIN_TILES + 1:
                        o = scores[s][:, 0:u.cols].rearrange("p (t k) -> p t k", k=P)[:, 0:WIN_TILES + 1:WIN_TILES, :]
                        b = bias[:]
                    else:
                        o, b = scores[s][:, u.cols - P:u.cols], bias[:, 1, :]
                    nc.vector.tensor_tensor(o, o, b, ALU.add).then_inc(biased, 1)
                    dve.wait_ge(biased, n + 1)
                    nc.vector.tensor_reduce(nmax[:, s:s + 1], scores[s][:, 0:u.cols], AXX, ALU.max, negate=True)\
                      .then_inc(nmax_set, 1)

                def scale(u):
                    n = N_UNIT * i + u.n
                    s = u.slot
                    dve.wait_ge(exp_done, n + 1 + PRIME_U)
                    nc.vector.reciprocal(weight[:, s:s + 1], rowsum[:, s:s + 1]).then_inc(weight_set, 1)
                    dve.wait_ge(weight_set, n + 1)
                    p, gate = prob[s][:, 0:u.cols], gcur[:, u.qt, u.j, u.gate:u.gate + 1]
                    nc.vector.tensor_scalar(p, p, weight[:, s:s + 1], gate, ALU.mult, ALU.mult).then_inc(scaled, 1)

                def output(u):
                    dve.wait_ge(o_done, N_OUT * i + u.n // AHEAD + 1)
                    nc.vector.tensor_copy(flat(m.oAT[head(u.j), bass.ds(i, 1), u.qt * P:(u.qt + 1) * P]),
                                          ps_o[0:HD, 0:P]).then_inc(o_used, 1)

                for u in units[:AHEAD]:
                    maximum(u)
                scale(units[0])
                for u in units:
                    if u.n + 1 < N_UNIT:
                        scale(units[u.n + 1])
                    if u.n + AHEAD < N_UNIT:
                        maximum(units[u.n + AHEAD])
                    if u.name == "win":
                        output(u)
            dve.wait_ge(o_used, PAIRS * N_OUT + PRIME_O)


def stage_merge(nc, g, m):
    with ExitStack() as ctx:
        sb, psum, sem = allocators(nc, ctx)
        ps = psum("ps_merge", [P, 8, HALF])
        wg = sb("wg", [P, 2, 2, KT * P])
        wab = sb("wab", [P, 2, 2 * PAIRS, P])
        sg = sb("sg", [P, 2, 2, HALF])
        part = sb("part", [P, 2, 2, HALF])
        w_in = [sem(f"w_in_m{s}") for s in range(2)]
        gated, sig_out, projected, weighed, merged = (
            sem(n) for n in ("gated", "sig_out", "projected", "weighed", "merged"))
        PRIME = 2
        TURNS = KT // 2
        block = ctx.enter_context(nc.Block())

        def half(h):
            return slice(h * HALF, (h + 1) * HALF)

        def load(sy, f, s):
            sy.dma_start(wg[:, s, :, :], g.w_tiles[:, bass.ds(2 * f + T_GATE, 2), :]).then_inc(w_in[s], 16)
            sy.dma_start(wab[:, s, :, :], g.w_ab[:, bass.ds(f * 8, 8), :]).then_inc(w_in[s], 16)

        @block.sync
        def _(sy):
            for s in range(2):
                load(sy, s, s)
            with nc.sync.Fori(1, TURNS) as i:
                for s in range(2):
                    sy.wait_ge(projected, 4 * i + 2 * s - 2)
                    load(sy, 2 * i + s, s)

        @block.tensor
        def _(pe):
            with nc.tensor.Fori(0, TURNS) as i:
                for s in range(2):
                    pe.wait_ge(w_in[s], 32 * i + 32)
                    for h in range(2):
                        n = 4 * i + 2 * s + h
                        pe.wait_ge(merged, n - 1 + PRIME)
                        for q in range(2):
                            for k in range(KT):
                                ins = nc.tensor.matmul(ps[:, 4 * h + q, :], wg[:, s, q, k * P:(k + 1) * P],
                                                       m.hT[:, k, half(h)], start=(k == 0), stop=(k == KT - 1))
                        ins.then_inc(gated, 1)
                        for q, src in enumerate((m.oAT, m.bmT)):
                            for k in range(PAIRS):
                                ins = nc.tensor.matmul(ps[:, 4 * h + 2 + q, :], wab[:, s, q * PAIRS + k, :],
                                                       src[:, k, half(h)], start=(k == 0), stop=(k == PAIRS - 1))
                        ins.then_inc(projected, 1)

        @block.scalar
        def _(act):
            with nc.scalar.Fori(0, TURNS) as i:
                for s in range(2):
                    for h in range(2):
                        act.wait_ge(gated, 4 * i + 2 * s + h + 1)
                        nc.scalar.activation(sg[:, h, :, :], ps[:, 4 * h:4 * h + 2, :], ACT.Sigmoid).then_inc(sig_out, 1)

        @block.vector
        def _(dve):
            nc.vector.sem_inc(merged, PRIME)
            with nc.vector.Fori(0, TURNS) as i:
                for s in range(2):
                    for h in range(2):
                        n = 4 * i + 2 * s + h
                        dve.wait_ge(sig_out, n + 1)
                        dve.wait_ge(projected, n + 1)
                        nc.vector.tensor_tensor(part[:, h, :, :], ps[:, 4 * h + 2:4 * h + 4, :], sg[:, h, :, :],
                                                ALU.mult).then_inc(weighed, 1)
                        dve.wait_ge(weighed, n + 1)
                        nc.vector.tensor_tensor(flat(m.mT[:, bass.ds(2 * i + s, 1), half(h)]), part[:, h, 0, :],
                                                part[:, h, 1, :], ALU.add).then_inc(merged, 1)
            dve.wait_ge(merged, 4 * TURNS + PRIME)


def stage_output(nc, g, m):
    with ExitStack() as ctx:
        sb, psum, sem = allocators(nc, ctx)
        ps = psum("ps_out", [P, 8, HALF])
        wout = sb("wout", [P, KT, D])
        gffn = sb("gffn", [P, D])
        wrt = sb("wrt", [P, KT, N_LOG])
        brt = sb("brt", [1, N_LOG])
        one_row = sb("one_row_o", [1, P])
        square = sb("square_o", [P, D])
        ss = sb("ss", [P, TT, 3])
        h2 = sb("h2", [P, 2, D])
        h2T = sb("h2T", [P, 2, D])
        small_in = sem("small_in_o")
        w_in = [sem(f"w_in_o{k}") for k in range(KT)]
        x_in = [sem(f"x_in_o{t}") for t in range(TT)]
        row_set, summed, x2_set, squared, rooted, inv_set, h2_set, turned, turned_out, logit_done, logit_out = (
            sem(n) for n in ("row_set_o", "summed_o", "x2_set", "squared_o", "rooted_o", "inv_set_o", "h2_set",
                             "turned_o", "turned_out_o", "logit_done", "logit_out"))
        h2_stored = [sem(f"h2_stored{s}") for s in range(2)]
        block = ctx.enter_context(nc.Block())

        @block.sync
        def _(sy):
            for k in range(KT):
                sy.dma_start(wout[:, k, :], g.w_out[:, k, :]).then_inc(w_in[k], 16)
                if k < 2:
                    sy.dma_start(m.x2[:, k, :], g.x[k * P:(k + 1) * P, :]).then_inc(x_in[k], 16)
            for dst, src in ((gffn[:], g.gffn), (wrt[:], g.w_rt), (brt[:], g.b_rt)):
                sy.dma_start(dst, src).then_inc(small_in, 16)
            for t in range(2, TT):
                sy.dma_start(m.x2[:, t, :], g.x[t * P:(t + 1) * P, :]).then_inc(x_in[t], 16)
            for t in range(TT):
                sy.wait_ge(h2_set, t + 1)
                sy.dma_start(g.h2[t * P:(t + 1) * P, :], h2[:, t % 2, :]).then_inc(h2_stored[t % 2], 16)
            for s in range(2):
                sy.wait_ge(h2_stored[s], 16 * TT // 2)

        @block.tensor
        def _(pe):
            def project(t):
                if t >= 2:
                    pe.wait_ge(x2_set, t - 1)
                for k in range(KT):
                    pe.wait_ge(w_in[k], 16)
                    for h in range(2):
                        ins = nc.tensor.matmul(ps[:, 2 * (t % 2) + h, :], m.mT[:, k, t * P:(t + 1) * P],
                                               wout[:, k, h * HALF:(h + 1) * HALF], start=(k == 0), stop=(k == KT - 1))
                ins.then_inc(summed, 1)

            def turn(t):
                pe.wait_ge(h2_set, t + 1)
                if t >= 1:
                    pe.wait_ge(turned_out, 2 * t)
                for k in range(KT):
                    ins = nc.tensor.transpose(ps[:, 4 + k // 4, (k % 4) * P:(k % 4 + 1) * P],
                                              h2[:, t % 2, k * P:(k + 1) * P], m.ident[:])
                    if k % 4 == 3:
                        ins.then_inc(turned, 1)

            def logits(t):
                pe.wait_ge(turned_out, 2 * t + 2)
                if t >= 2:
                    pe.wait_ge(logit_out, t - 1)
                o = ps[:, 6 + t % 2, 0:N_LOG]
                for k in range(KT):
                    nc.tensor.matmul(o, h2T[:, t % 2, k * P:(k + 1) * P], wrt[:, k, :], start=(k == 0), stop=False)
                nc.tensor.matmul(o, one_row[:], brt[:], start=False, stop=True).then_inc(logit_done, 1)

            project(0)
            project(1)
            pe.wait_ge(small_in, 48)
            pe.wait_ge(row_set, 1)
            for t in range(TT):
                if t + 2 < TT:
                    project(t + 2)
                turn(t)
                if t >= 1:
                    logits(t - 1)
            logits(TT - 1)

        @block.scalar
        def _(act):
            for t in range(TT):
                act.wait_ge(x2_set, t + 1)
                nc.scalar.activation(square[:], m.x2[:, t, :], ACT.Square, accum_out=ss[:, t, 0:1]).then_inc(squared, 1)
                act.wait_ge(squared, t + 1)
                nc.scalar.activation(ss[:, t, 1:2], ss[:, t, 0:1], ACT.Sqrt, bias=m.col[:, 3:4], scale=1.0 / D)\
                  .then_inc(rooted, 1)
                for q in range(2):
                    act.wait_ge(turned, 2 * t + q + 1)
                    if t >= 2:
                        act.wait_ge(logit_done, t - 1)
                    nc.scalar.activation(h2T[:, t % 2, q * HALF:(q + 1) * HALF], ps[:, 4 + q, :], ACT.Copy)\
                      .then_inc(turned_out, 1)

        @block.vector
        def _(dve):
            nc.vector.memset(one_row[:], 1.0).then_inc(row_set, 1)
            dve.wait_ge(small_in, 48)

            def residual(t):
                dve.wait_ge(x_in[t], 16)
                dve.wait_ge(summed, t + 1)
                b = 2 * (t % 2)
                nc.vector.tensor_tensor(m.x2[:, t, :], ps[:, b:b + 2, :].rearrange("p a n -> p (a n)"), m.x2[:, t, :],
                                        ALU.add).then_inc(x2_set, 1)

            residual(0)
            for t in range(TT):
                if t + 1 < TT:
                    residual(t + 1)
                dve.wait_ge(rooted, t + 1)
                nc.vector.reciprocal(ss[:, t, 2:3], ss[:, t, 1:2]).then_inc(inv_set, 1)
                dve.wait_ge(inv_set, t + 1)
                if t >= 2:
                    dve.wait_ge(h2_stored[t % 2], 16 * (t // 2))
                    dve.wait_ge(turned, 2 * (t - 1))
                nc.vector.scalar_tensor_tensor(out=h2[:, t % 2, :], in0=m.x2[:, t, :], scalar=ss[:, t, 2:3],
                                               in1=gffn[:], op0=ALU.mult, op1=ALU.mult).then_inc(h2_set, 1)
                if t >= 1:
                    dve.wait_ge(logit_done, t)
                    nc.vector.tensor_copy(m.logits[:, t - 1, :], ps[:, 6 + (t - 1) % 2, 0:N_LOG]).then_inc(logit_out, 1)
            dve.wait_ge(logit_done, TT)
            nc.vector.tensor_copy(m.logits[:, TT - 1, :], ps[:, 6 + (TT - 1) % 2, 0:N_LOG]).then_inc(logit_out, 1)
            dve.wait_ge(logit_out, TT)


def stage_route(nc, g, m):
    with ExitStack() as ctx:
        sb, psum, sem = allocators(nc, ctx)
        ps = psum("ps_route", [P, 4, HALF])
        iota = sb("iota_t", [P, P])
        down = sb("down", [P, PER_GRP])
        before = sb("before", [P, P])
        ones = sb("ones_t", [P, P])
        tokid = sb("tokid", [P, TT])
        first_slot = sb("first_slot", [P, N_EXP])
        more = sb("more", [P, N_EXP, TT - 1])
        red = sb("red", [P, 8, TT])
        eq = sb("eq", [P, TT, PER_GRP])
        oh_g = sb("oh_g", [P, TT, N_GRP])
        oh = sb("oh", [P, 2, TT, PER_GRP])
        picked = sb("picked", [P, TT, N_GRP, PER_GRP])
        in_grp = sb("in_grp", [P, 2, TT, PER_GRP])
        grp_e = sb("grp_e", [P, TT, N_GRP])
        asg = sb("asg", [P, 3, TT, N_EXP])
        total = sb("total", [P, TT, N_EXP])
        base = sb("base", [P, TT + 1, N_EXP])
        slot = sb("slot", [P, TT, N_EXP])
        late = sb("late", [P, TT, N_EXP])
        nblk = sb("nblk", [P, 3, N_EXP])
        cmp_m = sb("cmp_m", [P, N_EXP, TT - 1])
        cmp_b = sb("cmp_b", [P, OVER, N_EXP])
        own = sb("own", [P, OVER])
        slot_f = sb("slot_f", [P, 2, TT])
        slot_i = sb("slot_i", [P, 3, 2, TT], I32)
        hilo = sb("hilo", [P, 2, 2, TT])
        oh_lo = sb("oh_lo", [P, 2, P])
        oh_hi = sb("oh_hi", [P, 2, N_BLK])
        const_in, vstep, shifted, exped, gap_set, exp2, asg_set, counted, oh_set, oh_used, ids_done = (
            sem(n) for n in ("const_in_u", "vstep_u", "shifted", "exped", "gap_set", "exp2", "asg_set", "counted",
                             "oh_set", "oh_used", "ids_done"))
        N_CONST = 7
        block = ctx.enter_context(nc.Block())

        @block.sync
        def _(sy):
            for dst, src in ((iota[:], g.iota), (down[:], g.down), (before[:], g.before), (ones[:], g.ones),
                             (tokid[:], g.tokid), (first_slot[:], g.first_slot), (more[:], g.more)):
                sy.dma_start(dst, src).then_inc(const_in, 16)

        @block.scalar
        def _(act):
            act.wait_ge(shifted, 1)
            nc.scalar.activation(grp_e[:], grp_e[:], ACT.Exp).then_inc(exped, 1)
            act.wait_ge(gap_set, 1)
            nc.scalar.activation(red[:, 5, :], red[:, 4, :], ACT.Exp).then_inc(exp2, 1)

        @block.tensor
        def _(pe):
            pe.wait_ge(const_in, 16 * N_CONST)
            pe.wait_ge(asg_set, 1)
            both = asg[:, 2, :, :]
            nc.tensor.matmul(ps[:, 0, 0:TT * N_EXP], before[:], both, start=True, stop=True)
            nc.tensor.matmul(ps[:, 1, 0:TT * N_EXP], ones[:], both, start=True, stop=True).then_inc(counted, 1)
            for n in range(2 * TT):
                pe.wait_ge(oh_set, n + 1)
                nc.tensor.matmul(ps[:, 2, 0:N_BLK], oh_lo[:, n % 2, :], oh_hi[:, n % 2, :], start=(n == 0),
                                 stop=(n == 2 * TT - 1)).then_inc(oh_used, 1)

        @block.vector
        def _(dve):
            step = Steps(dve, vstep)
            v = nc.vector
            dve.wait_ge(const_in, 16 * N_CONST)

            def across(ap, n):
                return ap.rearrange("p (t a) -> p t a", a=1).broadcast_to([P, TT, n])

            def along(ap, n):
                return ap.rearrange("p (a n) -> p a n", a=1).broadcast_to([P, TT, n])

            def first_max(values, n, mx, tmp, out):
                step(v.tensor_reduce(mx, values, AXX, ALU.max))
                step(v.tensor_tensor(tmp, values, across(mx, n), ALU.is_equal))
                step(v.tensor_tensor(tmp, tmp, along(down[:, PER_GRP - n:], n), ALU.mult))
                step(v.tensor_reduce(red[:, 7, :], tmp, AXX, ALU.min))
                step(v.tensor_tensor(out, along(down[:, PER_GRP - n:], n), across(red[:, 7, :], n), ALU.is_equal))

            grp = m.logits[:, :, 0:N_GRP]
            exp_l = m.logits[:, :, N_GRP:N_LOG].rearrange("p t (g e) -> p t g e", g=N_GRP)
            first_max(grp, N_GRP, red[:, 0, :], eq[:, :, 0:N_GRP], oh_g[:])
            v.tensor_tensor(grp_e[:], grp, across(red[:, 0, :], N_GRP), ALU.subtract).then_inc(shifted, 1)
            by_g = oh_g[:].rearrange("p t (g a) -> p t g a", a=1).broadcast_to([P, TT, N_GRP, PER_GRP])
            step(v.tensor_tensor(picked[:], exp_l, by_g, ALU.mult))
            step(v.tensor_reduce(in_grp[:, 0, :, :], picked[:].rearrange("p t g e -> p t e g"), AXX, ALU.add))
            first_max(in_grp[:, 0, :, :], PER_GRP, red[:, 1, :], eq[:], oh[:, 0, :, :])
            step(v.scalar_tensor_tensor(out=in_grp[:, 1, :, :], in0=oh[:, 0, :, :], scalar=NEG, in1=in_grp[:, 0, :, :],
                                        op0=ALU.mult, op1=ALU.add))
            first_max(in_grp[:, 1, :, :], PER_GRP, red[:, 2, :], eq[:], oh[:, 1, :, :])
            v.tensor_tensor(red[:, 4, :], red[:, 2, :], red[:, 1, :], ALU.subtract).then_inc(gap_set, 1)
            dve.wait_ge(exped, 1)
            step(v.tensor_reduce(red[:, 3, :], grp_e[:], AXX, ALU.add))
            dve.wait_ge(exp2, 1)
            step(v.scalar_tensor_tensor(out=red[:, 6, :], in0=red[:, 5, :], scalar=1.0, in1=red[:, 3, :], op0=ALU.add,
                                        op1=ALU.mult))
            step(v.reciprocal(m.gate[:, 0, :], red[:, 6, :]))
            v.tensor_tensor(m.gate[:, 1, :], m.gate[:, 0, :], red[:, 5, :], ALU.mult)
            for a in range(2):
                by_e = oh[:, a, :, :].rearrange("p t (b e) -> p t b e", b=1).broadcast_to([P, TT, N_GRP, PER_GRP])
                ins = v.tensor_tensor(asg[:, a, :, :].rearrange("p t (g e) -> p t g e", g=N_GRP), by_g, by_e, ALU.mult)
            step(ins)
            v.tensor_tensor(asg[:, 2, :, :], asg[:, 0, :, :], asg[:, 1, :, :], ALU.add).then_inc(asg_set, 1)
            dve.wait_ge(counted, 1)
            v.memset(base[:, 0, :], 0.0)
            step(v.tensor_copy(total[:], ps[:, 1, 0:TT * N_EXP].rearrange("p (t e) -> p t e", t=TT)))
            for t in range(TT):
                step(v.tensor_tensor(base[:, t + 1, :], base[:, t, :], total[:, t, :], ALU.add))
            step(v.tensor_tensor(slot[:], ps[:, 0, 0:TT * N_EXP].rearrange("p (t e) -> p t e", t=TT), base[:, 0:TT, :],
                                 ALU.add))
            count = base[:, TT, :].rearrange("p (e a) -> p e a", a=1).broadcast_to([P, N_EXP, TT - 1])
            step(v.tensor_tensor(cmp_m[:], count, more[:], ALU.is_gt))
            step(v.tensor_reduce(nblk[:, 0, :], cmp_m[:], AXX, ALU.add))
            step(v.tensor_tensor_scan(nblk[:, 1, :], ones[:, 0:N_EXP], nblk[:, 0, :], 0.0, ALU.mult, ALU.add))
            step(v.tensor_tensor(nblk[:, 2, :], nblk[:, 1, :], nblk[:, 0, :], ALU.subtract))
            step(v.tensor_scalar(nblk[:, 2, :], nblk[:, 2, :], float(P), float((N_EXP - 1) * P), ALU.mult, ALU.add))
            step(v.tensor_tensor(nblk[:, 2, :], nblk[:, 2, :], first_slot[:], ALU.subtract))
            step(v.scalar_tensor_tensor(out=late[:], in0=slot[:], scalar=float(P), in1=along(nblk[:, 2, :], N_EXP),
                                        op0=ALU.is_ge, op1=ALU.mult))
            step(v.tensor_tensor(slot[:], slot[:], late[:], ALU.add))
            step(v.tensor_tensor(slot[:], slot[:], along(first_slot[:], N_EXP), ALU.add))
            for a in range(2):
                step(v.tensor_tensor(late[:], asg[:, a, :, :], slot[:], ALU.mult))
                step(v.tensor_reduce(slot_f[:, a, :], late[:], AXX, ALU.add))
            v.tensor_copy(m.slots[:], slot_f[:])
            step(v.tensor_copy(slot_i[:, 0, :, :], slot_f[:]))
            v.tensor_scalar(slot_i[:, 1, :, :], slot_i[:, 0, :, :], 7, None, ALU.arith_shift_right)
            step(v.tensor_scalar(slot_i[:, 2, :, :], slot_i[:, 0, :, :], P - 1, None, ALU.bitwise_and))
            step(v.tensor_copy(hilo[:], slot_i[:, 1:3, :, :]))
            for a in range(2):
                for t in range(TT):
                    n = a * TT + t
                    if n >= 2:
                        dve.wait_ge(oh_used, n - 1)
                    v.tensor_scalar(oh_hi[:, n % 2, :], iota[:, 0:N_BLK], hilo[:, 0, a, t:t + 1], tokid[:, t:t + 1],
                                    ALU.is_equal, ALU.mult)
                    v.tensor_scalar(oh_lo[:, n % 2, :], iota[:], hilo[:, 1, a, t:t + 1], None, ALU.is_equal)\
                     .then_inc(oh_set, 1)
            upto = nblk[:, 1, :].rearrange("p (a e) -> p a e", a=1).broadcast_to([P, OVER, N_EXP])
            which = iota[:, 0:OVER].rearrange("p (b a) -> p b a", a=1).broadcast_to([P, OVER, N_EXP])
            step(v.tensor_tensor(cmp_b[:], upto, which, ALU.is_le))
            step(v.tensor_reduce(own[:], cmp_b[:], AXX, ALU.add))
            step(v.tensor_scalar(own[:], own[:], float(N_EXP - 1), None, ALU.min))
            v.tensor_copy(m.over[:, 0:OVER], own[:])
            step(v.tensor_copy(m.over[:, OVER:OVER + 1], nblk[:, 1, N_EXP - 1:N_EXP]))
            dve.wait_ge(oh_used, 2 * TT)
            step(v.tensor_copy(m.ids[:], ps[:, 2, 0:N_BLK]))


def stage_experts(nc, g, m):
    with ExitStack() as ctx:
        sb, psum, sem = allocators(nc, ctx)
        ps = psum("ps_exp", [P, 8, HALF])
        w13 = [sb(f"w13_{s}", [P, KT, 2 * D_EXP]) for s in range(2)]
        w2 = [sb(f"w2_{s}", [P, 2, D]) for s in range(2)]
        idx = [sb(f"idx{s}", [P, 1], U32) for s in range(2)]
        rows = [sb(f"rows{s}", [P, D]) for s in range(2)]
        xT = [sb(f"xT{s}", [P, KT, P]) for s in range(2)]
        sil = [sb(f"sil{s}", [P, 2 * P]) for s in range(2)]
        hid = [sb(f"hid_e{s}", [P, 2 * P]) for s in range(2)]
        y = [sb(f"y{s}", [P, D]) for s in range(2)]

        def signals(tag):
            return {w: [sem(f"{w}_{tag}{s}") for s in range(2)] for w in
                    ("w_in", "idx_set", "rows_in", "turned", "xT_a", "xT_v", "up_done", "sil_out", "hid_out", "y_done",
                     "y_a", "y_v", "stored")}

        main, more = signals("first"), signals("more")
        over_free = sem("over_free")
        gather_open = sem("gather_open")
        block = ctx.enter_context(nc.Block())
        EXP_TURNS = N_EXP // 2

        def load_w(sy, q, s, k, e, dynamic_free=True):
            if dynamic_free:
                sy.wait_ge(q["y_done"][s], k)
            sy.dma_start(w13[s][:], flat(g.w13[bass.ds(e, 1), :, :, :].rearrange("e p k n -> p e (k n)"))
                         .rearrange("p (k n) -> p k n", k=KT)).then_inc(q["w_in"][s], 16)
            sy.dma_start(w2[s][:], flat(g.w2[bass.ds(e, 1), :, :, :].rearrange("e p k n -> p e (k n)"))
                         .rearrange("p (k n) -> p k n", k=2)).then_inc(q["w_in"][s], 16)

        def gather(pool, q, s, k, b, free=True):
            if free:
                pool.wait_ge(q["turned"][s], k)
            nc.gpsimd.tensor_copy(idx[s][:], m.ids[:, bass.ds(b, 1)]).then_inc(q["idx_set"][s], 1)
            pool.wait_ge(q["idx_set"][s], k + 1)
            nc.gpsimd.sem_inc(gather_open, 1)
            nc.gpsimd.indirect_dma_start(out=rows[s][:], out_offset=None, in_=g.h2,
                                         in_offset=bass.IndirectOffsetOnAxis(ap=idx[s][:], axis=0))\
              .then_inc(q["rows_in"][s], 16)

        def turn(pe, q, s, k, free):
            free()
            pe.wait_ge(q["rows_in"][s], 16 * k + 16)
            for c in range(KT):
                ins = nc.tensor.transpose(ps[:, c // 4, (c % 4) * P:(c % 4 + 1) * P], rows[s][:, c * P:(c + 1) * P],
                                          m.ident[:])
            ins.then_inc(q["turned"][s], 1)

        def up(pe, q, s, k):
            pe.wait_ge(q["xT_a"][s], k + 1)
            pe.wait_ge(q["xT_v"][s], k + 1)
            pe.wait_ge(q["w_in"][s], 32 * k + 32)
            for f in range(4):
                for c in range(KT):
                    ins = nc.tensor.matmul(ps[:, 2 + s, f * P:(f + 1) * P], w13[s][:, c, f * P:(f + 1) * P],
                                           xT[s][:, c, :], start=(c == 0), stop=(c == KT - 1))
            ins.then_inc(q["up_done"][s], 1)

        def downward(pe, q, s, k):
            pe.wait_ge(q["hid_out"][s], k + 1)
            for h in range(2):
                for f in range(2):
                    ins = nc.tensor.matmul(ps[:, 4 + 2 * s + h, :], hid[s][:, f * P:(f + 1) * P],
                                           w2[s][:, f, h * HALF:(h + 1) * HALF], start=(f == 0), stop=(f == 1))
            ins.then_inc(q["y_done"][s], 1)

        def act_turned(act, q, s, k):
            act.wait_ge(q["turned"][s], k + 1)
            nc.scalar.activation(xT[s][:, 0:4, :], ps[:, 0, :], ACT.Copy).then_inc(q["xT_a"][s], 1)

        def act_silu(act, q, s, k):
            act.wait_ge(q["up_done"][s], k + 1)
            nc.scalar.activation(sil[s][:], ps[:, 2 + s, 0:2 * P], ACT.Silu).then_inc(q["sil_out"][s], 1)

        def act_y(act, q, s, k, b, first=False):
            if not first:
                act.wait_ge(q["stored"][s], 16 * k)
            act.wait_ge(q["y_done"][s], k + 1)
            nc.scalar.activation(y[s][:, 0:HALF], ps[:, 4 + 2 * s, :], ACT.Copy).then_inc(q["y_a"][s], 1)
            act.wait_ge(q["y_a"][s], k + 1)
            act.wait_ge(q["y_v"][s], k + 1)
            act.dma_start(g.y[bass.ds(b * P, P), :], y[s][:]).then_inc(q["stored"][s], 16)

        def vec_turned(dve, q, s, k):
            dve.wait_ge(q["turned"][s], k + 1)
            nc.vector.tensor_copy(xT[s][:, 4:8, :], ps[:, 1, :]).then_inc(q["xT_v"][s], 1)

        def vec_hid(dve, q, s, k):
            dve.wait_ge(q["sil_out"][s], k + 1)
            nc.vector.tensor_tensor(hid[s][:], ps[:, 2 + s, 2 * P:4 * P], sil[s][:], ALU.mult)\
              .then_inc(q["hid_out"][s], 1)

        def vec_y(dve, q, s, k, first=False):
            if not first:
                dve.wait_ge(q["stored"][s], 16 * k)
            dve.wait_ge(q["y_done"][s], k + 1)
            nc.vector.tensor_copy(y[s][:, HALF:D], ps[:, 5 + 2 * s, :]).then_inc(q["y_v"][s], 1)

        @block.sync
        def _(sy):
            for s in range(2):
                load_w(sy, main, s, 0, s, False)
            with nc.sync.Fori(1, EXP_TURNS) as i:
                for s in range(2):
                    load_w(sy, main, s, i, 2 * i + s)
            sy.wait_ge(main["y_done"][0], EXP_TURNS)
            n_over = sy.value_load(m.over[0:1, OVER:OVER + 1], min_val=0, max_val=OVER)
            with nc.sync.Fori(0, OVER) as b:
                with nc.sync.If(b < n_over):
                    e = sy.value_load(m.over[0:1, bass.ds(b, 1)], min_val=0, max_val=N_EXP - 1)
                    sy.wait_ge(over_free, b + 1)
                    load_w(sy, more, 0, b, e, False)

        @block.gpsimd
        def _(pool):
            for s in range(2):
                gather(pool, main, s, 0, s, False)
            with nc.gpsimd.Fori(1, EXP_TURNS) as i:
                for s in range(2):
                    gather(pool, main, s, i, 2 * i + s)
            pool.wait_ge(main["turned"][0], EXP_TURNS)
            n_over = pool.value_load(m.over[0:1, OVER:OVER + 1], min_val=0, max_val=OVER)
            with nc.gpsimd.Fori(0, OVER) as b:
                with nc.gpsimd.If(b < n_over):
                    pool.wait_ge(over_free, b + 1)
                    gather(pool, more, 0, b, b + N_EXP, False)

        @block.tensor
        def _(pe):
            def copied(s, k):
                def wait():
                    pe.wait_ge(main["xT_a"][s], k)
                    pe.wait_ge(main["xT_v"][s], k)
                return wait

            turn(pe, main, 0, 0, lambda: None)
            with nc.tensor.Fori(0, EXP_TURNS - 1) as i:
                up(pe, main, 0, i)
                turn(pe, main, 1, i, copied(0, i + 1))
                downward(pe, main, 0, i)
                up(pe, main, 1, i)
                turn(pe, main, 0, i + 1, copied(1, i + 1))
                downward(pe, main, 1, i)
            k = EXP_TURNS - 1
            up(pe, main, 0, k)
            turn(pe, main, 1, k, copied(0, k + 1))
            downward(pe, main, 0, k)
            up(pe, main, 1, k)
            downward(pe, main, 1, k)
            n_over = pe.value_load(m.over[0:1, OVER:OVER + 1], min_val=0, max_val=OVER)
            with nc.tensor.Fori(0, OVER) as b:
                with nc.tensor.If(b < n_over):
                    pe.wait_ge(over_free, b + 1)
                    turn(pe, more, 0, b, lambda: None)
                    up(pe, more, 0, b)
                    downward(pe, more, 0, b)

        @block.scalar
        def _(act):
            act_turned(act, main, 0, 0)

            def pair(i, first=False, last=False):
                act_silu(act, main, 0, i)
                act_turned(act, main, 1, i)
                act_y(act, main, 0, i, 2 * i, first)
                act_silu(act, main, 1, i)
                if not last:
                    act_turned(act, main, 0, i + 1)
                act_y(act, main, 1, i, 2 * i + 1, first)

            pair(0, first=True)
            with nc.scalar.Fori(1, EXP_TURNS - 1) as i:
                pair(i)
            pair(EXP_TURNS - 1, last=True)
            for s in range(2):
                act.wait_ge(main["stored"][s], 16 * EXP_TURNS)
            nc.scalar.sem_inc(over_free, 1)
            n_over = act.value_load(m.over[0:1, OVER:OVER + 1], min_val=0, max_val=OVER)
            with nc.scalar.Fori(0, OVER) as b:
                with nc.scalar.If(b < n_over):
                    act_turned(act, more, 0, b)
                    act_silu(act, more, 0, b)
                    act_y(act, more, 0, b, b + N_EXP, True)
                    act.wait_ge(more["stored"][0], 16 * b + 16)
                    nc.scalar.sem_inc(over_free, 1)

        @block.vector
        def _(dve):
            vec_turned(dve, main, 0, 0)

            def pair(i, first=False, last=False):
                vec_hid(dve, main, 0, i)
                vec_turned(dve, main, 1, i)
                vec_y(dve, main, 0, i, first)
                vec_hid(dve, main, 1, i)
                if not last:
                    vec_turned(dve, main, 0, i + 1)
                vec_y(dve, main, 1, i, first)

            pair(0, first=True)
            with nc.vector.Fori(1, EXP_TURNS - 1) as i:
                pair(i)
            pair(EXP_TURNS - 1, last=True)
            n_over = dve.value_load(m.over[0:1, OVER:OVER + 1], min_val=0, max_val=OVER)
            with nc.vector.Fori(0, OVER) as b:
                with nc.vector.If(b < n_over):
                    dve.wait_ge(over_free, b + 1)
                    vec_turned(dve, more, 0, b)
                    vec_hid(dve, more, 0, b)
                    vec_y(dve, more, 0, b, True)


def stage_combine(nc, g, m):
    with ExitStack() as ctx:
        sb, psum, sem = allocators(nc, ctx)
        BUF = 4
        gfin = sb("gfin", [P, D])
        ya = sb("ya", [P, BUF, 2, D])
        square = sb("square_c", [P, D])
        ss = sb("ss_c", [P, TT, 3])
        res = sb("res", [P, 2, D])
        g_in = sem("g_in_c")
        y_in = [sem(f"y_in{s}") for s in range(BUF)]
        part, x3_set, squared, rooted, inv_set, res_set = (sem(n) for n in ("part_c", "x3_set", "squared_c", "rooted_c",
                                                                            "inv_set_c", "res_set"))
        stored = [sem(f"stored_c{s}") for s in range(2)]
        block = ctx.enter_context(nc.Block())

        @block.gpsimd
        def _(pool):
            for t in range(TT):
                if t >= BUF:
                    pool.wait_ge(x3_set, t - BUF + 1)
                for a in range(2):
                    nc.gpsimd.indirect_dma_start(out=ya[:, t % BUF, a, :], out_offset=None, in_=g.y,
                                                 in_offset=bass.IndirectOffsetOnAxis(ap=m.slots[:, a, t:t + 1], axis=0))\
                      .then_inc(y_in[t % BUF], 16)

        @block.sync
        def _(sy):
            sy.dma_start(gfin[:], g.gfin).then_inc(g_in, 16)
            for t in range(TT):
                sy.wait_ge(res_set, t + 1)
                sy.dma_start(g.out[t * P:(t + 1) * P, :], res[:, t % 2, :]).then_inc(stored[t % 2], 16)
            for s in range(2):
                sy.wait_ge(stored[s], 16 * TT // 2)

        @block.scalar
        def _(act):
            for t in range(TT):
                act.wait_ge(x3_set, t + 1)
                nc.scalar.activation(square[:], m.x2[:, t, :], ACT.Square, accum_out=ss[:, t, 0:1]).then_inc(squared, 1)
                act.wait_ge(squared, t + 1)
                nc.scalar.activation(ss[:, t, 1:2], ss[:, t, 0:1], ACT.Sqrt, bias=m.col[:, 3:4], scale=1.0 / D)\
                  .then_inc(rooted, 1)

        @block.vector
        def _(dve):
            dve.wait_ge(g_in, 16)

            def add(t):
                dve.wait_ge(y_in[t % BUF], 32 * (t // BUF + 1))
                nc.vector.scalar_tensor_tensor(out=m.x2[:, t, :], in0=ya[:, t % BUF, 0, :], scalar=m.gate[:, 0, t:t + 1],
                                               in1=m.x2[:, t, :], op0=ALU.mult, op1=ALU.add).then_inc(part, 1)
                dve.wait_ge(part, t + 1)
                nc.vector.scalar_tensor_tensor(out=m.x2[:, t, :], in0=ya[:, t % BUF, 1, :], scalar=m.gate[:, 1, t:t + 1],
                                               in1=m.x2[:, t, :], op0=ALU.mult, op1=ALU.add).then_inc(x3_set, 1)

            add(0)
            for t in range(TT):
                if t + 1 < TT:
                    add(t + 1)
                dve.wait_ge(rooted, t + 1)
                nc.vector.reciprocal(ss[:, t, 2:3], ss[:, t, 1:2]).then_inc(inv_set, 1)
                dve.wait_ge(inv_set, t + 1)
                if t >= 2:
                    dve.wait_ge(stored[t % 2], 16 * (t // 2))
                nc.vector.scalar_tensor_tensor(out=res[:, t % 2, :], in0=m.x2[:, t, :], scalar=ss[:, t, 2:3],
                                               in1=gfin[:], op0=ALU.mult, op1=ALU.mult).then_inc(res_set, 1)


def program(nc, g):
    m = Names()
    with ExitStack() as whole:
        def sb(ctx, name, shape, dt=F32, side=None):
            return ctx.enter_context(nc.sbuf_tensor(name, shape, dt, side=side))

        m.ident = sb(whole, "ident", [P, P])
        m.col = sb(whole, "col", [P, 8])
        m.logits = sb(whole, "logits", [P, TT, N_LOG])
        m.gate = sb(whole, "gate", [P, 2, TT])
        m.slots = sb(whole, "slots", [P, 2, TT], U32)
        m.ids = sb(whole, "ids", [P, N_BLK], U32)
        m.over = sb(whole, "over", [P, OVER + 1], I32)
        with ExitStack() as late:
            with ExitStack() as mixers:
                m.hT = sb(mixers, "hT", [P, KT, S])
                m.bmT = sb(mixers, "bmT", [P, PAIRS, S])
                with ExitStack() as ctx:
                    m.lo = sb(ctx, "lo", [P, 2, S])
                    stage_normalise(nc, g, m)
                    stage_recur(nc, g, m)
                m.oAT = sb(mixers, "oAT", [P, PAIRS, S])
                with ExitStack() as ctx:
                    m.qkv = sb(ctx, "qkv", [P, N_QKV, S])
                    m.vtok = sb(ctx, "vtok", [P, TT, 2 * P])
                    m.gates = sb(ctx, "gates", [P, TT, 24])
                    m.kcmp = sb(ctx, "kcmp", [P, N_CMP])
                    m.vcmp = sb(ctx, "vcmp", [HD, 2, HD])
                    stage_project(nc, g, m)
                    stage_attend(nc, g, m)
                m.mT = sb(late, "mT", [P, KT, S], side="right")
                stage_merge(nc, g, m)
            m.x2 = sb(whole, "x2", [P, TT, D])
            stage_output(nc, g, m)
        stage_route(nc, g, m)
        stage_experts(nc, g, m)
        stage_combine(nc, g, m)


def tile_columns():
    q, kc, vc, ksl, vsl, kwn, vwn, gat = 0, 512, 640, 768, 896, 1024, 1152, 1280
    r = 1304
    k, v, xw, xg, ga, gb = r + 512, r + 1024, r + 1536, r + 1664, r + 1792, r + 2816
    run = lambda a, n: list(range(a, a + n))
    tiles = [run(xw, P), run(xg, P)]
    for hp in range(PAIRS):
        tiles += [run(base + hp * P, P) for base in (r, k, v)]
    tiles += [run(kc, P), run(ksl, P), run(kwn, P)]
    tiles += [run(q + i * HD, HD) + run(q + (PAIRS + i) * HD, HD) for i in range(PAIRS)]
    tiles += [run(vc, P)]
    for f in range(KT):
        tiles += [run(ga + f * P, P), run(gb + f * P, P)]
    return tiles, run(vsl, P) + run(vwn, P) + run(gat, 24)


def constants():
    c = {}
    p = np.arange(P)
    c["ident"] = np.eye(P)
    col = np.zeros((P, 8))
    col[:, 0] = 10000.0 ** (-(p % 32) / 32.0)
    col[:, 1] = np.where(p % HD < 32, -1.0, 1.0)
    col[:, 2] = np.pi / 2
    col[:, 3] = RMS_EPS
    col[:, 4] = GN_EPS
    col[:, 5] = p >= 31
    col[:, 6] = p
    c["col"] = col
    s, t = p[:, None], p[None, :]
    c["ones"] = np.ones((P, P))
    c["mask4"] = np.concatenate([s < t, s <= t, s < t, s <= t], 1)
    c["lvl"] = np.stack([(s >> (b + 1) == t >> (b + 1)) & (s >> b & 1 == 0) & (t >> b & 1 == 1)
                         for b in range(7)], 1)
    c["heads1"] = s // HD == t // HD
    c["eye2"] = s % HD == np.arange(HD)[None, :]
    causal = np.where(t <= s, 0.0, NEG)
    c["bias"] = np.stack([np.where(t > s, 0.0, NEG), causal], 1)
    q = (np.arange(TT)[None, :, None] * P + p[:, None, None])
    c["bias_cmp"] = np.where(np.arange(N_CMP)[None, None, :] * 16 + 31 <= q, 0.0, NEG)
    c["down"] = np.broadcast_to(np.arange(-PER_GRP, 0), (P, PER_GRP))
    c["before"] = s < t
    c["iota"] = np.broadcast_to(np.arange(P), (P, P))
    c["tokid"] = np.arange(TT)[None, :] * P + p[:, None]
    c["first_slot"] = np.broadcast_to(np.arange(N_EXP) * P, (P, N_EXP))
    c["more"] = np.broadcast_to(np.arange(1, TT) * P, (P, N_EXP, TT - 1))
    return {k: np.ascontiguousarray(v.astype(np.float32)) for k, v in c.items()}


def layout(inp):
    a = {k: np.asarray(v) for k, v in inp.items()}
    cat, asc = np.concatenate, np.ascontiguousarray
    by_tile = lambda w: w.reshape(-1, P, w.shape[-1]).transpose(1, 0, 2)
    d = {}
    x, w_in = a["x"][0], a["w_in"][0]
    d["x"] = x
    d["xT"] = by_tile(asc(x.T))
    d["xT"] = d["xT"].reshape(P, KT * S)
    tiles, tokw = tile_columns()
    d["w_tiles"] = np.stack([by_tile(w_in[:, cols]).reshape(P, KT * P) for cols in tiles], 1)
    d["w_tok"] = by_tile(w_in[:, tokw])
    d["gmix"] = a["g_mix"][0].reshape(KT, P).T
    mu = a["rwkv_mu"][0]
    d["mu_lo"] = np.stack([mu[1536:1536 + P], mu[1536 + P:1536 + 2 * P]], 1)
    d["pos"] = np.broadcast_to(a["positions"][0], (P, S))
    pair = lambda v: v.reshape(PAIRS, P)
    vecs = [pair(mu[0:512]), pair(mu[512:1024]), pair(mu[1024:1536]), pair(a["rwkv_w0"][0]), pair(a["rwkv_a0"][0]),
            pair(a["rwkv_k_k"][0]), pair(a["rwkv_k_a"][0]), pair(a["rwkv_r_k"][0].reshape(-1)),
            pair(a["rwkv_ln_w"][0]), pair(a["rwkv_ln_b"][0])]
    d["vecs"] = np.stack(vecs, 2).transpose(1, 0, 2)
    wa = cat([a["rwkv_w2"][0], a["rwkv_a2"][0]], 0).reshape(P, PAIRS, P)
    g2 = a["rwkv_g2"][0].reshape(P, PAIRS, P)
    d["lora"] = np.stack([wa, g2], 2).reshape(P, PAIRS * 2, P)
    half_rows = lambda v: v.reshape(-1, P).T
    d["cmp_pe"] = np.stack([half_rows(a["cmp_pe_" + kv][0].reshape(-1)) for kv in "kv"], 1)
    d["cmp_w1"] = np.stack([by_tile(a["cmp_w1_" + kv][0]) for kv in "kv"])
    d["cmp_w2"] = np.stack([by_tile(a["cmp_w2_" + kv][0]) for kv in "kv"], 1)
    d["cmp_b1"] = np.stack([half_rows(a["cmp_b1_" + kv][0]) for kv in "kv"], 1)
    w_a = a["w_proj_a"][0].reshape(2, PAIRS, HD, D).transpose(1, 0, 2, 3).reshape(-1, D)
    w_ab = np.stack([by_tile(w_a), by_tile(a["w_proj_b"][0])], 1)
    d["w_ab"] = w_ab.reshape(P, 8, KT, P).transpose(0, 2, 1, 3).reshape(P, 8 * KT, P)
    d["w_out"] = by_tile(a["w_out"][0])
    d["gffn"] = np.broadcast_to(a["g_ffn"][0], (P, D))
    d["gfin"] = np.broadcast_to(a["g_final"], (P, D))
    d["w_rt"] = by_tile(cat([a["w_grp"][0], a["w_exp"][0]], 1))
    d["b_rt"] = cat([a["b_grp"][0], a["b_exp"][0]])[None, :]
    w13 = np.stack([a["e_w1"][0], a["e_w3"][0]], 2)
    d["w13"] = w13.reshape(N_EXP, KT, P, 2 * D_EXP).transpose(0, 2, 1, 3)
    d["w2"] = a["e_w2"][0].reshape(N_EXP, 2, P, D).transpose(0, 2, 1, 3)
    d["cmp_b2k"] = a["cmp_b2_k"][0][:, None]
    d["cmp_b2v"] = a["cmp_b2_v"][0][None, :]
    return {k: asc(v) for k, v in d.items()}


def kernel(**inputs):
    import concourse.bacc as bacc
    from concourse.bass_utils import run_bass_kernel_spmd

    nc = bacc.Bacc("TRN2", target_bir_lowering=False, num_devices=1)
    arrays, g = {}, Names()
    for name, a in {**constants(), **layout(inputs)}.items():
        arrays["in_" + name] = a
        g.__dict__[name] = nc.dram_tensor("in_" + name, a.shape, mybir.dt.from_np(a.dtype), kind="ExternalInput").ap()
    g.out = nc.dram_tensor("out", (S, D), F32, kind="ExternalOutput").ap()
    g.h2 = nc.dram_tensor("h2_rows", (S, D), F32, kind="Internal").ap()
    g.y = nc.dram_tensor("y_rows", (N_BLK * P, D), F32, kind="Internal").ap()
    program(nc, g)
    r = run_bass_kernel_spmd(nc, [arrays], core_ids=[0])
    return r.results[0]["out"].reshape(1, S, D)
```

```python
from contextlib import ExitStack
import math

import numpy as np
import concourse.bass as bass
from concourse import mybir

F32 = mybir.dt.float32
F32R = mybir.dt.float32r
I32 = mybir.dt.int32
U32 = mybir.dt.uint32
ACT = mybir.ActivationFunctionType
ALU = mybir.AluOpType
AXX = mybir.AxisListType.X

P = 128
S = 1024
D = 1024
KT = D // P
TT = S // P
HALF = 512
HD = 64
PAIRS = 4
N_CMP = 63
CMP_HID = 256
N_GRP, N_EXP, PER_GRP = 4, 32, 8
N_LOG = N_GRP + N_EXP
D_EXP = 256
RMS_EPS = 1e-6
GN_EPS = 64e-5
OVER = S * 2 // P - 1
N_BLK = N_EXP + OVER
W_DECAY = -math.exp(-0.5)

T_XWA, T_XG = 0, 1
T_RKV = 2
T_QKV = 14
N_QKV = 8
T_GATE = 22
N_ROPE = 7
TOKW = 2 * P + 24
NEG = -1e30


class Steps:

    def __init__(self, eng, sem):
        self.eng, self.sem, self.base, self.n = eng, sem, 0, 0

    def __call__(self, ins):
        self.n += 1
        ins.then_inc(self.sem, 1)
        self.eng.wait_ge(self.sem, self.base + self.n)

    def enter(self, i, per):
        self.start, self.per = self.base + self.n, per
        self.base, self.n = i * per + self.start, 0

    def leave(self, trips):
        assert self.n == self.per, f"steps per turn: {self.n}"
        self.base, self.n = self.start + trips * self.per, 0


class Names:
    pass


def flat(ap):
    return ap.rearrange("p a n -> p (a n)")


def allocators(nc, ctx):
    sems = []

    def retire():
        nc.clear_and_free_semaphores(sems)
        nc.all_engine_barrier()

    ctx.callback(retire)

    def sb(name, shape, dt=F32):
        return ctx.enter_context(nc.sbuf_tensor(name, shape, dt))

    def psum(name, shape):
        return ctx.enter_context(nc.psum_tensor(name, shape, F32))

    def sem(name):
        sems.append(nc.alloc_semaphore(name))
        return sems[-1]

    return sb, psum, sem


def stage_normalise(nc, g, m):
    with ExitStack() as ctx:
        sb, psum, sem = allocators(nc, ctx)
        ps = psum("ps_norm", [P, 8, HALF])
        ones = sb("ones_n", [P, P])
        square = sb("square", [P, 2, S])
        rstd = sb("rstd_x", [P, S])
        gmix = sb("gmix", [P, KT])
        wlo = sb("wlo", [P, 2, KT * P])
        x_in = [sem(f"x_in{k}") for k in range(KT)]
        small_in, w_in = sem("small_in"), sem("w_in_n")
        ones_set, squared, summed = sem("ones_set"), sem("squared"), sem("summed")
        ln_done, root_done, h_ready = sem("ln_done"), sem("root_done"), sem("h_ready")
        lo_done, lo_out = sem("lo_done"), sem("lo_out")
        zeros = sb("zeros_n", [P, D])
        zeros_set, zeros_out = sem("zeros_set"), sem("zeros_out")
        block = ctx.enter_context(nc.Block())

        @block.sync
        def _(sy):
            for k in range(KT):
                sy.dma_start(m.hT[:, k, :], g.xT[:, k * S:(k + 1) * S]).then_inc(x_in[k], 16)
            for dst, src in ((gmix[:], g.gmix), (m.mu_lo[:], g.mu_lo), (m.ident[:], g.ident), (m.col[:], g.col)):
                sy.dma_start(dst, src).then_inc(small_in, 16)
            for t in range(2):
                sy.dma_start(wlo[:, t, :], g.w_tiles[:, T_XWA + t, :]).then_inc(w_in, 16)
            load_pair(sy, g, m, 0)
            sy.wait_ge(zeros_set, 1)
            with nc.sync.Fori(0, OVER) as b:
                sy.dma_start(g.y[bass.ds(b * P + N_EXP * P, P), :], zeros[:]).then_inc(zeros_out, 16)
            sy.wait_ge(zeros_out, 16 * OVER)

        @block.tensor
        def _(pe):
            pe.wait_ge(ones_set, 1)
            for k in range(KT):
                pe.wait_ge(squared, k + 1)
                for h in range(2):
                    ins = nc.tensor.matmul(ps[:, 4 + h, :], ones[:], square[:, k % 2, h * HALF:(h + 1) * HALF],
                                           start=(k == 0), stop=(k == KT - 1))
                ins.then_inc(summed, 1)
            pe.wait_ge(w_in, 32)
            for t in range(2):
                for h in range(2):
                    for k in range(KT):
                        pe.wait_ge(h_ready, k + 1)
                        ins = nc.tensor.matmul(ps[:, 2 * t + h, :], wlo[:, t, k * P:(k + 1) * P],
                                               m.hT[:, k, h * HALF:(h + 1) * HALF], start=(k == 0), stop=(k == KT - 1))
                    ins.then_inc(lo_done, 1)

        @block.scalar
        def _(act):
            for k in range(KT):
                act.wait_ge(x_in[k], 16)
                if k >= 2:
                    act.wait_ge(summed, k - 1)
                nc.scalar.activation(square[:, k % 2, :], m.hT[:, k, :], ACT.Square).then_inc(squared, 1)
            act.wait_ge(small_in, 64)
            act.wait_ge(summed, KT)
            for h in range(2):
                nc.scalar.activation(rstd[:, h * HALF:(h + 1) * HALF], ps[:, 4 + h, :], ACT.Ln,
                                     bias=m.col[:, 3:4], scale=1.0 / D).then_inc(ln_done, 1)
            for h in range(2):
                act.wait_ge(ln_done, h + 1)
                nc.scalar.activation(rstd[:, h * HALF:(h + 1) * HALF], rstd[:, h * HALF:(h + 1) * HALF], ACT.Exp,
                                     scale=-0.5).then_inc(root_done, 1)
            for t in range(2):
                for h in range(2):
                    act.wait_ge(lo_done, 2 * t + h + 1)
                    nc.scalar.activation(m.lo[:, t, h * HALF:(h + 1) * HALF], ps[:, 2 * t + h, :], ACT.Copy)\
                      .then_inc(lo_out, 1)
            act.wait_ge(lo_out, 4)

        @block.vector
        def _(dve):
            nc.vector.memset(ones[:], 1.0).then_inc(ones_set, 1)
            nc.vector.memset(zeros[:], 0.0).then_inc(zeros_set, 1)
            dve.wait_ge(small_in, 64)
            dve.wait_ge(root_done, 2)
            for k in range(KT):
                dve.wait_ge(x_in[k], 16)
                nc.vector.scalar_tensor_tensor(out=m.hT[:, k, :], in0=m.hT[:, k, :], scalar=gmix[:, k:k + 1],
                                               in1=rstd[:], op0=ALU.mult, op1=ALU.mult).then_inc(h_ready, 1)
            dve.wait_ge(h_ready, KT)


def load_pair(sy, g, m, hp):
    sy.dma_start(m.wr[:], g.w_tiles[:, bass.ds(hp * 3 + T_RKV, 3), :]).then_inc(m.wr_in, 16)


def token_shift(nc, step, out, raw, tmp, mu, done):
    n = raw.shape[-1]
    nc.vector.tensor_tensor(tmp[:, 1:n], raw[:, 0:n - 1], raw[:, 1:n], ALU.subtract)
    step(nc.vector.tensor_scalar(tmp[:, 0:1], raw[:, 0:1], -1.0, None, ALU.mult))
    nc.vector.scalar_tensor_tensor(out=out, in0=tmp, scalar=mu, in1=raw, op0=ALU.mult, op1=ALU.add).then_inc(done, 1)


LANES = 2
ROUNDS = 2
LEVELS = 7
MID = P // 2 - 1
V_MU_R, V_MU_K, V_MU_V, V_W0, V_A0, V_KK, V_KA, V_RK, V_LNW, V_LNB = range(10)
N_VEC = 10
K_MT, K_RB, K_NT, K_RK = range(4)
TOK_A, TOK_B, TOK_K, TOK_V = range(4)
RECUR_STEPS = 17
LANE_SIGNALS = ("gram", "masked", "tt_set", "off", "t_turned", "t_set", "x_done", "x_out", "tx_done", "xt_done",
                "t_upd", "tt_upd", "nv_done", "nv_out", "wu_done", "wu_out", "gq_done", "gq_out", "rw_done",
                "rw_out", "y_done", "y_out")


def stage_recur(nc, g, m):
    with ExitStack() as ctx:
        sb, psum, sem = allocators(nc, ctx)
        ps = psum("ps_recur", [P, 8, HALF])
        lora = sb("lora", [P, 2, P])
        vecs = sb("vecs", [P, PAIRS, N_VEC])
        vec = sb("vec", [P, N_VEC])
        raw = sb("raw_r", [P, 2, S])
        mix = sb("mix_r", [P, 3, S])
        tmp = sb("tmp_r", [P, 2, S])
        av = sb("av", [P, S])
        sig = sb("sig", [P, S])
        lc = sb("lc", [P, S])
        kk = sb("kk", [P, S])
        bonus = sb("bonus", [P, S])
        yt = raw[:, 0, :]
        ar = sb("ar", [P, 2, TT, 2, P])
        kt = sb("kt_r", [P, S])
        bt = sb("bt_r", [P, S])
        tok = sb("tok_r", [P, TT, 4, P])
        ones = sb("ones_r", [P, P])
        mask4 = sb("mask4", [P, 4 * P])
        lvl = sb("lvl", [P, LEVELS, P])
        heads1 = sb("heads1", [P, P])
        eye2 = sb("eye2", [P, HD])
        dcol = sb("dcol", [P, TT])
        state = sb("state", [P, TT + 1, HD])
        mm = [sb(f"mm{x}", [P, 4, 4, P]) for x in range(LANES)]
        tinv = [sb(f"tinv{x}", [P, 4, P]) for x in range(LANES)]
        tinvT = [sb(f"tinvT{x}", [P, 4, P]) for x in range(LANES)]
        xs = [sb(f"xs{x}", [P, 4, P]) for x in range(LANES)]
        moff = [sb(f"moff{x}", [P, 4, P]) for x in range(LANES)]
        wu = [xs[x][:].rearrange("p u (a n) -> p u a n", a=2) for x in range(LANES)]
        nv = [sb(f"nv{x}", [P, 4, HD]) for x in range(LANES)]
        gm = [sb(f"gm{x}", [P, 2, HD]) for x in range(LANES)]
        qd = [sb(f"qd{x}", [P, 2, HD]) for x in range(LANES)]
        rw = [sb(f"rw{x}", [P, 2, P]) for x in range(LANES)]

        const_in, lora_in = sem("const_in_r"), sem("lora_in")
        x_mixed, x_set, other_zero = sem("x_mixed"), sem("x_set"), sem("other_zero")
        vec_set, raw_done, raw_out, lo_done, lo_out = (sem(n) for n in ("vec_set", "raw_done", "raw_out", "lora_done",
                                                                        "lora_out"))
        mixed, kraw, ksq, kn_sum, kn_max, kn_ln, kn_root = (sem(n) for n in ("mixed", "kraw", "ksq", "kn_sum", "kn_max",
                                                                             "kn_ln", "kn_root"))
        lc_ready, exps, rk_ready, rk_sum, bonus_set = (sem(n) for n in ("lc_ready", "exps", "rk_ready", "rk_sum",
                                                                        "bonus_set"))
        factors, pool_factors, turned, turned_out = (sem(n) for n in ("factors", "pool_factors", "turned", "turned_out"))
        y_mean, y_cent, y_sq, y_var, y_ln, y_root, bm_set = (sem(n) for n in ("y_mean", "y_cent", "y_sq", "y_var", "y_ln",
                                                                              "y_root", "bm_set"))
        g_done = sem("g_done")
        chain_open = sem("chain_open")
        zero_set, state_set, chained, vstep = sem("zero_set"), sem("state_set"), sem("chained"), sem("vstep_r")
        lane = [{what: sem(f"{what}_{x}") for what in LANE_SIGNALS} for x in range(LANES)]
        PRIME_Y, PRIME_LN, PRIME_BM = 1, 2, 1
        block = ctx.enter_context(nc.Block())
        N_CONST = 6

        spare = bt

        def head(j):
            return slice(HD * j, HD * j + HD)

        def units(r, x):
            return [(2 * cc + j, cc, 4 * r + 2 * x + cc, j) for cc in range(2) for j in range(2)]

        def half(h):
            return slice(h * HALF, (h + 1) * HALF)

        @block.sync
        def _(sy):
            def load_lora(hp):
                sy.dma_start(lora[:], g.lora[:, bass.ds(hp * 2, 2), :]).then_inc(lora_in, 16)

            load_lora(0)
            for dst, src in ((vecs[:], g.vecs), (ones[:], g.ones), (mask4[:], g.mask4), (lvl[:], g.lvl),
                             (heads1[:], g.heads1), (eye2[:], g.eye2)):
                sy.dma_start(dst, src).then_inc(const_in, 16)
            with nc.sync.Fori(1, PAIRS) as hp:
                sy.wait_ge(raw_done, 6 * hp)
                load_pair(sy, g, m, hp)
                sy.wait_ge(g_done, 2 * hp)
                load_lora(hp)

        @block.tensor
        def _(pe):
            def project(hp, t, bank, h):
                for k in range(KT):
                    ins = nc.tensor.matmul(ps[:, bank + h, :], m.wr[:, t, k * P:(k + 1) * P], m.hT[:, k, half(h)],
                                           start=(k == 0), stop=(k == KT - 1))
                ins.then_inc(raw_done, 1)

            def front(hp):
                pe.wait_ge(m.wr_in, 16 * hp + 16)
                for h in range(2):
                    project(hp, 1, 0, h)
                pe.wait_ge(lora_in, 16 * hp + 16)
                pe.wait_ge(x_set, 2)
                pe.wait_ge(other_zero, 2)
                pe.wait_ge(const_in, 16 * N_CONST)
                pe.wait_ge(bm_set, hp + PRIME_BM)
                for h in range(2):
                    nc.tensor.matmul(ps[:, 6 + h, :], lora[0:HD, 0, :], m.lo[0:HD, 0, half(h)], start=True, stop=True)\
                      .then_inc(lo_done, 1)
                pe.wait_ge(y_ln, 2 * hp + PRIME_LN)
                for h in range(2):
                    project(hp, 0, 2, h)
                for h in range(2):
                    pe.wait_ge(raw_out, 6 * hp + h + 1)
                    nc.tensor.matmul(ps[:, h, :], lora[HD:P, 0, :], m.lo[HD:P, 0, half(h)], start=True, stop=True)\
                      .then_inc(lo_done, 1)
                pe.wait_ge(lo_out, 4 * hp + 2)
                for h in range(2):
                    pe.wait_ge(ksq, 2 * hp + h + 1)
                    nc.tensor.matmul(ps[:, 6 + h, :], heads1[:], bonus[:, half(h)], start=True, stop=True)\
                      .then_inc(kn_sum, 1)
                for h in range(2):
                    project(hp, 2, 4, h)
                pe.wait_ge(kn_max, 2 * hp + 2)
                pe.wait_ge(rk_ready, hp + 1)
                for h in range(2):
                    nc.tensor.matmul(ps[:, 6 + h, :], heads1[:], tmp[:, 0, half(h)], start=True, stop=True)\
                      .then_inc(rk_sum, 1)
                pe.wait_ge(factors, 2 * hp + 2)
                pe.wait_ge(pool_factors, 3 * hp + 3)
                pe.wait_ge(lo_out, 4 * hp + 4)
                pe.wait_ge(raw_out, 6 * hp + 6)
                for c in range(TT):
                    if c % 4 == 0:
                        pe.wait_ge(mixed, 4 * hp + 3 + c // 4)
                    if c == 6:
                        pe.wait_ge(bonus_set, 2 * hp + 2)
                    col = slice(c * P, (c + 1) * P)
                    for q, src in enumerate((bt[:, col], kt[:, col], mix[:, 2, col])):
                        nc.tensor.transpose(ps[:, c, (q + 1) * P:(q + 2) * P], src, m.ident[:])
                    for j in range(2):
                        ins = nc.tensor.matmul(ps[:, c, HD * j:HD * (j + 1)], ar[:, j, c, 0, :], m.ident[:, head(j)],
                                               start=True, stop=True)
                    ins.then_inc(turned, 1)

            def grams(hp, r, x, n):
                if r == 0:
                    pe.wait_ge(turned_out, 8 * hp + 4 * x + 4)
                else:
                    pe.wait_ge(state_set, 8 * hp + 2 * x + 2)
                pe.wait_ge(lane[x]["y_out"], n + PRIME_Y)
                for u, cc, c, j in units(r, x):
                    col = slice(c * P, (c + 1) * P)
                    nc.tensor.matmul(ps[:, 4 * x + u, 0:2 * P], bt[:, col], ar[:, j, c, :, :],
                                     start=True, stop=True)
                    nc.tensor.matmul(ps[:, 4 * x + u, 2 * P:4 * P], kt[:, col], ar[:, j, c, :, :],
                                     start=True, stop=True).then_inc(lane[x]["gram"], 1)

            def turn_t(hp, r, x, n):
                pe.wait_ge(lane[x]["tt_set"], n + 1)
                for u in range(4):
                    ins = nc.tensor.transpose(ps[:, 4 * x, u * P:(u + 1) * P], tinvT[x][:, u, :], m.ident[:])
                ins.then_inc(lane[x]["t_turned"], 1)

            def level_x(lv, hp, r, x, n):
                s = lane[x]
                pe.wait_ge(s["off"], 6 * n + lv)
                if lv == 1:
                    pe.wait_ge(s["t_set"], n + 1)
                else:
                    pe.wait_ge(s["t_upd"], 5 * n + lv - 1)
                for u in range(4):
                    ins = nc.tensor.matmul(ps[:, 4 * x + 1, u * P:(u + 1) * P], moff[x][:, u, :],
                                           tinv[x][:, u, :], start=True, stop=True)
                ins.then_inc(s["x_done"], 1)
                if lv == 1:
                    for u, cc, c, j in units(r, x):
                        ins = nc.tensor.matmul(ps[:, 4 * x, u * HD:(u + 1) * HD], mm[x][:, u, K_NT, :],
                                               tok[:, c, TOK_V, head(j)], start=True, stop=True)
                    ins.then_inc(s["nv_done"], 1)

            def level_t(lv, hp, r, x, n):
                s = lane[x]
                pe.wait_ge(s["x_out"], 6 * n + lv)
                if lv > 1:
                    pe.wait_ge(s["tt_upd"], 6 * n + lv - 1)
                if lv < LEVELS - 1:
                    for u in range(4):
                        ins = nc.tensor.matmul(ps[:, 4 * x + 2, u * P:(u + 1) * P], tinvT[x][:, u, :], xs[x][:, u, :],
                                               start=True, stop=True)
                    ins.then_inc(s["tx_done"], 1)
                else:
                    for u in range(4):
                        ins = nc.tensor.matmul(ps[:, 4 * x + 3, u * P:(u + 1) * P], xs[x][:, u, :], tinvT[x][:, u, :],
                                               start=True, stop=True)
                    ins.then_inc(s["xt_done"], 1)

            def turn_grown(lv, hp, r, x, n):
                pe.wait_ge(lane[x]["t_upd"], 5 * n + lv)
                for u in range(4):
                    ins = nc.tensor.transpose(ps[:, 4 * x + 3, u * P:(u + 1) * P], tinv[x][:, u, :], m.ident[:])
                ins.then_inc(lane[x]["xt_done"], 1)

            def apply_t(hp, r, x, n):
                s = lane[x]
                pe.wait_ge(s["tt_upd"], 6 * n + 6)
                pe.wait_ge(s["nv_out"], n + 1)
                for u, cc, c, j in units(r, x):
                    nc.tensor.matmul(ps[:, 4 * x + 1, u * P:u * P + HD], tinvT[x][:, u, :], tok[:, c, TOK_A, head(j)],
                                     start=True, stop=True)
                    ins = nc.tensor.matmul(ps[:, 4 * x + 1, u * P + HD:(u + 1) * P], tinvT[x][:, u, :],
                                           nv[x][:, u, :], start=True, stop=True)
                ins.then_inc(s["wu_done"], 1)

            def state_parts(hp, r, x, n):
                s = lane[x]
                pe.wait_ge(s["wu_out"], n + 1)
                for u, cc, c, j in units(r, x):
                    o = ps[head(j), 4 * x + 2, cc * P:(cc + 1) * P]
                    nc.tensor.matmul(o[:, 0:HD], wu[x][:, u, 0, :], tok[:, c, TOK_B, head(j)], start=True, stop=True)
                    nc.tensor.matmul(o[:, HD:P], tok[:, c, TOK_B, head(j)], wu[x][:, u, 1, :], start=True, stop=False)
                    ins = nc.tensor.matmul(o[:, HD:P], tok[:, c, TOK_K, head(j)], tok[:, c, TOK_V, head(j)],
                                           start=False, stop=True)
                ins.then_inc(s["gq_done"], 1)
                for u, cc, c, j in units(r, x):
                    ins = nc.tensor.matmul(ps[head(j), 4 * x + 3, cc * P:(cc + 1) * P], wu[x][:, u, 0, :],
                                           mm[x][:, u, K_RB, :], start=True, stop=True)
                ins.then_inc(s["rw_done"], 1)

            def chain(hp, r, x, n):
                pe.wait_ge(lane[x]["gq_out"], n + 1)
                for cc in range(2):
                    c = 4 * r + 2 * x + cc
                    if c:
                        pe.wait_ge(state_set, 8 * hp + c)
                    else:
                        pe.wait_ge(zero_set, 1)
                    nc.tensor.sem_inc(chain_open, 1)
                    for j in range(2):
                        ins = nc.tensor.matmul(ps[head(j), 4 * x, cc * HD:(cc + 1) * HD], gm[x][head(j), cc, :],
                                               state[head(j), c, :], start=True, stop=True)
                    ins.then_inc(chained, 1)

            def outputs(hp, r, x, n):
                s = lane[x]
                pe.wait_ge(s["rw_out"], n + 1)
                for u, cc, c, j in units(r, x):
                    o = ps[head(j), 4 * x + 1, cc * P:(cc + 1) * P]
                    nc.tensor.matmul(o, wu[x][:, u, 1, :], mm[x][:, u, K_RB, :], start=True, stop=False)
                    nc.tensor.matmul(o, state[head(j), c, :], rw[x][head(j), cc, :], start=False, stop=False)
                    ins = nc.tensor.matmul(o, tok[:, c, TOK_V, head(j)], mm[x][:, u, K_RK, :], start=False, stop=True)
                ins.then_inc(s["y_done"], 1)

            def group_norm(hp):
                pe.wait_ge(state_set, 8 * hp + 8)
                for x in range(LANES):
                    pe.wait_ge(lane[x]["y_out"], ROUNDS * hp + ROUNDS + PRIME_Y)
                for h in range(2):
                    nc.tensor.matmul(ps[:, h, :], heads1[:], yt[:, half(h)], start=True, stop=True).then_inc(y_mean, 1)
                for h in range(2):
                    nc.tensor.matmul(ps[:, 6 + h, :], lora[:, 1, :], m.lo[:, 1, half(h)], start=True, stop=True)\
                      .then_inc(g_done, 1)
                for h in range(2):
                    pe.wait_ge(y_sq, 2 * hp + h + 1)
                    nc.tensor.matmul(ps[:, 2 + h, :], heads1[:], tmp[:, 0, half(h)], start=True, stop=True)\
                      .then_inc(y_var, 1)

            with nc.tensor.Fori(0, PAIRS) as hp:
                front(hp)
                for r in range(ROUNDS):
                    n = ROUNDS * hp + r
                    for part in (grams, turn_t):
                        for x in range(LANES):
                            part(hp, r, x, n)
                    for lv in range(1, LEVELS):
                        for x in range(LANES):
                            level_x(lv, hp, r, x, n)
                            if lv > 1:
                                turn_grown(lv - 1, hp, r, x, n)
                        for x in range(LANES):
                            level_t(lv, hp, r, x, n)
                    for part in (apply_t, state_parts, chain, outputs):
                        for x in range(LANES):
                            part(hp, r, x, n)
                group_norm(hp)

        @block.scalar
        def _(act):
            nc.scalar.sem_inc(y_ln, PRIME_LN)
            for x in range(LANES):
                nc.scalar.sem_inc(lane[x]["y_out"], PRIME_Y)
            act.wait_ge(x_mixed, 1)
            nc.scalar.activation(m.lo[0:HD, 0, :], m.lo[0:HD, 0, :], ACT.Tanh).then_inc(x_set, 1)
            act.wait_ge(x_mixed, 2)
            nc.scalar.activation(m.lo[:, 1, :], m.lo[:, 1, :], ACT.Sigmoid).then_inc(x_set, 1)
            with nc.scalar.Fori(0, PAIRS) as hp:
                def copy_raw(t, bank, h, n):
                    act.wait_ge(raw_done, 6 * hp + n)
                    dst = lc if t == 2 else raw[:, t, :]
                    nc.scalar.activation(dst[:, half(h)], ps[:, bank + h, :], ACT.Copy).then_inc(raw_out, 1)

                def low_rank(dst, bank, v, q):
                    for h in range(2):
                        act.wait_ge(lo_done, 4 * hp + 2 * q + h + 1)
                        nc.scalar.activation(dst[:, half(h)], ps[:, bank + h, :], ACT.Sigmoid,
                                             bias=vec[:, v:v + 1]).then_inc(lo_out, 1)

                copy_raw(1, 0, 0, 1)
                copy_raw(1, 0, 1, 2)
                act.wait_ge(vec_set, hp + 1)
                low_rank(sig, 6, V_W0, 0)
                act.wait_ge(kraw, hp + 1)
                for h in range(2):
                    nc.scalar.activation(bonus[:, half(h)], kk[:, half(h)], ACT.Square).then_inc(ksq, 1)
                copy_raw(0, 2, 0, 3)
                act.wait_ge(lc_ready, hp + 1)
                nc.scalar.activation(dcol[:], dcol[:], ACT.Exp, scale=W_DECAY).then_inc(exps, 1)
                nc.scalar.activation(raw[:, 1, :], lc[:], ACT.Exp, scale=-W_DECAY).then_inc(exps, 1)
                nc.scalar.activation(tmp[:, 1, :], tmp[:, 1, :], ACT.Exp, scale=W_DECAY).then_inc(exps, 1)
                copy_raw(0, 2, 1, 4)
                low_rank(av, 0, V_A0, 1)
                act.wait_ge(mixed, 4 * hp + 2)
                nc.scalar.activation(raw[:, 0, :], lc[:], ACT.Exp, scale=W_DECAY).then_inc(exps, 1)
                act.wait_ge(kn_max, 2 * hp + 2)
                nc.scalar.activation(spare[:], spare[:], ACT.Ln).then_inc(kn_ln, 1)
                act.wait_ge(kn_ln, hp + 1)
                nc.scalar.activation(spare[:], spare[:], ACT.Exp, scale=-0.5).then_inc(kn_root, 1)
                copy_raw(2, 4, 0, 5)
                copy_raw(2, 4, 1, 6)
                for c in range(TT):
                    act.wait_ge(turned, 8 * hp + c + 1)
                    nc.scalar.activation(tok[:, c, :, :], ps[:, c, :], ACT.Copy).then_inc(turned_out, 1)
                for r in range(ROUNDS):
                    n = ROUNDS * hp + r
                    for x in range(LANES):
                        act.wait_ge(lane[x]["t_turned"], n + 1)
                        nc.scalar.activation(tinv[x][:], ps[:, 4 * x, :], ACT.Copy).then_inc(lane[x]["t_set"], 1)
                    for lv in range(1, LEVELS):
                        for x in range(LANES):
                            act.wait_ge(lane[x]["x_done"], 6 * n + lv)
                            nc.scalar.activation(xs[x][:], ps[:, 4 * x + 1, :], ACT.Copy).then_inc(lane[x]["x_out"], 1)
                            if lv == 1:
                                act.wait_ge(lane[x]["nv_done"], n + 1)
                                nc.scalar.activation(nv[x][:], ps[:, 4 * x, 0:4 * HD], ACT.Copy)\
                                  .then_inc(lane[x]["nv_out"], 1)
                    for x in range(LANES):
                        act.wait_ge(lane[x]["wu_done"], n + 1)
                        nc.scalar.activation(wu[x][:], ps[:, 4 * x + 1, :], ACT.Copy).then_inc(lane[x]["wu_out"], 1)
                    for x in range(LANES):
                        act.wait_ge(lane[x]["y_done"], n + 1)
                        c0 = 4 * r + 2 * x
                        nc.scalar.activation(yt[:, c0 * P:(c0 + 2) * P], ps[:, 4 * x + 1, 0:2 * P], ACT.Copy)\
                          .then_inc(lane[x]["y_out"], 1)
                for h in range(2):
                    act.wait_ge(y_cent, 2 * hp + h + 1)
                    nc.scalar.activation(tmp[:, 0, half(h)], kk[:, half(h)], ACT.Square).then_inc(y_sq, 1)
                for h in range(2):
                    act.wait_ge(y_var, 2 * hp + h + 1)
                    nc.scalar.activation(sig[:, half(h)], ps[:, 2 + h, :], ACT.Ln, bias=m.col[:, 4:5],
                                         scale=1.0 / HD).then_inc(y_ln, 1)
                act.wait_ge(y_ln, 2 * hp + 2 + PRIME_LN)
                nc.scalar.activation(sig[:], sig[:], ACT.Exp, scale=-0.5).then_inc(y_root, 1)

        @block.gpsimd
        def _(pool):
            for j in range(2):
                nc.gpsimd.memset(ar[head(1 - j), j, :, :, :], 0.0).then_inc(other_zero, 1)
                pool.wait_ge(other_zero, j + 1)
            pool.wait_ge(const_in, 16 * N_CONST)
            with nc.gpsimd.Fori(0, PAIRS) as hp:
                pool.wait_ge(mixed, 4 * hp + 2)
                pool.wait_ge(exps, 4 * hp + 4)
                for j in range(2):
                    ins = nc.gpsimd.tensor_tensor(ar[head(j), j, :, 1, :],
                                                  mix[head(j), 0, :].rearrange("p (c t) -> p c t", c=TT),
                                                  raw[head(j), 0, :].rearrange("p (c t) -> p c t", c=TT), ALU.mult)
                    ins.then_inc(pool_factors, 1)
                    pool.wait_ge(pool_factors, 3 * hp + j + 1)
                pool.wait_ge(rk_ready, hp + 1)
                pool.wait_ge(exps, 4 * hp + 2)
                nc.gpsimd.tensor_tensor(kt[:], mix[:, 1, :], raw[:, 1, :], ALU.mult).then_inc(pool_factors, 1)
                for r in range(ROUNDS):
                    n = ROUNDS * hp + r
                    for lv in range(1, LEVELS):
                        for x in range(LANES):
                            pool.wait_ge(lane[x]["masked"], 4 * n + 4)
                            if lv >= 2:
                                pool.wait_ge(lane[x]["x_done"], 6 * n + lv - 1)
                            nc.gpsimd.tensor_tensor(moff[x][:], mm[x][:, :, K_MT, :],
                                                    lvl[:, lv:lv + 1, :].broadcast_to([P, 4, P]), ALU.mult)\
                              .then_inc(lane[x]["off"], 1)

        @block.vector
        def _(dve):
            step = Steps(dve, vstep)
            nc.vector.sem_inc(bm_set, PRIME_BM)
            nc.vector.memset(state[:, 0, :], 0.0).then_inc(zero_set, 1)
            for t in range(2):
                token_shift(nc, step, m.lo[:, t, :], m.lo[:, t, :], tmp[:, t, :], m.mu_lo[:, t:t + 1], x_mixed)
            dve.wait_ge(const_in, 16 * N_CONST)

            def col(v):
                return vec[:, v:v + 1]

            def front(hp):
                nc.vector.tensor_copy(vec[:], flat(vecs[:, bass.ds(hp, 1), :])).then_inc(vec_set, 1)
                dve.wait_ge(vec_set, hp + 1)
                dve.wait_ge(raw_out, 6 * hp + 2)
                token_shift(nc, step, mix[:, 1, :], raw[:, 1, :], tmp[:, 0, :], col(V_MU_K), mixed)
                dve.wait_ge(mixed, 4 * hp + 1)
                nc.vector.tensor_scalar(kk[:], mix[:, 1, :], col(V_KK), None, ALU.mult).then_inc(kraw, 1)
                dve.wait_ge(lo_out, 4 * hp + 2)
                for c in range(TT):
                    chunk = slice(c * P, (c + 1) * P)
                    ins = nc.vector.tensor_tensor_scan(tmp[:, 0, chunk], ones[:], sig[:, chunk], 0.0, ALU.mult, ALU.add)
                step(ins)
                cum = tmp[:, 0, :].rearrange("p (c t) -> p c t", c=TT)
                lcv = lc[:].rearrange("p (c t) -> p c t", c=TT)
                step(nc.vector.tensor_tensor(lcv, cum, cum[:, :, MID:MID + 1].broadcast_to([P, TT, P]), ALU.subtract))
                nc.vector.tensor_copy(dcol[:, TT - 1:TT], lcv[:, TT - 1, P - 1:P])
                nc.vector.tensor_tensor(dcol[:, 0:TT - 1], lcv[:, 0:TT - 1, P - 1], cum[:, 1:TT, MID], ALU.add)
                nc.vector.tensor_tensor(tmp[:, 1, :], lc[:], sig[:], ALU.subtract).then_inc(lc_ready, 1)
                dve.wait_ge(raw_out, 6 * hp + 4)
                token_shift(nc, step, mix[:, 0, :], raw[:, 0, :], tmp[:, 0, :], col(V_MU_R), mixed)
                dve.wait_ge(lo_out, 4 * hp + 4)
                step(nc.vector.tensor_scalar(spare[:], av[:], 1.0, col(V_KA), ALU.subtract, ALU.mult))
                step(nc.vector.scalar_tensor_tensor(out=mix[:, 1, :], in0=spare[:], scalar=1.0, in1=mix[:, 1, :],
                                                    op0=ALU.add, op1=ALU.mult))
                dve.wait_ge(mixed, 4 * hp + 2)
                nc.vector.scalar_tensor_tensor(out=tmp[:, 0, :], in0=mix[:, 0, :], scalar=col(V_RK), in1=mix[:, 1, :],
                                               op0=ALU.mult, op1=ALU.mult).then_inc(rk_ready, 1)
                for h in range(2):
                    dve.wait_ge(kn_sum, 2 * hp + h + 1)
                    nc.vector.tensor_scalar(spare[:, half(h)], ps[:, 6 + h, :], 1e-24, None, ALU.max)\
                      .then_inc(kn_max, 1)
                dve.wait_ge(kn_root, hp + 1)
                step(nc.vector.tensor_tensor(kk[:], kk[:], spare[:], ALU.mult))
                step(nc.vector.tensor_tensor(av[:], av[:], kk[:], ALU.mult))
                dve.wait_ge(exps, 4 * hp + 4)
                nc.vector.tensor_tensor(bt[:], av[:], raw[:, 1, :], ALU.mult).then_inc(factors, 1)
                for j in range(2):
                    ins = nc.vector.scalar_tensor_tensor(
                        out=ar[head(j), j, :, 0, :], in0=kk[head(j), :].rearrange("p (c t) -> p c t", c=TT), scalar=-1.0,
                        in1=tmp[head(j), 1, :].rearrange("p (c t) -> p c t", c=TT), op0=ALU.mult, op1=ALU.mult)
                ins.then_inc(factors, 1)
                dve.wait_ge(raw_out, 6 * hp + 5)
                token_shift(nc, step, mix[:, 2, half(0)], lc[:, half(0)], sig[:, half(0)], col(V_MU_V), mixed)
                dve.wait_ge(raw_out, 6 * hp + 6)
                step(nc.vector.tensor_tensor(sig[:, half(1)], lc[:, HALF - 1:S - 1], lc[:, half(1)], ALU.subtract))
                nc.vector.scalar_tensor_tensor(out=mix[:, 2, half(1)], in0=sig[:, half(1)], scalar=col(V_MU_V),
                                               in1=lc[:, half(1)], op0=ALU.mult, op1=ALU.add).then_inc(mixed, 1)
                dve.wait_ge(mixed, 4 * hp + 4)
                for h in range(2):
                    dve.wait_ge(rk_sum, 2 * hp + h + 1)
                    nc.vector.tensor_tensor(bonus[:, half(h)], ps[:, 6 + h, :], mix[:, 2, half(h)], ALU.mult)\
                      .then_inc(bonus_set, 1)

            def masks(hp, r, x, n):
                s = lane[x]
                dve.wait_ge(s["y_out"], n + PRIME_Y)
                for u in range(4):
                    dve.wait_ge(s["gram"], 4 * n + u + 1)
                    nc.vector.tensor_tensor(mm[x][:, u, :, :], ps[:, 4 * x + u, :], mask4[:], ALU.mult)\
                      .then_inc(s["masked"], 1)

            def blocks_of_2(hp, r, x, n):
                s = lane[x]
                dve.wait_ge(s["masked"], 4 * n + 4)
                step(nc.vector.tensor_tensor(tinvT[x][:], mm[x][:, :, K_MT, :], lvl[:, 0:1, :].broadcast_to([P, 4, P]),
                                             ALU.mult))
                nc.vector.tensor_tensor(tinvT[x][:], tinvT[x][:],
                                        m.ident[:].rearrange("p (a n) -> p a n", a=1).broadcast_to([P, 4, P]),
                                        ALU.add).then_inc(s["tt_set"], 1)

            def grow(lv, hp, r, x, n):
                s = lane[x]
                dve.wait_ge(s["tx_done"], 5 * n + lv)
                nc.vector.tensor_tensor(tinv[x][:], ps[:, 4 * x + 2, :], tinv[x][:], ALU.add).then_inc(s["t_upd"], 1)

            def copy_turned(lv, hp, r, x, n):
                s = lane[x]
                dve.wait_ge(s["xt_done"], 6 * n + lv)
                nc.vector.tensor_copy(tinvT[x][:], ps[:, 4 * x + 3, :]).then_inc(s["tt_upd"], 1)

            def grow_last(hp, r, x, n):
                s = lane[x]
                dve.wait_ge(s["xt_done"], 6 * n + LEVELS - 1)
                nc.vector.tensor_tensor(tinvT[x][:], ps[:, 4 * x + 3, :], tinvT[x][:], ALU.add)\
                  .then_inc(s["tt_upd"], 1)

            def state_parts(hp, r, x, n):
                s = lane[x]
                dve.wait_ge(s["gq_done"], n + 1)
                parts = ps[:, 4 * x + 2, 0:2 * P].rearrange("p (c n) -> p c n", c=2)
                nc.vector.tensor_tensor(gm[x][:], parts[:, :, 0:HD],
                                        eye2[:].rearrange("p (a n) -> p a n", a=1).broadcast_to([P, 2, HD]), ALU.add)
                for cc in range(2):
                    c = 4 * r + 2 * x + cc
                    ins = nc.vector.tensor_scalar(qd[x][:, cc, :], parts[:, cc, HD:P], dcol[:, c:c + 1], None, ALU.mult)
                ins.then_inc(s["gq_out"], 1)
                dve.wait_ge(s["rw_done"], n + 1)
                c0 = 4 * r + 2 * x
                for j in range(2):
                    ins = nc.vector.tensor_tensor(rw[x][head(j), :, :],
                                                  ps[head(j), 4 * x + 3, 0:2 * P].rearrange("p (c n) -> p c n", c=2),
                                                  ar[head(j), j, c0:c0 + 2, 1, :], ALU.add)
                ins.then_inc(s["rw_out"], 1)

            def chain(hp, r, x, n):
                dve.wait_ge(lane[x]["gq_out"], n + 1)
                for cc in range(2):
                    c = 4 * r + 2 * x + cc
                    dve.wait_ge(chained, 8 * hp + c + 1)
                    nc.vector.scalar_tensor_tensor(out=state[:, c + 1, :], in0=ps[:, 4 * x, cc * HD:(cc + 1) * HD],
                                                   scalar=dcol[:, c:c + 1], in1=qd[x][:, cc, :], op0=ALU.mult,
                                                   op1=ALU.add).then_inc(state_set, 1)

            def group_norm(hp):
                for h in range(2):
                    dve.wait_ge(y_mean, 2 * hp + h + 1)
                    nc.vector.scalar_tensor_tensor(out=kk[:, half(h)], in0=ps[:, h, :], scalar=-1.0 / HD,
                                                   in1=yt[:, half(h)], op0=ALU.mult, op1=ALU.add).then_inc(y_cent, 1)
                dve.wait_ge(y_root, hp + 1)
                step(nc.vector.tensor_tensor(kk[:], kk[:], sig[:], ALU.mult))
                step(nc.vector.tensor_scalar(kk[:], kk[:], col(V_LNW), col(V_LNB), ALU.mult, ALU.add))
                step(nc.vector.tensor_tensor(kk[:], kk[:], bonus[:], ALU.add))
                dve.wait_ge(g_done, 2 * hp + 2)
                nc.vector.tensor_tensor(flat(m.bmT[:, bass.ds(hp, 1), :]), ps[:, 6:8, :].rearrange("p a n -> p (a n)"),
                                        kk[:], ALU.mult).then_inc(bm_set, 1)
                dve.wait_ge(bm_set, hp + 1 + PRIME_BM)

            with nc.vector.Fori(0, PAIRS) as hp:
                step.enter(hp, RECUR_STEPS)
                front(hp)
                for r in range(ROUNDS):
                    n = ROUNDS * hp + r
                    for part in (masks, blocks_of_2):
                        for x in range(LANES):
                            part(hp, r, x, n)
                    for lv in range(1, LEVELS - 1):
                        for part in (grow, copy_turned):
                            for x in range(LANES):
                                part(lv, hp, r, x, n)
                    for x in range(LANES):
                        grow_last(hp, r, x, n)
                    for part in (state_parts, chain):
                        for x in range(LANES):
                            part(hp, r, x, n)
                group_norm(hp)
                step.leave(PAIRS)


MAGIC = 1.5 * 2.0 ** 23
TWO_PI_PARTS = (6.28125, 0.0019350051879882812, 3.0198870e-07)
PI_IN = 3.1415925


def stage_project(nc, g, m):
    with ExitStack() as ctx:
        sb, psum, sem = allocators(nc, ctx)
        ps = psum("ps_proj", [P, 8, HALF])
        wslot = sb("wslot_p", [P, 2, KT * P])
        wtok = sb("wtok", [P, KT, TOKW])
        pos = sb("pos_i", [P, S], I32)
        angle = sb("angle", [P, S])
        turns = sb("turns", [P, S])
        cos_t = sb("cos_t", [P, S])
        sin_t = sb("sin_t", [P, S])
        swap = sb("swap", [P, 2, S])
        prod = [turns, angle]
        paired = sb("paired", [P, 2, S])
        blk = sb("blk", [P, 16, 2, N_CMP])
        pe_t = sb("pe_t", [P, 2, 16])
        cw1 = sb("cw1", [P, 16, CMP_HID])
        cw2 = sb("cw2", [P, 2, 2, HD])
        cb1 = sb("cb1", [P, 2, 2])
        cb2k = sb("cb2k", [HD, 1])
        cb2v = sb("cb2v", [1, HD])
        one_row = sb("one_row", [1, HD])
        hid = sb("hid", [P, 2, 2 * N_CMP])

        small_in, wtok_in, cw1_in = sem("small_in_p"), sem("wtok_in"), sem("cw1_in")
        cw1_v = [sem(f"cw1_v{f}") for f in range(2)]
        w_in = [sem(f"w_in_p{s}") for s in range(2)]
        tile_done, tile_out, vtok_done, vtok_out = sem("tile_done"), sem("tile_out"), sem("vtok_done"), sem("vtok_out")
        reduced, absed, tables = sem("reduced"), sem("absed"), sem("tables")
        swapped = [sem(f"swapped{s}") for s in range(2)]
        sin_prod, rotated, paired_in, blk_set = sem("sin_prod"), sem("rotated"), sem("paired_in"), sem("blk_set")
        row_set, hid_half, gelu_out, cmp_done, cmp_out = (sem(n) for n in ("row_set", "hid_half", "gelu_out", "cmp_done",
                                                                           "cmp_out"))
        vstep = sem("vstep_p")
        PRIME_TILE = 4
        TURNS = N_QKV // 2
        VC = N_QKV - 1
        N_SMALL = 6
        block = ctx.enter_context(nc.Block())

        def half(h):
            return slice(h * HALF, (h + 1) * HALF)

        def pair_up(sy, src):
            for grp in range(2):
                rows = slice(HD * grp, HD * grp + HD)
                sy.dma_start(paired[0:HD, grp, :], src[rows, :]).then_inc(paired_in, 16)
                sy.dma_start(paired[HD:P, grp, 0:S - 1], src[rows, 1:S]).then_inc(paired_in, 16)

        @block.sync
        def _(sy):
            sy.dma_start(pos[:], g.pos).then_inc(small_in, 16)
            for s in range(2):
                sy.dma_start(wslot[:, s, :], g.w_tiles[:, T_QKV + s, :]).then_inc(w_in[s], 16)
            for dst, src in ((pe_t[:], g.cmp_pe), (cw2[:], g.cmp_w2), (cb1[:], g.cmp_b1), (cb2k[:], g.cmp_b2k),
                             (cb2v[:], g.cmp_b2v)):
                sy.dma_start(dst, src).then_inc(small_in, 16)
            sy.dma_start(wtok[:], g.w_tok).then_inc(wtok_in, 16)
            sy.dma_start(cw1[:], g.cmp_w1[0]).then_inc(cw1_in, 16)
            with nc.sync.Fori(1, TURNS) as i:
                for s in range(2):
                    sy.wait_ge(tile_done, 4 * i + 2 * s - 2 + PRIME_TILE)
                    sy.dma_start(wslot[:, s, :], flat(g.w_tiles[:, bass.ds(2 * i + T_QKV + s, 1), :]))\
                      .then_inc(w_in[s], 16)
            for t in range(N_ROPE):
                sy.wait_ge(tile_out, 2 * (t + 1) + PRIME_TILE)
                if t >= 2:
                    sy.wait_ge(sin_prod, t - 1)
                for q in range(4):
                    o = q ^ 1
                    sy.dma_start(swap[32 * q:32 * q + 32, t % 2, :], m.qkv[32 * o:32 * o + 32, t, :])\
                      .then_inc(swapped[t % 2], 16)
                if t == 2:
                    sy.wait_ge(rotated, 1)
                    pair_up(sy, m.qkv[:, 0, :])
            sy.wait_ge(tile_out, 2 * (VC + 1) + PRIME_TILE)
            sy.wait_ge(blk_set, 1)
            pair_up(sy, m.qkv[:, VC, :])
            for f in range(2):
                sy.wait_ge(hid_half, f + 1)
                sy.dma_start(cw1[:, :, f * P:(f + 1) * P], g.cmp_w1[1][:, :, f * P:(f + 1) * P]).then_inc(cw1_v[f], 16)

        @block.tensor
        def _(pe):
            nc.tensor.sem_inc(tile_done, PRIME_TILE)
            with nc.tensor.Fori(0, TURNS) as i:
                for s in range(2):
                    pe.wait_ge(w_in[s], 16 * i + 16)
                    for h in range(2):
                        pe.wait_ge(tile_out, 4 * i + 2 * s + h + 1)
                        for k in range(KT):
                            ins = nc.tensor.matmul(ps[:, 2 * s + h, :], wslot[:, s, k * P:(k + 1) * P],
                                                   m.hT[:, k, half(h)], start=(k == 0), stop=(k == KT - 1))
                        ins.then_inc(tile_done, 1)
            pe.wait_ge(wtok_in, 16)
            for t in range(TT):
                if t >= 2:
                    pe.wait_ge(vtok_out, t - 1)
                for k in range(KT):
                    ins = nc.tensor.matmul(ps[:, 4 + t % 2, 0:TOKW], m.hT[:, k, t * P:(t + 1) * P], wtok[:, k, :],
                                           start=(k == 0), stop=(k == KT - 1))
                ins.then_inc(vtok_done, 1)
            pe.wait_ge(small_in, 16 * N_SMALL)
            pe.wait_ge(row_set, 1)
            for kv in range(2):
                pe.wait_ge(cw1_in, 16)
                pe.wait_ge(blk_set, kv + 1)
                for f in range(2):
                    if kv:
                        pe.wait_ge(cw1_v[f], 16)
                    for c in range(16):
                        ins = nc.tensor.matmul(ps[:, 6, f * 2 * N_CMP:(f + 1) * 2 * N_CMP], cw1[:, c, f * P:(f + 1) * P],
                                               blk[:, c, :, :], start=(c == 0), stop=(c == 15))
                    ins.then_inc(hid_half, 1)
                pe.wait_ge(gelu_out, 2 * kv + 2)
                if kv == 0:
                    for f in range(2):
                        ins = nc.tensor.matmul(ps[0:HD, 7, 0:2 * N_CMP], cw2[:, 0, f, :], hid[:, f, :],
                                               start=(f == 0), stop=(f == 1))
                    ins.then_inc(cmp_done, 1)
                else:
                    pe.wait_ge(cmp_out, 1)
                    for grp in range(2):
                        o = ps[0:N_CMP, 7, grp * HD:(grp + 1) * HD]
                        for f in range(2):
                            nc.tensor.matmul(o, hid[:, f, grp * N_CMP:(grp + 1) * N_CMP], cw2[:, 1, f, :],
                                             start=(f == 0), stop=False)
                        ins = nc.tensor.matmul(o, one_row[0:1, 0:N_CMP], cb2v[:], start=False, stop=True)
                    ins.then_inc(cmp_done, 1)

        @block.scalar
        def _(act):
            nc.scalar.sem_inc(tile_out, PRIME_TILE)
            act.wait_ge(reduced, 1)
            nc.scalar.activation(turns[:], angle[:], ACT.Abs).then_inc(absed, 1)
            nc.scalar.activation(sin_t[:], angle[:], ACT.Sin, scale=m.col[:, 1:2]).then_inc(tables, 1)
            act.wait_ge(absed, 1)
            nc.scalar.activation(cos_t[:], turns[:], ACT.Sin, bias=m.col[:, 2:3], scale=-1.0).then_inc(tables, 1)
            with nc.scalar.Fori(0, TURNS) as i:
                for s in range(2):
                    for h in range(2):
                        act.wait_ge(tile_done, 4 * i + 2 * s + h + 1 + PRIME_TILE)
                        nc.scalar.activation(flat(m.qkv[:, bass.ds(2 * i + s, 1), half(h)]), ps[:, 2 * s + h, :],
                                             ACT.Copy).then_inc(tile_out, 1)
            for t in range(TT):
                act.wait_ge(vtok_done, t + 1)
                nc.scalar.activation(m.vtok[:, t, :], ps[:, 4 + t % 2, 0:2 * P], ACT.Copy)
                nc.scalar.activation(m.gates[:, t, :], ps[:, 4 + t % 2, 2 * P:TOKW], ACT.Sigmoid).then_inc(vtok_out, 1)
            act.wait_ge(small_in, 16 * N_SMALL)
            for kv in range(2):
                act.wait_ge(hid_half, 2 * kv + 2)
                if kv:
                    act.wait_ge(cmp_done, 1)
                for f in range(2):
                    nc.scalar.activation(hid[:, f, :], ps[:, 6, f * 2 * N_CMP:(f + 1) * 2 * N_CMP], ACT.Gelu_apprx_tanh,
                                         bias=cb1[:, kv, f:f + 1]).then_inc(gelu_out, 1)
                act.wait_ge(cmp_done, kv + 1)
                if kv == 0:
                    for grp in range(2):
                        ins = nc.scalar.activation(m.kcmp[HD * grp:HD * grp + HD, :],
                                                   ps[0:HD, 7, grp * N_CMP:(grp + 1) * N_CMP], ACT.Identity, bias=cb2k[:])
                else:
                    ins = nc.scalar.activation(m.vcmp[0:N_CMP, :, :], ps[0:N_CMP, 7, 0:2 * HD], ACT.Copy)
                ins.then_inc(cmp_out, 1)
            act.wait_ge(cmp_out, 2)

        @block.gpsimd
        def _(pool):
            nc.gpsimd.memset(one_row[:], 1.0).then_inc(row_set, 1)
            pool.wait_ge(tables, 2)
            for t in range(N_ROPE):
                pool.wait_ge(swapped[t % 2], 64 * (t // 2 + 1))
                if t >= 2:
                    pool.wait_ge(rotated, t - 1)
                nc.gpsimd.tensor_tensor(prod[t % 2][:], swap[:, t % 2, :], sin_t[:], ALU.mult).then_inc(sin_prod, 1)

        @block.vector
        def _(dve):
            step = Steps(dve, vstep)
            dve.wait_ge(small_in, 16 * N_SMALL)
            step(nc.vector.tensor_copy(angle[:], pos[:]))
            step(nc.vector.tensor_scalar(angle[:], angle[:], m.col[:, 0:1], None, ALU.mult))
            step(nc.vector.tensor_scalar(turns[:], angle[:], 1.0 / (2 * math.pi), MAGIC, ALU.mult, ALU.add))
            step(nc.vector.tensor_scalar(turns[:], turns[:], MAGIC, None, ALU.subtract))
            for part in TWO_PI_PARTS:
                step(nc.vector.scalar_tensor_tensor(out=angle[:], in0=turns[:], scalar=-part, in1=angle[:],
                                                    op0=ALU.mult, op1=ALU.add))
            nc.vector.tensor_scalar(angle[:], angle[:], PI_IN, -PI_IN, ALU.min, ALU.max).then_inc(reduced, 1)
            dve.wait_ge(tables, 2)

            def blocks(kv):
                dve.wait_ge(paired_in, 64 * (kv + 1))
                if kv:
                    dve.wait_ge(hid_half, 2)
                for c in range(16):
                    ins = nc.vector.tensor_scalar(blk[:, c, :, :], paired[:, :, 2 * c:2 * c + 16 * (N_CMP - 1) + 1:16],
                                                  pe_t[:, kv, c:c + 1], None, ALU.add)
                ins.then_inc(blk_set, 1)

            for t in range(N_ROPE):
                dve.wait_ge(swapped[t % 2], 64 * (t // 2 + 1))
                step(nc.vector.tensor_tensor(m.qkv[:, t, :], m.qkv[:, t, :], cos_t[:], ALU.mult))
                dve.wait_ge(sin_prod, t + 1)
                nc.vector.tensor_tensor(m.qkv[:, t, :], m.qkv[:, t, :], prod[t % 2][:], ALU.add).then_inc(rotated, 1)
            blocks(0)
            blocks(1)
            dve.wait_ge(rotated, N_ROPE)


WIN_TILES = 4


def attention_units():
    units, chunks = [], 0
    for j in range(2):
        for qt in range(TT):
            for br, name in enumerate(("cmp", "slc", "win")):
                first = max(0, qt - WIN_TILES) if name == "win" else 0
                tiles = [None] if name == "cmp" else list(range(first, qt + 1))
                u = Names()
                u.n, u.j, u.qt, u.name, u.tiles, u.slot = len(units), j, qt, name, tiles, br
                u.gate = BRANCH_GATE[name]
                u.first_chunk = chunks
                u.chunks = [tiles[a:a + 4] for a in range(0, len(tiles), 4)]
                u.cols = N_CMP if name == "cmp" else P * len(tiles)
                chunks += len(u.chunks)
                units.append(u)
    return units, chunks


BRANCH_GATE = {"cmp": 0, "slc": 1, "win": 2}
AHEAD = 3


def stage_attend(nc, g, m):
    units, N_CHUNK = attention_units()
    N_UNIT = len(units)
    with ExitStack() as ctx:
        sb, psum, sem = allocators(nc, ctx)
        scores = [psum("ps_s_cmp", [P, HALF]), psum("ps_s_slc", [P, 2 * HALF]), psum("ps_s_win", [P, 2 * HALF])]
        ps_pt = psum("ps_pt", [P, 2, HALF])
        ps_o = psum("ps_o", [P, HALF])
        qcur = sb("qcur", [P, 2, S])
        gcur = sb("gcur", [P, TT, 2, 3])
        bias = sb("bias", [P, 2, P])
        bias_cmp = sb("bias_cmp", [P, TT, N_CMP])
        prob = [sb("prob_cmp", [P, N_CMP]), m.qkv[:, N_QKV - 1, :],
                sb("prob_win", [P, (WIN_TILES + 1) * P])]
        pt = sb("pt", [P, 2, HALF])
        nmax = sb("nmax", [P, AHEAD])
        rowsum = sb("rowsum", [P, AHEAD])
        weight = sb("weight", [P, AHEAD])

        const_in, q_set, copied, g_set = sem("const_in_t"), sem("q_set"), sem("g_copied"), sem("g_set")
        scored, biased, nmax_set, exp_done = sem("scored"), sem("biased"), sem("nmax_set"), sem("exp_done")
        pt_done, pt_out, o_done, weight_set, scaled, o_used = (sem(n) for n in ("pt_done", "pt_out", "o_done",
                                                                                "weight_set", "scaled", "o_used"))
        turn_open = sem("turn_open")
        block = ctx.enter_context(nc.Block())
        PRIME_U, PRIME_C, PRIME_O = AHEAD, 2, 1
        N_OUT = 2 * TT

        def head(j):
            return slice(HD * j, HD * j + HD)

        @block.sync
        def _(sy):
            sy.dma_start(bias[:], g.bias).then_inc(const_in, 16)
            sy.dma_start(bias_cmp[:], g.bias_cmp).then_inc(const_in, 16)
            for s in range(2):
                load_ab(sy, g, m, s, s)
            load_gates(sy, g, m, 0)

        @block.tensor
        def _(pe):
            def score(i, u):
                if u.n == 0:
                    pe.wait_ge(q_set, i + 1)
                pe.wait_ge(exp_done, N_UNIT * i + u.n - AHEAD + 1 + PRIME_U)
                q = qcur[:, u.j, u.qt * P:(u.qt + 1) * P]
                o = scores[u.slot]
                if u.name == "cmp":
                    ins = nc.tensor.matmul(o[:, 0:N_CMP], q, m.kcmp[:], start=True, stop=True)
                else:
                    keys = m.qkv[:, 1 if u.name == "slc" else 2, :]
                    for a in range(0, u.cols, HALF):
                        w = min(HALF, u.cols - a)
                        k0 = u.tiles[0] * P + a
                        ins = nc.tensor.matmul(o[:, a:a + w], q, keys[:, k0:k0 + w], start=True, stop=True)
                ins.then_inc(scored, 1)

            def turn(i, u, c):
                e = N_CHUNK * i + u.first_chunk + c
                if c == 0:
                    pe.wait_ge(scaled, N_UNIT * i + u.n + 1)
                slot = (u.first_chunk + c) % 2
                pe.wait_ge(pt_out, e - 2 + 1 + PRIME_C)
                if u.name == "cmp":
                    nc.tensor.sem_inc(turn_open, 1)
                for b, _ in enumerate(u.chunks[c]):
                    if u.name == "cmp":
                        ins = nc.tensor.transpose(ps_pt[0:N_CMP, slot, 0:P], prob[u.slot][:], m.ident[:])
                    else:
                        a = (4 * c + b) * P
                        ins = nc.tensor.transpose(ps_pt[:, slot, b * P:(b + 1) * P], prob[u.slot][:, a:a + P],
                                                  m.ident[:])
                ins.then_inc(pt_done, 1)

            def weigh(i, u, c):
                e = N_CHUNK * i + u.first_chunk + c
                slot = (u.first_chunk + c) % 2
                if u.name == "cmp":
                    pe.wait_ge(o_used, N_OUT * i + u.n // AHEAD + PRIME_O)
                pe.wait_ge(pt_out, e + 1 + PRIME_C)
                if u.name == "cmp":
                    nc.tensor.sem_inc(turn_open, 1)
                o = ps_o[0:HD, 0:P]
                for b, t in enumerate(u.chunks[c]):
                    if u.name == "cmp":
                        ins = nc.tensor.matmul(o, m.vcmp[0:N_CMP, u.j, :], pt[0:N_CMP, slot, 0:P], start=True, stop=False)
                    else:
                        v0 = (0 if u.name == "slc" else P) + u.j * HD
                        last = u.name == "win" and t == u.tiles[-1]
                        ins = nc.tensor.matmul(o, m.vtok[:, t, v0:v0 + HD], pt[:, slot, b * P:(b + 1) * P],
                                               start=False, stop=last)
                        if last:
                            ins.then_inc(o_done, 1)

            pe.wait_ge(const_in, 32)
            with nc.tensor.Fori(0, PAIRS) as i:
                for u in units[:AHEAD]:
                    score(i, u)
                for u in units:
                    n = len(u.chunks)
                    turn(i, u, 0)
                    if u.n + AHEAD < N_UNIT:
                        score(i, units[u.n + AHEAD])
                    for c in range(n):
                        if c + 1 < n:
                            turn(i, u, c + 1)
                        weigh(i, u, c)

        @block.scalar
        def _(act):
            nc.scalar.sem_inc(exp_done, PRIME_U)
            nc.scalar.sem_inc(pt_out, PRIME_C)
            with nc.scalar.Fori(0, PAIRS) as i:
                def softmax(u):
                    act.wait_ge(nmax_set, N_UNIT * i + u.n + 1)
                    s = u.slot
                    if u.n >= AHEAD:
                        b = units[u.n - AHEAD]
                        act.wait_ge(pt_done, N_CHUNK * i + b.first_chunk + len(b.chunks))
                    nc.scalar.activation(prob[s][:, 0:u.cols], scores[s][:, 0:u.cols], ACT.Exp, bias=nmax[:, s:s + 1],
                                         accum_out=rowsum[:, s:s + 1]).then_inc(exp_done, 1)

                def copy_pt(u, c):
                    e = N_CHUNK * i + u.first_chunk + c
                    slot = (u.first_chunk + c) % 2
                    act.wait_ge(pt_done, e + 1)
                    rows = N_CMP if u.name == "cmp" else P
                    w = P * len(u.chunks[c])
                    nc.scalar.activation(pt[0:rows, slot, 0:w], ps_pt[0:rows, slot, 0:w], ACT.Copy).then_inc(pt_out, 1)

                softmax(units[0])
                softmax(units[1])
                for u in units:
                    for c in range(len(u.chunks)):
                        copy_pt(u, c)
                    if u.n + 2 < N_UNIT:
                        softmax(units[u.n + 2])

        @block.vector
        def _(dve):
            nc.vector.sem_inc(o_used, PRIME_O)
            for j in range(2):
                nc.vector.memset(qcur[head(1 - j), j, :], 0.0)
            dve.wait_ge(const_in, 32)
            with nc.vector.Fori(0, PAIRS) as i:
                dve.wait_ge(o_used, N_OUT * i + PRIME_O)
                for j in range(2):
                    ins = nc.vector.tensor_scalar(qcur[head(j), j, :], flat(m.qkv[head(j), bass.ds(i + 3, 1), :]),
                                                  HD ** -0.5, None, ALU.mult)
                ins.then_inc(q_set, 1)
                for j in range(2):
                    ins = nc.vector.tensor_copy(gcur[:, :, j, :], m.gates[:, :, bass.ds(i * 3 + 3 * PAIRS * j, 3)])
                ins.then_inc(copied, 1)
                dve.wait_ge(copied, i + 1)
                nc.vector.tensor_scalar(gcur[:, 0, :, BRANCH_GATE["cmp"]], gcur[:, 0, :, BRANCH_GATE["cmp"]],
                                        m.col[:, 5:6], None, ALU.mult).then_inc(g_set, 1)
                dve.wait_ge(g_set, i + 1)

                def maximum(u):
                    n = N_UNIT * i + u.n
                    s = u.slot
                    dve.wait_ge(scored, n + 1)
                    if u.name == "cmp":
                        o, b = scores[s][:, 0:N_CMP], bias_cmp[:, u.qt, :]
                    elif u.name == "win" and len(u.tiles) == WIN_TILES + 1:
                        o = scores[s][:, 0:u.cols].rearrange("p (t k) -> p t k", k=P)[:, 0:WIN_TILES + 1:WIN_TILES, :]
                        b = bias[:]
                    else:
                        o, b = scores[s][:, u.cols - P:u.cols], bias[:, 1, :]
                    nc.vector.tensor_tensor(o, o, b, ALU.add).then_inc(biased, 1)
                    dve.wait_ge(biased, n + 1)
                    nc.vector.tensor_reduce(nmax[:, s:s + 1], scores[s][:, 0:u.cols], AXX, ALU.max, negate=True)\
                      .then_inc(nmax_set, 1)

                def scale(u):
                    n = N_UNIT * i + u.n
                    s = u.slot
                    dve.wait_ge(exp_done, n + 1 + PRIME_U)
                    nc.vector.reciprocal(weight[:, s:s + 1], rowsum[:, s:s + 1]).then_inc(weight_set, 1)
                    dve.wait_ge(weight_set, n + 1)
                    p, gate = prob[s][:, 0:u.cols], gcur[:, u.qt, u.j, u.gate:u.gate + 1]
                    nc.vector.tensor_scalar(p, p, weight[:, s:s + 1], gate, ALU.mult, ALU.mult).then_inc(scaled, 1)

                def output(u):
                    dve.wait_ge(o_done, N_OUT * i + u.n // AHEAD + 1)
                    nc.vector.tensor_copy(flat(m.oAT[head(u.j), bass.ds(i, 1), u.qt * P:(u.qt + 1) * P]),
                                          ps_o[0:HD, 0:P]).then_inc(o_used, 1)

                for u in units[:AHEAD]:
                    maximum(u)
                scale(units[0])
                for u in units:
                    if u.n + 1 < N_UNIT:
                        scale(units[u.n + 1])
                    if u.n + AHEAD < N_UNIT:
                        maximum(units[u.n + AHEAD])
                    if u.name == "win":
                        output(u)
            dve.wait_ge(o_used, PAIRS * N_OUT + PRIME_O)


def load_ab(sy, g, m, f, s):
    sy.dma_start(m.wab[:, s, :, :], g.w_ab[:, bass.ds(f * 8, 8), :]).then_inc(m.wab_in[s], 16)


def load_gates(sy, g, m, f):
    sy.dma_start(m.wg[:], g.w_tiles[:, bass.ds(2 * f + T_GATE, 2), :]).then_inc(m.wg_in, 16)


def stage_merge(nc, g, m):
    with ExitStack() as ctx:
        sb, psum, sem = allocators(nc, ctx)
        ps = psum("ps_merge", [P, 8, HALF])
        h_hi = sb("h_hi", [P, KT, S], F32R)
        h_lo = sb("h_lo", [P, KT, S], F32R)
        wg, wab, wg_in, wab_in = m.wg, m.wab, m.wg_in, m.wab_in
        wg_hi = sb("wg_hi", [P, 2, KT * P], F32R)
        wg_lo = sb("wg_lo", [P, 2, KT * P], F32R)
        sg = sb("sg", [P, 2, 2, HALF])
        h_high, h_low, w_high, w_low = (sem(n) for n in ("h_high", "h_low", "w_high", "w_low"))
        gated, sig_out, projected, weighed, merged = (
            sem(n) for n in ("gated", "sig_out", "projected", "weighed", "merged"))
        PRIME = 2
        PRIME_W = 2
        TURNS = KT // 2
        block = ctx.enter_context(nc.Block())

        def half(h):
            return slice(h * HALF, (h + 1) * HALF)

        @block.sync
        def _(sy):
            sy.wait_ge(w_low, 2)
            load_gates(sy, g, m, 1)
            with nc.sync.Fori(1, TURNS) as i:
                for s in range(2):
                    sy.wait_ge(projected, 4 * i + 2 * s - 2)
                    load_ab(sy, g, m, 2 * i + s, s)
                    sy.wait_ge(w_low, 4 * i + 2 * s)
                    load_gates(sy, g, m, 2 * i + s)

        @block.tensor
        def _(pe):
            def unit(i, s, h, first):
                n = 4 * i + 2 * s + h
                pe.wait_ge(merged, n - 1 + PRIME)
                for q, src in enumerate((m.oAT, m.bmT)):
                    for k in range(PAIRS):
                        ins = nc.tensor.matmul(ps[:, 4 * h + 2 + q, :], wab[:, s, q * PAIRS + k, :],
                                               src[:, k, half(h)], start=(k == 0), stop=(k == PAIRS - 1))
                ins.then_inc(projected, 1)
                if h == 0:
                    pe.wait_ge(w_high, 4 * i + 2 * s + 2)
                for k in range(KT):
                    if first:
                        pe.wait_ge(h_high, k + 1)
                    for q in range(2):
                        nc.tensor.matmul(ps[:, 4 * h + q, :], wg_hi[:, q, k * P:(k + 1) * P], h_hi[:, k, half(h)],
                                         start=(k == 0), stop=False)
                for k in range(KT):
                    if first:
                        pe.wait_ge(h_low, k + 1)
                    for q in range(2):
                        nc.tensor.matmul(ps[:, 4 * h + q, :], wg_hi[:, q, k * P:(k + 1) * P], h_lo[:, k, half(h)],
                                         start=False, stop=False)
                if h == 0:
                    pe.wait_ge(w_low, 4 * i + 2 * s + 2)
                for k in range(KT):
                    for q in range(2):
                        ins = nc.tensor.matmul(ps[:, 4 * h + q, :], wg_lo[:, q, k * P:(k + 1) * P], h_hi[:, k, half(h)],
                                               start=False, stop=(k == KT - 1))
                ins.then_inc(gated, 1)

            for s in range(2):
                pe.wait_ge(wab_in[s], 16)
                for h in range(2):
                    unit(0, s, h, s == 0 and h == 0)
            with nc.tensor.Fori(1, TURNS) as i:
                for s in range(2):
                    pe.wait_ge(wab_in[s], 16 * i + 16)
                    for h in range(2):
                        unit(i, s, h, False)

        @block.scalar
        def _(act):
            nc.scalar.sem_inc(gated, PRIME_W)

            def tile(i, s, first):
                act.wait_ge(wg_in, 32 * i + 16 * s + 16)
                act.wait_ge(gated, 4 * i + 2 * s + PRIME_W)
                for q in range(2):
                    nc.scalar.activation(wg_hi[:, q, :], wg[:, q, :], ACT.Copy).then_inc(w_high, 1)
                if first:
                    for k in range(KT):
                        nc.scalar.activation(h_hi[:, k, :], m.hT[:, k, :], ACT.Copy).then_inc(h_high, 1)
                for h in range(2):
                    act.wait_ge(gated, 4 * i + 2 * s + h + 1 + PRIME_W)
                    nc.scalar.activation(sg[:, h, :, :], ps[:, 4 * h:4 * h + 2, :], ACT.Sigmoid).then_inc(sig_out, 1)

            for s in range(2):
                tile(0, s, s == 0)
            with nc.scalar.Fori(1, TURNS) as i:
                for s in range(2):
                    tile(i, s, False)

        @block.gpsimd
        def _(pool):
            with nc.gpsimd.Fori(0, TURNS) as i:
                for s in range(2):
                    for q in range(2):
                        pool.wait_ge(w_high, 4 * i + 2 * s + q + 1)
                        nc.gpsimd.tensor_tensor(wg_lo[:, q, :], wg[:, q, :], wg_hi[:, q, :], ALU.subtract)\
                          .then_inc(w_low, 1)

        @block.vector
        def _(dve):
            nc.vector.sem_inc(merged, PRIME)
            for k in range(KT):
                dve.wait_ge(h_high, k + 1)
                nc.vector.tensor_tensor(h_lo[:, k, :], m.hT[:, k, :], h_hi[:, k, :], ALU.subtract).then_inc(h_low, 1)
            with nc.vector.Fori(0, TURNS) as i:
                for s in range(2):
                    for h in range(2):
                        n = 4 * i + 2 * s + h
                        dve.wait_ge(projected, n + 1)
                        dve.wait_ge(sig_out, n + 1)
                        nc.vector.tensor_tensor(sg[:, h, :, :], ps[:, 4 * h + 2:4 * h + 4, :], sg[:, h, :, :],
                                                ALU.mult).then_inc(weighed, 1)
                        dve.wait_ge(weighed, n + 1)
                        nc.vector.tensor_tensor(flat(m.mT[:, bass.ds(2 * i + s, 1), half(h)]), sg[:, h, 0, :],
                                                sg[:, h, 1, :], ALU.add).then_inc(merged, 1)
            dve.wait_ge(merged, 4 * TURNS + PRIME)


def stage_output(nc, g, m):
    with ExitStack() as ctx:
        sb, psum, sem = allocators(nc, ctx)
        ps = psum("ps_out", [P, 8, HALF])
        wout = sb("wout", [P, KT, D])
        gffn = sb("gffn", [P, D])
        wrt = sb("wrt", [P, KT, N_LOG])
        brt = sb("brt", [1, N_LOG])
        one_row = sb("one_row_o", [1, P])
        square = sb("square_o", [P, D])
        ss = sb("ss", [P, TT, 3])
        h2 = sb("h2", [P, 2, D])
        h2T = sb("h2T", [P, 2, D])
        small_in = sem("small_in_o")
        w_in = [sem(f"w_in_o{k}") for k in range(KT)]
        x_in = [sem(f"x_in_o{t}") for t in range(TT)]
        row_set, summed, x2_set, squared, rooted, inv_set, h2_set, turned, turned_out, logit_done, logit_out = (
            sem(n) for n in ("row_set_o", "summed_o", "x2_set", "squared_o", "rooted_o", "inv_set_o", "h2_set",
                             "turned_o", "turned_out_o", "logit_done", "logit_out"))
        h2_stored = [sem(f"h2_stored{s}") for s in range(2)]
        block = ctx.enter_context(nc.Block())

        @block.sync
        def _(sy):
            for k in range(KT):
                sy.dma_start(wout[:, k, :], g.w_out[:, k, :]).then_inc(w_in[k], 16)
                if k < 2:
                    sy.dma_start(m.x2[:, k, :], g.x[k * P:(k + 1) * P, :]).then_inc(x_in[k], 16)
            for dst, src in ((gffn[:], g.gffn), (wrt[:], g.w_rt), (brt[:], g.b_rt)):
                sy.dma_start(dst, src).then_inc(small_in, 16)
            for t in range(2, TT):
                sy.dma_start(m.x2[:, t, :], g.x[t * P:(t + 1) * P, :]).then_inc(x_in[t], 16)
            for t in range(TT):
                sy.wait_ge(h2_set, t + 1)
                sy.dma_start(g.h2[t * P:(t + 1) * P, :], h2[:, t % 2, :]).then_inc(h2_stored[t % 2], 16)
            for s in range(2):
                sy.wait_ge(h2_stored[s], 16 * TT // 2)

        @block.tensor
        def _(pe):
            def project(t):
                if t >= 2:
                    pe.wait_ge(x2_set, t - 1)
                for k in range(KT):
                    pe.wait_ge(w_in[k], 16)
                    for h in range(2):
                        ins = nc.tensor.matmul(ps[:, 2 * (t % 2) + h, :], m.mT[:, k, t * P:(t + 1) * P],
                                               wout[:, k, h * HALF:(h + 1) * HALF], start=(k == 0), stop=(k == KT - 1))
                ins.then_inc(summed, 1)

            def turn(t):
                pe.wait_ge(h2_set, t + 1)
                if t >= 1:
                    pe.wait_ge(turned_out, 2 * t)
                for k in range(KT):
                    ins = nc.tensor.transpose(ps[:, 4 + k // 4, (k % 4) * P:(k % 4 + 1) * P],
                                              h2[:, t % 2, k * P:(k + 1) * P], m.ident[:])
                    if k % 4 == 3:
                        ins.then_inc(turned, 1)

            def logits(t):
                pe.wait_ge(turned_out, 2 * t + 2)
                if t >= 2:
                    pe.wait_ge(logit_out, t - 1)
                o = ps[:, 6 + t % 2, 0:N_LOG]
                for k in range(KT):
                    nc.tensor.matmul(o, h2T[:, t % 2, k * P:(k + 1) * P], wrt[:, k, :], start=(k == 0), stop=False)
                nc.tensor.matmul(o, one_row[:], brt[:], start=False, stop=True).then_inc(logit_done, 1)

            project(0)
            project(1)
            pe.wait_ge(small_in, 48)
            pe.wait_ge(row_set, 1)
            for t in range(TT):
                if t + 2 < TT:
                    project(t + 2)
                turn(t)
                if t >= 1:
                    logits(t - 1)
            logits(TT - 1)

        @block.scalar
        def _(act):
            for t in range(TT):
                act.wait_ge(x2_set, t + 1)
                nc.scalar.activation(square[:], m.x2[:, t, :], ACT.Square, accum_out=ss[:, t, 0:1]).then_inc(squared, 1)
                act.wait_ge(squared, t + 1)
                nc.scalar.activation(ss[:, t, 1:2], ss[:, t, 0:1], ACT.Sqrt, bias=m.col[:, 3:4], scale=1.0 / D)\
                  .then_inc(rooted, 1)
                for q in range(2):
                    act.wait_ge(turned, 2 * t + q + 1)
                    if t >= 2:
                        act.wait_ge(logit_done, t - 1)
                    nc.scalar.activation(h2T[:, t % 2, q * HALF:(q + 1) * HALF], ps[:, 4 + q, :], ACT.Copy)\
                      .then_inc(turned_out, 1)

        @block.vector
        def _(dve):
            nc.vector.memset(one_row[:], 1.0).then_inc(row_set, 1)
            dve.wait_ge(small_in, 48)

            def residual(t):
                dve.wait_ge(x_in[t], 16)
                dve.wait_ge(summed, t + 1)
                b = 2 * (t % 2)
                nc.vector.tensor_tensor(m.x2[:, t, :], ps[:, b:b + 2, :].rearrange("p a n -> p (a n)"), m.x2[:, t, :],
                                        ALU.add).then_inc(x2_set, 1)

            residual(0)
            for t in range(TT):
                if t + 1 < TT:
                    residual(t + 1)
                dve.wait_ge(rooted, t + 1)
                nc.vector.reciprocal(ss[:, t, 2:3], ss[:, t, 1:2]).then_inc(inv_set, 1)
                dve.wait_ge(inv_set, t + 1)
                if t >= 2:
                    dve.wait_ge(h2_stored[t % 2], 16 * (t // 2))
                    dve.wait_ge(turned, 2 * (t - 1))
                nc.vector.scalar_tensor_tensor(out=h2[:, t % 2, :], in0=m.x2[:, t, :], scalar=ss[:, t, 2:3],
                                               in1=gffn[:], op0=ALU.mult, op1=ALU.mult).then_inc(h2_set, 1)
                if t >= 1:
                    dve.wait_ge(logit_done, t)
                    nc.vector.tensor_copy(m.logits[:, t - 1, :], ps[:, 6 + (t - 1) % 2, 0:N_LOG]).then_inc(logit_out, 1)
            dve.wait_ge(logit_done, TT)
            nc.vector.tensor_copy(m.logits[:, TT - 1, :], ps[:, 6 + (TT - 1) % 2, 0:N_LOG]).then_inc(logit_out, 1)
            dve.wait_ge(logit_out, TT)


def stage_route(nc, g, m):
    with ExitStack() as ctx:
        sb, psum, sem = allocators(nc, ctx)
        ps = psum("ps_route", [P, 4, HALF])
        iota = sb("iota_t", [P, P])
        down = sb("down", [P, PER_GRP])
        before = sb("before", [P, P])
        ones = sb("ones_t", [P, P])
        tokid = sb("tokid", [P, TT])
        first_slot = sb("first_slot", [P, N_EXP])
        more = sb("more", [P, N_EXP, TT - 1])
        red = sb("red", [P, 8, TT])
        eq = sb("eq", [P, TT, PER_GRP])
        oh_g = sb("oh_g", [P, TT, N_GRP])
        oh = sb("oh", [P, 2, TT, PER_GRP])
        picked = sb("picked", [P, TT, N_GRP, PER_GRP])
        in_grp = sb("in_grp", [P, 2, TT, PER_GRP])
        grp_e = sb("grp_e", [P, TT, N_GRP])
        asg = sb("asg", [P, 3, TT, N_EXP])
        total = sb("total", [P, TT, N_EXP])
        base = sb("base", [P, TT + 1, N_EXP])
        slot = sb("slot", [P, TT, N_EXP])
        late = sb("late", [P, TT, N_EXP])
        nblk = sb("nblk", [P, 3, N_EXP])
        cmp_m = sb("cmp_m", [P, N_EXP, TT - 1])
        cmp_b = sb("cmp_b", [P, OVER, N_EXP])
        own = sb("own", [P, OVER])
        slot_f = sb("slot_f", [P, 2, TT])
        slot_i = sb("slot_i", [P, 3, 2, TT], I32)
        hilo = sb("hilo", [P, 2, 2, TT])
        oh_lo = sb("oh_lo", [P, 2, P])
        oh_hi = sb("oh_hi", [P, 2, N_BLK])
        const_in, vstep, shifted, exped, gap_set, exp2, asg_set, counted, oh_set, oh_used, ids_done = (
            sem(n) for n in ("const_in_u", "vstep_u", "shifted", "exped", "gap_set", "exp2", "asg_set", "counted",
                             "oh_set", "oh_used", "ids_done"))
        N_CONST = 7
        block = ctx.enter_context(nc.Block())

        @block.sync
        def _(sy):
            for dst, src in ((iota[:], g.iota), (down[:], g.down), (before[:], g.before), (ones[:], g.ones),
                             (tokid[:], g.tokid), (first_slot[:], g.first_slot), (more[:], g.more)):
                sy.dma_start(dst, src).then_inc(const_in, 16)
            for s in range(W_SLOTS):
                load_expert(sy, g, m, s, s, m.w_in[s])

        @block.scalar
        def _(act):
            act.wait_ge(shifted, 1)
            nc.scalar.activation(grp_e[:], grp_e[:], ACT.Exp).then_inc(exped, 1)
            act.wait_ge(gap_set, 1)
            nc.scalar.activation(red[:, 5, :], red[:, 4, :], ACT.Exp).then_inc(exp2, 1)

        @block.tensor
        def _(pe):
            pe.wait_ge(const_in, 16 * N_CONST)
            pe.wait_ge(asg_set, 1)
            both = asg[:, 2, :, :]
            nc.tensor.matmul(ps[:, 0, 0:TT * N_EXP], before[:], both, start=True, stop=True)
            nc.tensor.matmul(ps[:, 1, 0:TT * N_EXP], ones[:], both, start=True, stop=True).then_inc(counted, 1)
            for n in range(2 * TT):
                pe.wait_ge(oh_set, n + 1)
                nc.tensor.matmul(ps[:, 2, 0:N_BLK], oh_lo[:, n % 2, :], oh_hi[:, n % 2, :], start=(n == 0),
                                 stop=(n == 2 * TT - 1)).then_inc(oh_used, 1)

        @block.vector
        def _(dve):
            step = Steps(dve, vstep)
            v = nc.vector
            dve.wait_ge(const_in, 16 * N_CONST)

            def across(ap, n):
                return ap.rearrange("p (t a) -> p t a", a=1).broadcast_to([P, TT, n])

            def along(ap, n):
                return ap.rearrange("p (a n) -> p a n", a=1).broadcast_to([P, TT, n])

            def first_max(values, n, mx, tmp, out):
                step(v.tensor_reduce(mx, values, AXX, ALU.max))
                step(v.tensor_tensor(tmp, values, across(mx, n), ALU.is_equal))
                step(v.tensor_tensor(tmp, tmp, along(down[:, PER_GRP - n:], n), ALU.mult))
                step(v.tensor_reduce(red[:, 7, :], tmp, AXX, ALU.min))
                step(v.tensor_tensor(out, along(down[:, PER_GRP - n:], n), across(red[:, 7, :], n), ALU.is_equal))

            grp = m.logits[:, :, 0:N_GRP]
            exp_l = m.logits[:, :, N_GRP:N_LOG].rearrange("p t (g e) -> p t g e", g=N_GRP)
            first_max(grp, N_GRP, red[:, 0, :], eq[:, :, 0:N_GRP], oh_g[:])
            v.tensor_tensor(grp_e[:], grp, across(red[:, 0, :], N_GRP), ALU.subtract).then_inc(shifted, 1)
            by_g = oh_g[:].rearrange("p t (g a) -> p t g a", a=1).broadcast_to([P, TT, N_GRP, PER_GRP])
            step(v.tensor_tensor(picked[:], exp_l, by_g, ALU.mult))
            step(v.tensor_reduce(in_grp[:, 0, :, :], picked[:].rearrange("p t g e -> p t e g"), AXX, ALU.add))
            first_max(in_grp[:, 0, :, :], PER_GRP, red[:, 1, :], eq[:], oh[:, 0, :, :])
            step(v.scalar_tensor_tensor(out=in_grp[:, 1, :, :], in0=oh[:, 0, :, :], scalar=NEG, in1=in_grp[:, 0, :, :],
                                        op0=ALU.mult, op1=ALU.add))
            first_max(in_grp[:, 1, :, :], PER_GRP, red[:, 2, :], eq[:], oh[:, 1, :, :])
            v.tensor_tensor(red[:, 4, :], red[:, 2, :], red[:, 1, :], ALU.subtract).then_inc(gap_set, 1)
            dve.wait_ge(exped, 1)
            step(v.tensor_reduce(red[:, 3, :], grp_e[:], AXX, ALU.add))
            dve.wait_ge(exp2, 1)
            step(v.scalar_tensor_tensor(out=red[:, 6, :], in0=red[:, 5, :], scalar=1.0, in1=red[:, 3, :], op0=ALU.add,
                                        op1=ALU.mult))
            step(v.reciprocal(m.gate[:, 0, :], red[:, 6, :]))
            v.tensor_tensor(m.gate[:, 1, :], m.gate[:, 0, :], red[:, 5, :], ALU.mult)
            for a in range(2):
                by_e = oh[:, a, :, :].rearrange("p t (b e) -> p t b e", b=1).broadcast_to([P, TT, N_GRP, PER_GRP])
                ins = v.tensor_tensor(asg[:, a, :, :].rearrange("p t (g e) -> p t g e", g=N_GRP), by_g, by_e, ALU.mult)
            step(ins)
            v.tensor_tensor(asg[:, 2, :, :], asg[:, 0, :, :], asg[:, 1, :, :], ALU.add).then_inc(asg_set, 1)
            dve.wait_ge(counted, 1)
            v.memset(base[:, 0, :], 0.0)
            step(v.tensor_copy(total[:], ps[:, 1, 0:TT * N_EXP].rearrange("p (t e) -> p t e", t=TT)))
            for t in range(TT):
                step(v.tensor_tensor(base[:, t + 1, :], base[:, t, :], total[:, t, :], ALU.add))
            step(v.tensor_tensor(slot[:], ps[:, 0, 0:TT * N_EXP].rearrange("p (t e) -> p t e", t=TT), base[:, 0:TT, :],
                                 ALU.add))
            count = base[:, TT, :].rearrange("p (e a) -> p e a", a=1).broadcast_to([P, N_EXP, TT - 1])
            step(v.tensor_tensor(cmp_m[:], count, more[:], ALU.is_gt))
            step(v.tensor_reduce(nblk[:, 0, :], cmp_m[:], AXX, ALU.add))
            step(v.tensor_tensor_scan(nblk[:, 1, :], ones[:, 0:N_EXP], nblk[:, 0, :], 0.0, ALU.mult, ALU.add))
            step(v.tensor_tensor(nblk[:, 2, :], nblk[:, 1, :], nblk[:, 0, :], ALU.subtract))
            step(v.tensor_scalar(nblk[:, 2, :], nblk[:, 2, :], float(P), float((N_EXP - 1) * P), ALU.mult, ALU.add))
            step(v.tensor_tensor(nblk[:, 2, :], nblk[:, 2, :], first_slot[:], ALU.subtract))
            step(v.scalar_tensor_tensor(out=late[:], in0=slot[:], scalar=float(P), in1=along(nblk[:, 2, :], N_EXP),
                                        op0=ALU.is_ge, op1=ALU.mult))
            step(v.tensor_tensor(slot[:], slot[:], late[:], ALU.add))
            step(v.tensor_tensor(slot[:], slot[:], along(first_slot[:], N_EXP), ALU.add))
            for a in range(2):
                step(v.tensor_tensor(late[:], asg[:, a, :, :], slot[:], ALU.mult))
                step(v.tensor_reduce(slot_f[:, a, :], late[:], AXX, ALU.add))
            v.tensor_copy(m.slots[:], slot_f[:])
            step(v.tensor_copy(slot_i[:, 0, :, :], slot_f[:]))
            v.tensor_scalar(slot_i[:, 1, :, :], slot_i[:, 0, :, :], 7, None, ALU.arith_shift_right)
            step(v.tensor_scalar(slot_i[:, 2, :, :], slot_i[:, 0, :, :], P - 1, None, ALU.bitwise_and))
            step(v.tensor_copy(hilo[:], slot_i[:, 1:3, :, :]))
            for a in range(2):
                for t in range(TT):
                    n = a * TT + t
                    if n >= 2:
                        dve.wait_ge(oh_used, n - 1)
                    v.tensor_scalar(oh_hi[:, n % 2, :], iota[:, 0:N_BLK], hilo[:, 0, a, t:t + 1], tokid[:, t:t + 1],
                                    ALU.is_equal, ALU.mult)
                    v.tensor_scalar(oh_lo[:, n % 2, :], iota[:], hilo[:, 1, a, t:t + 1], None, ALU.is_equal)\
                     .then_inc(oh_set, 1)
            upto = nblk[:, 1, :].rearrange("p (a e) -> p a e", a=1).broadcast_to([P, OVER, N_EXP])
            which = iota[:, 0:OVER].rearrange("p (b a) -> p b a", a=1).broadcast_to([P, OVER, N_EXP])
            step(v.tensor_tensor(cmp_b[:], upto, which, ALU.is_le))
            step(v.tensor_reduce(own[:], cmp_b[:], AXX, ALU.add))
            step(v.tensor_scalar(own[:], own[:], float(N_EXP - 1), None, ALU.min))
            v.tensor_copy(m.over[:, 0:OVER], own[:])
            step(v.tensor_copy(m.over[:, OVER:OVER + 1], nblk[:, 1, N_EXP - 1:N_EXP]))
            dve.wait_ge(oh_used, 2 * TT)
            step(v.tensor_copy(m.ids[:], ps[:, 2, 0:N_BLK]))


W_SLOTS = 4


def load_expert(sy, g, m, ws, e, done):
    sy.dma_start(m.w13[ws][:], flat(g.w13[bass.ds(e, 1), :, :, :].rearrange("e p k n -> p e (k n)"))
                 .rearrange("p (k n) -> p k n", k=KT)).then_inc(done, 16)
    sy.dma_start(m.w2[ws][:], flat(g.w2[bass.ds(e, 1), :, :, :].rearrange("e p k n -> p e (k n)"))
                 .rearrange("p (k n) -> p k n", k=2)).then_inc(done, 16)


def stage_experts(nc, g, m):
    with ExitStack() as ctx:
        sb, psum, sem = allocators(nc, ctx)
        ps = psum("ps_exp", [P, 8, HALF])
        w13, w2 = m.w13, m.w2
        idx = [sb(f"idx{s}", [P, 1], U32) for s in range(2)]
        rows = [sb(f"rows{s}", [P, D]) for s in range(2)]
        xT = [sb(f"xT{s}", [P, KT, P]) for s in range(2)]
        sil = [sb(f"sil{s}", [P, 2 * P]) for s in range(2)]
        hid = [sb(f"hid_e{s}", [P, 2 * P]) for s in range(2)]
        y = [sb(f"y{s}", [P, D]) for s in range(2)]

        def signals(tag):
            return {w: [sem(f"{w}_{tag}{s}") for s in range(2)] for w in
                    ("idx_set", "rows_in", "turned", "xT_a", "xT_v", "up_done", "sil_out", "hid_out", "y_done",
                     "y_a", "y_v", "stored")}

        main, more = signals("first"), signals("more")
        w_in = m.w_in + [sem("w_in_more")]
        over_free = sem("over_free")
        gather_open = sem("gather_open")
        block = ctx.enter_context(nc.Block())
        EXP_TURNS = N_EXP // W_SLOTS
        PER = W_SLOTS // 2
        MORE = W_SLOTS

        def gather(pool, q, s, k, b, free=True):
            if free:
                pool.wait_ge(q["turned"][s], k)
            nc.gpsimd.tensor_copy(idx[s][:], m.ids[:, bass.ds(b, 1)]).then_inc(q["idx_set"][s], 1)
            pool.wait_ge(q["idx_set"][s], k + 1)
            nc.gpsimd.sem_inc(gather_open, 1)
            nc.gpsimd.indirect_dma_start(out=rows[s][:], out_offset=None, in_=g.h2,
                                         in_offset=bass.IndirectOffsetOnAxis(ap=idx[s][:], axis=0))\
              .then_inc(q["rows_in"][s], 16)

        def turn(pe, q, s, k, free):
            free()
            pe.wait_ge(q["rows_in"][s], 16 * k + 16)
            for c in range(KT):
                ins = nc.tensor.transpose(ps[:, c // 4, (c % 4) * P:(c % 4 + 1) * P], rows[s][:, c * P:(c + 1) * P],
                                          m.ident[:])
            ins.then_inc(q["turned"][s], 1)

        def up(pe, q, s, k, ws, w_count, w_sem=None):
            pe.wait_ge(q["xT_a"][s], k + 1)
            pe.wait_ge(q["xT_v"][s], k + 1)
            pe.wait_ge(w_in[ws if w_sem is None else w_sem], 32 * w_count + 32)
            for f in range(4):
                for c in range(KT):
                    ins = nc.tensor.matmul(ps[:, 2 + s, f * P:(f + 1) * P], w13[ws][:, c, f * P:(f + 1) * P],
                                           xT[s][:, c, :], start=(c == 0), stop=(c == KT - 1))
            ins.then_inc(q["up_done"][s], 1)

        def downward(pe, q, s, k, ws):
            pe.wait_ge(q["hid_out"][s], k + 1)
            for h in range(2):
                for f in range(2):
                    ins = nc.tensor.matmul(ps[:, 4 + 2 * s + h, :], hid[s][:, f * P:(f + 1) * P],
                                           w2[ws][:, f, h * HALF:(h + 1) * HALF], start=(f == 0), stop=(f == 1))
            ins.then_inc(q["y_done"][s], 1)

        def act_turned(act, q, s, k):
            act.wait_ge(q["turned"][s], k + 1)
            nc.scalar.activation(xT[s][:, 0:4, :], ps[:, 0, :], ACT.Copy).then_inc(q["xT_a"][s], 1)

        def act_silu(act, q, s, k):
            act.wait_ge(q["up_done"][s], k + 1)
            nc.scalar.activation(sil[s][:], ps[:, 2 + s, 0:2 * P], ACT.Silu).then_inc(q["sil_out"][s], 1)

        def act_y(act, q, s, k, b, first=False):
            if not first:
                act.wait_ge(q["stored"][s], 16 * k)
            act.wait_ge(q["y_done"][s], k + 1)
            nc.scalar.activation(y[s][:, 0:HALF], ps[:, 4 + 2 * s, :], ACT.Copy).then_inc(q["y_a"][s], 1)
            act.wait_ge(q["y_a"][s], k + 1)
            act.wait_ge(q["y_v"][s], k + 1)
            act.dma_start(g.y[bass.ds(b * P, P), :], y[s][:]).then_inc(q["stored"][s], 16)

        def vec_turned(dve, q, s, k):
            dve.wait_ge(q["turned"][s], k + 1)
            nc.vector.tensor_copy(xT[s][:, 4:8, :], ps[:, 1, :]).then_inc(q["xT_v"][s], 1)

        def vec_hid(dve, q, s, k):
            dve.wait_ge(q["sil_out"][s], k + 1)
            nc.vector.tensor_tensor(hid[s][:], ps[:, 2 + s, 2 * P:4 * P], sil[s][:], ALU.mult)\
              .then_inc(q["hid_out"][s], 1)

        def vec_y(dve, q, s, k, first=False):
            if not first:
                dve.wait_ge(q["stored"][s], 16 * k)
            dve.wait_ge(q["y_done"][s], k + 1)
            nc.vector.tensor_copy(y[s][:, HALF:D], ps[:, 5 + 2 * s, :]).then_inc(q["y_v"][s], 1)

        @block.sync
        def _(sy):
            with nc.sync.Fori(1, EXP_TURNS) as i:
                for j in range(W_SLOTS):
                    sy.wait_ge(main["y_done"][j % 2], PER * i - PER + j // 2 + 1)
                    load_expert(sy, g, m, j, W_SLOTS * i + j, w_in[j])
            sy.wait_ge(main["y_done"][0], PER * EXP_TURNS)
            n_over = sy.value_load(m.over[0:1, OVER:OVER + 1], min_val=0, max_val=OVER)
            with nc.sync.Fori(0, OVER) as b:
                with nc.sync.If(b < n_over):
                    e = sy.value_load(m.over[0:1, bass.ds(b, 1)], min_val=0, max_val=N_EXP - 1)
                    sy.wait_ge(over_free, b + 1)
                    load_expert(sy, g, m, 0, e, w_in[MORE])

        @block.gpsimd
        def _(pool):
            for s in range(2):
                gather(pool, main, s, 0, s, False)
            with nc.gpsimd.Fori(1, N_EXP // 2) as i:
                for s in range(2):
                    gather(pool, main, s, i, 2 * i + s)
            pool.wait_ge(main["turned"][0], N_EXP // 2)
            n_over = pool.value_load(m.over[0:1, OVER:OVER + 1], min_val=0, max_val=OVER)
            with nc.gpsimd.Fori(0, OVER) as b:
                with nc.gpsimd.If(b < n_over):
                    pool.wait_ge(over_free, b + 1)
                    gather(pool, more, 0, b, b + N_EXP, False)

        @block.tensor
        def _(pe):
            def copied(s, k):
                def wait():
                    pe.wait_ge(main["xT_a"][s], k)
                    pe.wait_ge(main["xT_v"][s], k)
                return wait

            def turn_of(i, last):
                for j in range(W_SLOTS):
                    s, k = j % 2, PER * i + j // 2
                    up(pe, main, s, k, j, i)
                    if not (last and j == W_SLOTS - 1):
                        turn(pe, main, 1 - s, k + s, copied(s, k + 1))
                    downward(pe, main, s, k, j)

            turn(pe, main, 0, 0, lambda: None)
            with nc.tensor.Fori(0, EXP_TURNS - 1) as i:
                turn_of(i, False)
            turn_of(EXP_TURNS - 1, True)
            n_over = pe.value_load(m.over[0:1, OVER:OVER + 1], min_val=0, max_val=OVER)
            with nc.tensor.Fori(0, OVER) as b:
                with nc.tensor.If(b < n_over):
                    pe.wait_ge(over_free, b + 1)
                    turn(pe, more, 0, b, lambda: None)
                    up(pe, more, 0, b, 0, b, MORE)
                    downward(pe, more, 0, b, 0)

        @block.scalar
        def _(act):
            act_turned(act, main, 0, 0)

            def pair(i, first=False, last=False):
                act_silu(act, main, 0, i)
                act_turned(act, main, 1, i)
                act_y(act, main, 0, i, 2 * i, first)
                act_silu(act, main, 1, i)
                if not last:
                    act_turned(act, main, 0, i + 1)
                act_y(act, main, 1, i, 2 * i + 1, first)

            pair(0, first=True)
            with nc.scalar.Fori(1, N_EXP // 2 - 1) as i:
                pair(i)
            pair(N_EXP // 2 - 1, last=True)
            for s in range(2):
                act.wait_ge(main["stored"][s], 16 * (N_EXP // 2))
            nc.scalar.sem_inc(over_free, 1)
            n_over = act.value_load(m.over[0:1, OVER:OVER + 1], min_val=0, max_val=OVER)
            with nc.scalar.Fori(0, OVER) as b:
                with nc.scalar.If(b < n_over):
                    act_turned(act, more, 0, b)
                    act_silu(act, more, 0, b)
                    act_y(act, more, 0, b, b + N_EXP, True)
                    act.wait_ge(more["stored"][0], 16 * b + 16)
                    nc.scalar.sem_inc(over_free, 1)

        @block.vector
        def _(dve):
            vec_turned(dve, main, 0, 0)

            def pair(i, first=False, last=False):
                vec_hid(dve, main, 0, i)
                vec_turned(dve, main, 1, i)
                vec_y(dve, main, 0, i, first)
                vec_hid(dve, main, 1, i)
                if not last:
                    vec_turned(dve, main, 0, i + 1)
                vec_y(dve, main, 1, i, first)

            pair(0, first=True)
            with nc.vector.Fori(1, N_EXP // 2 - 1) as i:
                pair(i)
            pair(N_EXP // 2 - 1, last=True)
            n_over = dve.value_load(m.over[0:1, OVER:OVER + 1], min_val=0, max_val=OVER)
            with nc.vector.Fori(0, OVER) as b:
                with nc.vector.If(b < n_over):
                    dve.wait_ge(over_free, b + 1)
                    vec_turned(dve, more, 0, b)
                    vec_hid(dve, more, 0, b)
                    vec_y(dve, more, 0, b, True)


def stage_combine(nc, g, m):
    with ExitStack() as ctx:
        sb, psum, sem = allocators(nc, ctx)
        BUF = 4
        gfin = sb("gfin", [P, D])
        ya = sb("ya", [P, BUF, 2, D])
        square = sb("square_c", [P, D])
        ss = sb("ss_c", [P, TT, 3])
        res = sb("res", [P, 2, D])
        g_in = sem("g_in_c")
        y_in = [sem(f"y_in{s}") for s in range(BUF)]
        part, x3_set, squared, rooted, inv_set, res_set = (sem(n) for n in ("part_c", "x3_set", "squared_c", "rooted_c",
                                                                            "inv_set_c", "res_set"))
        stored = [sem(f"stored_c{s}") for s in range(2)]
        block = ctx.enter_context(nc.Block())

        @block.gpsimd
        def _(pool):
            for t in range(TT):
                if t >= BUF:
                    pool.wait_ge(x3_set, t - BUF + 1)
                for a in range(2):
                    nc.gpsimd.indirect_dma_start(out=ya[:, t % BUF, a, :], out_offset=None, in_=g.y,
                                                 in_offset=bass.IndirectOffsetOnAxis(ap=m.slots[:, a, t:t + 1], axis=0))\
                      .then_inc(y_in[t % BUF], 16)

        @block.sync
        def _(sy):
            sy.dma_start(gfin[:], g.gfin).then_inc(g_in, 16)
            for t in range(TT):
                sy.wait_ge(res_set, t + 1)
                sy.dma_start(g.out[t * P:(t + 1) * P, :], res[:, t % 2, :]).then_inc(stored[t % 2], 16)
            for s in range(2):
                sy.wait_ge(stored[s], 16 * TT // 2)

        @block.scalar
        def _(act):
            for t in range(TT):
                act.wait_ge(x3_set, t + 1)
                nc.scalar.activation(square[:], m.x2[:, t, :], ACT.Square, accum_out=ss[:, t, 0:1]).then_inc(squared, 1)
                act.wait_ge(squared, t + 1)
                nc.scalar.activation(ss[:, t, 1:2], ss[:, t, 0:1], ACT.Sqrt, bias=m.col[:, 3:4], scale=1.0 / D)\
                  .then_inc(rooted, 1)

        @block.vector
        def _(dve):
            dve.wait_ge(g_in, 16)

            def add(t):
                dve.wait_ge(y_in[t % BUF], 32 * (t // BUF + 1))
                nc.vector.scalar_tensor_tensor(out=m.x2[:, t, :], in0=ya[:, t % BUF, 0, :], scalar=m.gate[:, 0, t:t + 1],
                                               in1=m.x2[:, t, :], op0=ALU.mult, op1=ALU.add).then_inc(part, 1)
                dve.wait_ge(part, t + 1)
                nc.vector.scalar_tensor_tensor(out=m.x2[:, t, :], in0=ya[:, t % BUF, 1, :], scalar=m.gate[:, 1, t:t + 1],
                                               in1=m.x2[:, t, :], op0=ALU.mult, op1=ALU.add).then_inc(x3_set, 1)

            add(0)
            for t in range(TT):
                if t + 1 < TT:
                    add(t + 1)
                dve.wait_ge(rooted, t + 1)
                nc.vector.reciprocal(ss[:, t, 2:3], ss[:, t, 1:2]).then_inc(inv_set, 1)
                dve.wait_ge(inv_set, t + 1)
                if t >= 2:
                    dve.wait_ge(stored[t % 2], 16 * (t // 2))
                nc.vector.scalar_tensor_tensor(out=res[:, t % 2, :], in0=m.x2[:, t, :], scalar=ss[:, t, 2:3],
                                               in1=gfin[:], op0=ALU.mult, op1=ALU.mult).then_inc(res_set, 1)


def program(nc, g):
    m = Names()
    with ExitStack() as whole:
        def sb(ctx, name, shape, dt=F32, side=None):
            return ctx.enter_context(nc.sbuf_tensor(name, shape, dt, side=side))

        m.ident = sb(whole, "ident", [P, P])
        m.col = sb(whole, "col", [P, 8])
        with ExitStack() as late:
            with ExitStack() as mixers:
                m.hT = sb(mixers, "hT", [P, KT, S])
                m.bmT = sb(mixers, "bmT", [P, PAIRS, S])
                with ExitStack() as ctx:
                    m.lo = sb(ctx, "lo", [P, 2, S])
                    m.mu_lo = sb(ctx, "mu_lo", [P, 2])
                    m.wr = sb(ctx, "wr", [P, 3, KT * P])
                    m.wr_in = nc.alloc_semaphore("wr_in")
                    stage_normalise(nc, g, m)
                    stage_recur(nc, g, m)
                m.oAT = sb(mixers, "oAT", [P, PAIRS, S])
                m.wg = sb(mixers, "wg", [P, 2, KT * P])
                m.wab = sb(mixers, "wab", [P, 2, 2 * PAIRS, P])
                m.wg_in = nc.alloc_semaphore("wg_in")
                m.wab_in = [nc.alloc_semaphore(f"wab_in{s}") for s in range(2)]
                with ExitStack() as ctx:
                    m.qkv = sb(ctx, "qkv", [P, N_QKV, S])
                    m.vtok = sb(ctx, "vtok", [P, TT, 2 * P])
                    m.gates = sb(ctx, "gates", [P, TT, 24])
                    m.kcmp = sb(ctx, "kcmp", [P, N_CMP])
                    m.vcmp = sb(ctx, "vcmp", [HD, 2, HD])
                    stage_project(nc, g, m)
                    stage_attend(nc, g, m)
                m.mT = sb(late, "mT", [P, KT, S], side="right")
                stage_merge(nc, g, m)
            m.x2 = sb(whole, "x2", [P, TT, D])
            m.logits = sb(whole, "logits", [P, TT, N_LOG])
            m.gate = sb(whole, "gate", [P, 2, TT])
            m.slots = sb(whole, "slots", [P, 2, TT], U32)
            m.ids = sb(whole, "ids", [P, N_BLK], U32)
            m.over = sb(whole, "over", [P, OVER + 1], I32)
            stage_output(nc, g, m)
        m.w_in = [nc.alloc_semaphore(f"w_in_e{s}") for s in range(W_SLOTS)]
        with ExitStack() as ctx:
            m.w13 = [sb(ctx, f"w13_{s}", [P, KT, 2 * D_EXP]) for s in range(W_SLOTS)]
            m.w2 = [sb(ctx, f"w2_{s}", [P, 2, D]) for s in range(W_SLOTS)]
            stage_route(nc, g, m)
            stage_experts(nc, g, m)
        stage_combine(nc, g, m)


def tile_columns():
    q, kc, vc, ksl, vsl, kwn, vwn, gat = 0, 512, 640, 768, 896, 1024, 1152, 1280
    r = 1304
    k, v, xw, xg, ga, gb = r + 512, r + 1024, r + 1536, r + 1664, r + 1792, r + 2816
    run = lambda a, n: list(range(a, a + n))
    tiles = [run(xw, P), run(xg, P)]
    for hp in range(PAIRS):
        tiles += [run(base + hp * P, P) for base in (r, k, v)]
    tiles += [run(kc, P), run(ksl, P), run(kwn, P)]
    tiles += [run(q + i * HD, HD) + run(q + (PAIRS + i) * HD, HD) for i in range(PAIRS)]
    tiles += [run(vc, P)]
    for f in range(KT):
        tiles += [run(ga + f * P, P), run(gb + f * P, P)]
    return tiles, run(vsl, P) + run(vwn, P) + run(gat, 24)


def constants():
    c = {}
    p = np.arange(P)
    c["ident"] = np.eye(P)
    col = np.zeros((P, 8))
    col[:, 0] = 10000.0 ** (-(p % 32) / 32.0)
    col[:, 1] = np.where(p % HD < 32, -1.0, 1.0)
    col[:, 2] = np.pi / 2
    col[:, 3] = RMS_EPS
    col[:, 4] = GN_EPS
    col[:, 5] = p >= 31
    col[:, 6] = p
    c["col"] = col
    s, t = p[:, None], p[None, :]
    c["ones"] = np.ones((P, P))
    c["mask4"] = np.concatenate([s < t, s <= t, s < t, s <= t], 1)
    c["lvl"] = np.stack([(s >> (b + 1) == t >> (b + 1)) & (s >> b & 1 == 0) & (t >> b & 1 == 1)
                         for b in range(7)], 1)
    c["heads1"] = s // HD == t // HD
    c["eye2"] = s % HD == np.arange(HD)[None, :]
    causal = np.where(t <= s, 0.0, NEG)
    c["bias"] = np.stack([np.where(t > s, 0.0, NEG), causal], 1)
    q = (np.arange(TT)[None, :, None] * P + p[:, None, None])
    c["bias_cmp"] = np.where(np.arange(N_CMP)[None, None, :] * 16 + 31 <= q, 0.0, NEG)
    c["down"] = np.broadcast_to(np.arange(-PER_GRP, 0), (P, PER_GRP))
    c["before"] = s < t
    c["iota"] = np.broadcast_to(np.arange(P), (P, P))
    c["tokid"] = np.arange(TT)[None, :] * P + p[:, None]
    c["first_slot"] = np.broadcast_to(np.arange(N_EXP) * P, (P, N_EXP))
    c["more"] = np.broadcast_to(np.arange(1, TT) * P, (P, N_EXP, TT - 1))
    return {k: np.ascontiguousarray(v.astype(np.float32)) for k, v in c.items()}


def layout(inp):
    a = {k: np.asarray(v) for k, v in inp.items()}
    cat, asc = np.concatenate, np.ascontiguousarray
    by_tile = lambda w: w.reshape(-1, P, w.shape[-1]).transpose(1, 0, 2)
    d = {}
    x, w_in = a["x"][0], a["w_in"][0]
    d["x"] = x
    d["xT"] = by_tile(asc(x.T))
    d["xT"] = d["xT"].reshape(P, KT * S)
    tiles, tokw = tile_columns()
    d["w_tiles"] = np.stack([by_tile(w_in[:, cols]).reshape(P, KT * P) for cols in tiles], 1)
    d["w_tok"] = by_tile(w_in[:, tokw])
    d["gmix"] = a["g_mix"][0].reshape(KT, P).T
    mu = a["rwkv_mu"][0]
    d["mu_lo"] = np.stack([mu[1536:1536 + P], mu[1536 + P:1536 + 2 * P]], 1)
    d["pos"] = np.broadcast_to(a["positions"][0], (P, S))
    pair = lambda v: v.reshape(PAIRS, P)
    vecs = [pair(mu[0:512]), pair(mu[512:1024]), pair(mu[1024:1536]), pair(a["rwkv_w0"][0]), pair(a["rwkv_a0"][0]),
            pair(a["rwkv_k_k"][0]), pair(a["rwkv_k_a"][0]), pair(a["rwkv_r_k"][0].reshape(-1)),
            pair(a["rwkv_ln_w"][0]), pair(a["rwkv_ln_b"][0])]
    d["vecs"] = np.stack(vecs, 2).transpose(1, 0, 2)
    wa = cat([a["rwkv_w2"][0], a["rwkv_a2"][0]], 0).reshape(P, PAIRS, P)
    g2 = a["rwkv_g2"][0].reshape(P, PAIRS, P)
    d["lora"] = np.stack([wa, g2], 2).reshape(P, PAIRS * 2, P)
    half_rows = lambda v: v.reshape(-1, P).T
    d["cmp_pe"] = np.stack([half_rows(a["cmp_pe_" + kv][0].reshape(-1)) for kv in "kv"], 1)
    d["cmp_w1"] = np.stack([by_tile(a["cmp_w1_" + kv][0]) for kv in "kv"])
    d["cmp_w2"] = np.stack([by_tile(a["cmp_w2_" + kv][0]) for kv in "kv"], 1)
    d["cmp_b1"] = np.stack([half_rows(a["cmp_b1_" + kv][0]) for kv in "kv"], 1)
    w_a = a["w_proj_a"][0].reshape(2, PAIRS, HD, D).transpose(1, 0, 2, 3).reshape(-1, D)
    w_ab = np.stack([by_tile(w_a), by_tile(a["w_proj_b"][0])], 1)
    d["w_ab"] = w_ab.reshape(P, 8, KT, P).transpose(0, 2, 1, 3).reshape(P, 8 * KT, P)
    d["w_out"] = by_tile(a["w_out"][0])
    d["gffn"] = np.broadcast_to(a["g_ffn"][0], (P, D))
    d["gfin"] = np.broadcast_to(a["g_final"], (P, D))
    d["w_rt"] = by_tile(cat([a["w_grp"][0], a["w_exp"][0]], 1))
    d["b_rt"] = cat([a["b_grp"][0], a["b_exp"][0]])[None, :]
    w13 = np.stack([a["e_w1"][0], a["e_w3"][0]], 2)
    d["w13"] = w13.reshape(N_EXP, KT, P, 2 * D_EXP).transpose(0, 2, 1, 3)
    d["w2"] = a["e_w2"][0].reshape(N_EXP, 2, P, D).transpose(0, 2, 1, 3)
    d["cmp_b2k"] = a["cmp_b2_k"][0][:, None]
    d["cmp_b2v"] = a["cmp_b2_v"][0][None, :]
    return {k: asc(v) for k, v in d.items()}


def kernel(**inputs):
    import concourse.bacc as bacc
    from concourse.bass_utils import run_bass_kernel_spmd

    nc = bacc.Bacc("TRN2", target_bir_lowering=False, num_devices=1)
    arrays, g = {}, Names()
    for name, a in {**constants(), **layout(inputs)}.items():
        arrays["in_" + name] = a
        g.__dict__[name] = nc.dram_tensor("in_" + name, a.shape, mybir.dt.from_np(a.dtype), kind="ExternalInput").ap()
    g.out = nc.dram_tensor("out", (S, D), F32, kind="ExternalOutput").ap()
    g.h2 = nc.dram_tensor("h2_rows", (S, D), F32, kind="Internal").ap()
    g.y = nc.dram_tensor("y_rows", (N_BLK * P, D), F32, kind="Internal").ap()
    program(nc, g)
    r = run_bass_kernel_spmd(nc, [arrays], core_ids=[0])
    return r.results[0]["out"].reshape(1, S, D)
```
